# Optimizing a Trainium2 kernel written in Bass

```python
import math
import jax
import jax.numpy as jnp
from jax import lax
import numpy as np

D_MODEL = 1024
BATCH = 1
SEQ = 128
DEPTH = 2
DEC_BATCH = 1
DEC_SEQ = 512
PAST_LEN = 128

GRID_W = 64
EPS = 1e-6
ROPE_THETA = 10000.0
CHUNK = 128
Q_BLOCK = 128
ATT_HEAD_DIM = 64
ATT_WIDTH = D_MODEL // 2
ATT_HEADS = ATT_WIDTH // ATT_HEAD_DIM
ATT_KV_HEADS = ATT_HEADS // 4
ATT_KV_WIDTH = ATT_KV_HEADS * ATT_HEAD_DIM
SSD_WIDTH = D_MODEL // 2
SSD_HEAD_DIM = 64
SSD_HEADS = SSD_WIDTH // SSD_HEAD_DIM
SSD_GROUPS = 2
SSD_STATE = 64
SSD_CONV = 5
SSD_XBC = SSD_WIDTH + 2 * SSD_GROUPS * SSD_STATE
L0_IN = ATT_WIDTH + 2 * ATT_KV_WIDTH + SSD_WIDTH + SSD_XBC + 2 * SSD_HEADS
RET_HEADS = 4
RET_QK_WIDTH = D_MODEL
RET_V_WIDTH = 2 * D_MODEL
RET_DK = RET_QK_WIDTH // RET_HEADS
RET_DV = RET_V_WIDTH // RET_HEADS
L1_IN = 2 * RET_QK_WIDTH + 2 * RET_V_WIDTH
D_FF = -(-8 * D_MODEL // (3 * 256)) * 256

kernel_name = "hybrid_ssd_gqa_retention_diffusion_step"

F32 = jnp.float32

def rmsnorm(x, w):
    xf = x.astype(F32)
    y = xf * lax.rsqrt(jnp.mean(xf * xf, axis=-1, keepdims=True) + EPS)
    return (y * w.astype(F32)).astype(x.dtype)

def axial_rope(n_tokens, dim):
    rows = n_tokens // GRID_W
    row = jnp.repeat(jnp.arange(rows), GRID_W).astype(F32)
    col = jnp.tile(jnp.arange(GRID_W), rows).astype(F32)
    n_freq = dim // 4
    inv = ROPE_THETA ** (-jnp.arange(n_freq, dtype=F32) / n_freq)
    ang = jnp.concatenate([row[:, None] * inv, col[:, None] * inv], axis=-1)
    return jnp.cos(ang)[:, None, :], jnp.sin(ang)[:, None, :]

def apply_rope(x, rope):
    cos, sin = rope[0].astype(x.dtype), rope[1].astype(x.dtype)
    x1, x2 = jnp.split(x, 2, axis=-1)
    return jnp.concatenate([x1 * cos - x2 * sin, x2 * cos + x1 * sin], axis=-1)

def block_attention(q, k, v):
    b, lq, nkv, g, d = q.shape
    nb = lq // Q_BLOCK
    qb = q.reshape(b, nb, Q_BLOCK, nkv, g, d).swapaxes(0, 1)
    scale = d ** -0.5

    def one(qblk):
        s = jnp.einsum("bqkgd,btkd->bkgqt", qblk, k).astype(F32) * scale
        p = jax.nn.softmax(s, axis=-1).astype(v.dtype)
        return jnp.einsum("bkgqt,btkd->bqkgd", p, v)

    o = lax.map(one, qb)
    return o.swapaxes(0, 1).reshape(b, lq, nkv * g * d)

def dwconv_centred(x, w, bias):
    kw, ch = w.shape
    y = lax.conv_general_dilated(x, w[:, None, :].astype(x.dtype), window_strides=(1,),
                                 padding=[(kw // 2, kw // 2)],
                                 dimension_numbers=("NWC", "WIO", "NWC"),
                                 feature_group_count=ch)
    return y + bias

def chunked_decay_scan(q, k, v, log_a, s0):
    b, l, h, dk = q.shape
    dv = v.shape[-1]
    nc = l // CHUNK

    def to_chunks(t):
        return t.reshape((b, nc, CHUNK) + t.shape[2:]).swapaxes(0, 1)

    idx = jnp.arange(CHUNK)
    lower = idx[:, None] >= idx[None, :]

    def step(s, xs):
        qc, kc, vc, ac = xs
        cum = jnp.cumsum(ac.astype(F32), axis=1)
        cum_h = cum.transpose(0, 2, 1)
        decay = jnp.exp(jnp.where(lower, cum_h[..., :, None] - cum_h[..., None, :], -jnp.inf)).astype(qc.dtype)
        scores = jnp.einsum("bihd,bjhd->bhij", qc, kc) * decay
        y = (jnp.einsum("bhij,bjhe->bihe", scores, vc)
             + jnp.einsum("bihd,bhde->bihe", qc * jnp.exp(cum)[..., None].astype(qc.dtype), s))
        total = cum[:, -1]
        w_in = jnp.exp(total[:, None, :] - cum).astype(kc.dtype)
        s_new = (s * jnp.exp(total)[..., None, None].astype(s.dtype)
                 + jnp.einsum("bjhd,bjhe->bhde", kc * w_in[..., None], vc)).astype(s.dtype)
        return s_new, y

    s_fin, ys = lax.scan(step, s0, (to_chunks(q), to_chunks(k), to_chunks(v), to_chunks(log_a)))
    return ys.swapaxes(0, 1).reshape(b, l, h, dv), s_fin

def bidir_scan(q, k, v_f, v_b, a_f, a_b, s0):
    flip = lambda t: jnp.flip(t, axis=1)
    y_f, s_f = chunked_decay_scan(q, k, v_f, a_f, s0[:, 0])
    y_b, s_b = chunked_decay_scan(flip(q), flip(k), flip(v_b), flip(a_b), s0[:, 1])
    return y_f + flip(y_b), jnp.stack([s_f, s_b], axis=1)

def mixer_ab(h, w_in, w_out, q_gain, k_gain, conv_w, conv_b, dt_bias, a_log, d_skip, ssd_gain,
             s0, rope, cache_k, cache_v):
    b, l, _ = h.shape
    o1 = ATT_WIDTH
    o2 = o1 + ATT_KV_WIDTH
    o3 = o2 + ATT_KV_WIDTH
    o4 = o3 + SSD_WIDTH
    o5 = o4 + SSD_XBC
    q, k, v, z, xbc, dt = jnp.split(h @ w_in, [o1, o2, o3, o4, o5], axis=-1)
    q = rmsnorm(q.reshape(b, l, ATT_HEADS, ATT_HEAD_DIM), q_gain)
    k = rmsnorm(k.reshape(b, l, ATT_KV_HEADS, ATT_HEAD_DIM), k_gain)
    v = v.reshape(b, l, ATT_KV_HEADS, ATT_HEAD_DIM)
    k_ctx, v_ctx = k, v
    if rope is None:
        k_all, v_all = k, v
    else:
        q = apply_rope(q, rope)
        k_all = jnp.concatenate([cache_k, apply_rope(k, rope)], axis=1)
        v_all = jnp.concatenate([cache_v, v], axis=1)
    att = block_attention(q.reshape(b, l, ATT_KV_HEADS, ATT_HEADS // ATT_KV_HEADS, ATT_HEAD_DIM), k_all, v_all)
    xbc = jax.nn.silu(dwconv_centred(xbc, conv_w, conv_b))
    xs, bm, cm = jnp.split(xbc, [SSD_WIDTH, SSD_WIDTH + SSD_GROUPS * SSD_STATE], axis=-1)
    xs = xs.reshape(b, l, SSD_HEADS, SSD_HEAD_DIM)
    rep = SSD_HEADS // SSD_GROUPS
    bm = jnp.repeat(bm.reshape(b, l, SSD_GROUPS, SSD_STATE), rep, axis=2)
    cm = jnp.repeat(cm.reshape(b, l, SSD_GROUPS, SSD_STATE), rep, axis=2)
    dt = jax.nn.softplus(dt.reshape(b, l, 2, SSD_HEADS) + dt_bias)
    a = dt * (-jnp.exp(a_log))
    y, s_fin = bidir_scan(cm, bm, xs * dt[:, :, 0, :, None], xs * dt[:, :, 1, :, None],
                          a[:, :, 0], a[:, :, 1], s0)
    y = y + d_skip[:, None] * xs
    y = rmsnorm(y.reshape(b, l, SSD_WIDTH) * jax.nn.silu(z), ssd_gain)
    out = jnp.concatenate([att, y], axis=-1) @ w_out
    return out, k_ctx, v_ctx, s_fin

def mixer_c(h, w_in, w_out, decay, ret_gain, s0, rope):
    b, l, _ = h.shape
    q, k, v, g = jnp.split(h @ w_in, [RET_QK_WIDTH, 2 * RET_QK_WIDTH, 2 * RET_QK_WIDTH + RET_V_WIDTH], axis=-1)
    q = q.reshape(b, l, RET_HEADS, RET_DK)
    k = k.reshape(b, l, RET_HEADS, RET_DK) * (RET_DK ** -0.5)
    v = v.reshape(b, l, RET_HEADS, RET_DV)
    if rope is not None:
        q = apply_rope(q, rope)
        k = apply_rope(k, rope)
    log_g = (-jnp.exp(decay)).astype(h.dtype)
    a_f = jnp.broadcast_to(log_g[0], (b, l, RET_HEADS))
    a_b = jnp.broadcast_to(log_g[1], (b, l, RET_HEADS))
    y, s_fin = bidir_scan(q, k, v, v, a_f, a_b, s0)
    y = rmsnorm(y, ret_gain.reshape(RET_HEADS, RET_DV))
    out = (jax.nn.silu(g) * y.reshape(b, l, RET_V_WIDTH)) @ w_out
    return out, s_fin

def swiglu(h, w_gate, w_up, w_down):
    return (jax.nn.silu(h @ w_gate) * (h @ w_up)) @ w_down

def setup_inputs(seed: int = 0) -> dict:
    key = jax.random.key(seed)
    ks = iter(jax.random.split(key, 64))
    d = D_MODEL

    def nrm(shape, scale=1.0):
        return jax.random.normal(next(ks), shape, F32) * scale

    def gain(n):
        return 1.0 + nrm((n,), 0.02)

    dt0 = jnp.exp(jax.random.uniform(next(ks), (2, SSD_HEADS), F32, math.log(1e-3), math.log(1e-1)))
    ret_base = jnp.log(-jnp.log1p(-(2.0 ** (-5.0 - jnp.arange(RET_HEADS, dtype=F32)))))
    inp = {}
    inp["x_prompt"] = nrm((BATCH, SEQ, d))
    inp["x_sample"] = nrm((DEC_BATCH, DEC_SEQ, d))
    inp["c"] = nrm((DEC_BATCH, d))
    inp["cache_k0"] = nrm((DEC_BATCH, PAST_LEN, ATT_KV_HEADS, ATT_HEAD_DIM))
    inp["cache_v0"] = nrm((DEC_BATCH, PAST_LEN, ATT_KV_HEADS, ATT_HEAD_DIM))
    inp["state_ssd0"] = nrm((DEC_BATCH, 2, SSD_HEADS, SSD_STATE, SSD_HEAD_DIM), 0.5)
    inp["state_ret1"] = nrm((DEC_BATCH, 2, RET_HEADS, RET_DK, RET_DV), 0.5)
    inp["c_ctx"] = nrm((d,))
    inp["l0_w_ada"] = nrm((d, 6 * d), d ** -0.5)
    inp["l0_b_ada"] = nrm((6 * d,), 0.02)
    inp["l0_norm_mix"] = gain(d)
    inp["l0_norm_ffn"] = gain(d)
    inp["l0_w_in"] = nrm((d, L0_IN), d ** -0.5)
    inp["l0_w_out"] = nrm((ATT_WIDTH + SSD_WIDTH, d), (ATT_WIDTH + SSD_WIDTH) ** -0.5)
    inp["l0_q_gain"] = gain(ATT_HEAD_DIM)
    inp["l0_k_gain"] = gain(ATT_HEAD_DIM)
    inp["l0_conv_w"] = nrm((SSD_CONV, SSD_XBC), SSD_CONV ** -0.5)
    inp["l0_conv_b"] = nrm((SSD_XBC,), 0.02)
    inp["l0_dt_bias"] = dt0 + jnp.log(-jnp.expm1(-dt0))
    inp["l0_a_log"] = jnp.log(jax.random.uniform(next(ks), (2, SSD_HEADS), F32, 1.0, 16.0))
    inp["l0_d_skip"] = 1.0 + nrm((SSD_HEADS,), 0.1)
    inp["l0_ssd_gain"] = gain(SSD_WIDTH)
    inp["l0_w_gate"] = nrm((d, D_FF), d ** -0.5)
    inp["l0_w_up"] = nrm((d, D_FF), d ** -0.5)
    inp["l0_w_down"] = nrm((D_FF, d), D_FF ** -0.5)
    inp["l1_w_ada"] = nrm((d, 6 * d), d ** -0.5)
    inp["l1_b_ada"] = nrm((6 * d,), 0.02)
    inp["l1_norm_mix"] = gain(d)
    inp["l1_norm_ffn"] = gain(d)
    inp["l1_w_in"] = nrm((d, L1_IN), d ** -0.5)
    inp["l1_w_out"] = nrm((RET_V_WIDTH, d), RET_V_WIDTH ** -0.5)
    inp["l1_decay"] = ret_base[None, :] + nrm((2, RET_HEADS), 0.1)
    inp["l1_ret_gain"] = gain(RET_V_WIDTH)
    inp["l1_w_gate"] = nrm((d, D_FF), d ** -0.5)
    inp["l1_w_up"] = nrm((d, D_FF), d ** -0.5)
    inp["l1_w_down"] = nrm((D_FF, d), D_FF ** -0.5)
    inp["final_norm"] = gain(d)
    return inp

def reference(x_prompt, x_sample, c, cache_k0, cache_v0, state_ssd0, state_ret1, c_ctx,
              l0_w_ada, l0_b_ada, l0_norm_mix, l0_norm_ffn, l0_w_in, l0_w_out, l0_q_gain, l0_k_gain,
              l0_conv_w, l0_conv_b, l0_dt_bias, l0_a_log, l0_d_skip, l0_ssd_gain,
              l0_w_gate, l0_w_up, l0_w_down,
              l1_w_ada, l1_b_ada, l1_norm_mix, l1_norm_ffn, l1_w_in, l1_w_out, l1_decay, l1_ret_gain,
              l1_w_gate, l1_w_up, l1_w_down, final_norm):
    layers = (
        dict(w_ada=l0_w_ada, b_ada=l0_b_ada, norm_mix=l0_norm_mix, norm_ffn=l0_norm_ffn,
             w_gate=l0_w_gate, w_up=l0_w_up, w_down=l0_w_down),
        dict(w_ada=l1_w_ada, b_ada=l1_b_ada, norm_mix=l1_norm_mix, norm_ffn=l1_norm_ffn,
             w_gate=l1_w_gate, w_up=l1_w_up, w_down=l1_w_down),
    )

    def trunk(x, cond, rope_att, rope_ret, caches):
        b = x.shape[0]
        ctx_out = []
        for i in range(DEPTH):
            p = layers[i]
            mod = (jax.nn.silu(cond) @ p["w_ada"] + p["b_ada"])[:, None, :]
            sh1, sc1, g1, sh2, sc2, g2 = jnp.split(mod, 6, axis=-1)
            h = rmsnorm(x, p["norm_mix"]) * (1.0 + sc1) + sh1
            if i % 2 == 0:
                if caches is None:
                    ck, cv = None, None
                    s0 = jnp.zeros((b, 2, SSD_HEADS, SSD_STATE, SSD_HEAD_DIM), x.dtype)
                else:
                    ck, cv, s0 = caches[i]
                mix, k_ctx, v_ctx, s_fin = mixer_ab(h, l0_w_in, l0_w_out, l0_q_gain, l0_k_gain, l0_conv_w,
                                                    l0_conv_b, l0_dt_bias, l0_a_log, l0_d_skip, l0_ssd_gain,
                                                    s0, rope_att, ck, cv)
                ctx_out += [k_ctx, v_ctx, s_fin]
            else:
                if caches is None:
                    s0 = jnp.zeros((b, 2, RET_HEADS, RET_DK, RET_DV), x.dtype)
                else:
                    s0 = caches[i][0]
                mix, s_fin = mixer_c(h, l1_w_in, l1_w_out, l1_decay, l1_ret_gain, s0, rope_ret)
                ctx_out += [s_fin]
            x = x + g1 * mix
            h = rmsnorm(x, p["norm_ffn"]) * (1.0 + sc2) + sh2
            x = x + g2 * swiglu(h, p["w_gate"], p["w_up"], p["w_down"])
        return rmsnorm(x, final_norm), ctx_out

    y_prompt, ctx = trunk(x_prompt, c_ctx[None, :], None, None, None)
    new_k0, new_v0, new_ssd0, new_ret1 = ctx
    n_lat = x_sample.shape[1]
    rope_att = axial_rope(n_lat, ATT_HEAD_DIM)
    rope_ret = axial_rope(n_lat, RET_DK)
    caches = ((cache_k0, cache_v0, state_ssd0), (state_ret1,))
    y_sample, _ = trunk(x_sample, c, rope_att, rope_ret, caches)
    return (y_prompt, y_sample, new_k0, new_v0, new_ssd0, new_ret1)


_drawn_inputs = setup_inputs


def setup_inputs(seed=0):
    import zlib

    import numpy as np

    out = dict(_drawn_inputs(seed))
    spreads = {}
    factors = {'cache_k0': 4.174,
     'cache_v0': 2.97,
     'l0_norm_ffn': 3.693,
     'l0_q_gain': 8.0,
     'l0_d_skip': 3.906,
     'l0_ssd_gain': 6.279,
     'l1_norm_mix': 4.167,
     'l1_norm_ffn': 14.414,
     'l1_ret_gain': 7.493,
     'final_norm': 2.675,
     'state_ret1': 4.476}
    for name, (base, spread) in spreads.items():
        noise = np.random.default_rng([zlib.crc32(name.encode()), seed]).standard_normal(out[name].shape)
        drawn = base * np.exp(spread * noise) if base else spread * noise
        out[name] = jnp.asarray(drawn.astype(out[name].dtype))
    for name, factor in factors.items():
        out[name] = (out[name] * factor).astype(out[name].dtype)
    return out
```

```python
import concourse.bass as bass
from concourse import mybir
from contextlib import ExitStack, contextmanager

P = 128
D = 1024
KT = D // P
N_CTX = 128
N_LAT = 512
N = N_CTX + N_LAT
TT = N // P
GRID_W = 64
LT = N_LAT // P
HALF = N // 2
PAST = 128
EPS = 1e-6
HD = 64
NH = 8
NKV = 2
ATT_W = NH * HD
KV_W = NKV * HD
QKV_W = ATT_W + 2 * KV_W
SSD_W = NH * HD
ST = SSD_W // P
XBC_T = ST + 2
TAPS = 5
PADDED = N + 8
RH = 4
DK = 256
DV = 512
VT = DV // P
STRIP = N_LAT + (LT - 1) * P
D_FF = 2816
FT = D_FF // P
CHUNKS = [(0, 8), (8, 8), (16, 6)]
W = 256
SLOT = KT * W
OFF_Z = QKV_W
OFF_X = OFF_Z + SSD_W
OFF_DT = OFF_X + XBC_T * P
DTS = 2 * NH
ATT_SCALE = HD ** -0.5
K_SCALE = DK ** -0.5
ADA_JOBS = 6 * D // W
NM, NF, FIN, COND, CONV_B, SSD_G, CONV_W = (0, 16), (8, 24), 32, 40, 56, 62, 66
N_ROWS = 96
SH, SC, GA = (0, 24), (8, 32), (16, 40)


class Line:

    def __init__(self, eng, own):
        self.e, self.last = eng, own
        self.made, self.took, self.turn, self.per = {}, {}, None, {}

    def value(self, name, n):
        return n if self.turn is None else n + self.turn * self.per.get(name, 0)

    def up(self, name, k=1):
        self.last = name
        return self.told(name, k)

    def told(self, name, k=1):
        self.made[name] = self.made.get(name, 0) + k
        return k

    def ended(self):
        return self.value(self.last, self.made[self.last])

    def next(self, name, k=1):
        self.took[name] = self.took.get(name, 0) + k
        return self.value(name, self.took[name])

    def due(self, name, behind):
        self.next(name)
        assert self.turn is None or self.took[name] > behind, name
        return self.took[name] > behind

    def now(self, name, behind=0):
        return self.value(name, self.took[name] - behind)

    def skip(self, name, k=1):
        self.took[name] = self.took.get(name, 0) + k

    @contextmanager
    def loop(self, turns, per):
        made, took = dict(self.made), dict(self.took)
        with self.e.Fori(0, turns) as i:
            self.turn, self.per = i, per
            yield i
        self.turn = None
        for now, was in ((self.made, made), (self.took, took)):
            for name in now:
                grown = now[name] - was.get(name, 0)
                assert grown in (0, per.get(name, 0)), (name, grown, per)
                now[name] += grown * (turns - 1)


class Sems(dict):

    def __init__(self, nc, ctx):
        super().__init__()
        self.nc, self.ctx = nc, ctx

    def __missing__(self, name):
        self[name] = self.ctx.enter_context(self.nc.semaphore(name))
        return self[name]


class Floor:

    def __init__(self, nc):
        self.nc, self.at, self.top = nc, (nc.sbuf_base + 31) // 32 * 32, nc.sbuf_usable_end

    def __call__(self, name, shape, dt=mybir.dt.float32):
        size = 4
        for n in shape[1:]:
            size *= n
        t = self.nc.alloc_sbuf_tensor_at(name, shape, dt, offset=self.at)
        self.at += (size + 31) // 32 * 32
        assert self.at <= self.top, (name, self.at, self.top)
        return t


def trunk_kernel(nc, I, O):
    f32, f32r = mybir.dt.float32, mybir.dt.float32r
    ALU, ACT = mybir.AluOpType, mybir.ActivationFunctionType
    X = mybir.AxisListType.X
    ctx = ExitStack()
    with ctx:
        sb = Floor(nc)
        xT = sb("xT", [P, KT, N])
        h_at = sb.at
        h_hi, h_lo = sb("h_hi", [P, KT, N], f32r), sb("h_lo", [P, KT, N], f32r)
        h_end = sb.at
        raw = [sb(f"raw{s}", [P, SLOT]) for s in range(2)]
        w_hi = [sb(f"w_hi{s}", [P, SLOT], f32r) for s in range(2)]
        w_lo = [sb(f"w_lo{s}", [P, SLOT], f32r) for s in range(2)]
        ident, upto, onward, ones = (sb(n, [P, P]) for n in ("ident", "upto", "onward", "ones"))
        b_ada = sb("b_ada", [P, 2, 48])
        vec = sb("vec", [P, N_ROWS])
        scond = sb("scond", [P, KT, 2])
        mod = [sb(f"mod{l}", [P, 48, 2]) for l in range(2)]
        gain = [[sb(f"gain{l}{m}", [P, KT, 2]) for m in range(2)] for l in range(2)]
        sq, sq_sum, rB = sb("sq", [P, N]), sb("sq_sum", [P, N]), sb("rB", [P, N])
        stt = sb("stt", [P, 5, TT * 10])
        tbuf = sb("tbuf", [P, 2, N])
        h32 = sb("h32", [P, N])
        phase_at = sb.at

        ada_raw = [sb(f"ada_raw{s}", [P, SLOT]) for s in range(2)]
        part_at = sb.at
        x_stage = sb("x_stage", [P, TT, D])
        stg_a, stg_b = sb("stg_a", [96, P]), sb("stg_b", [N_ROWS, P])
        sb.at = part_at
        conv = sb("conv", [P, XBC_T, PADDED])
        sb.at = part_at + 4 * PADDED
        xpad = sb("xpad", [P, XBC_T, PADDED])
        att_tok = sb("att_tok", [P, TT, ATT_W])
        dt_tok, a_tok = sb("dt_tok", [P, TT, DTS]), sb("a_tok", [P, TT, DTS])
        dt_t = [sb(f"dt_t{i}", [P, TT, DTS]) for i in range(4)]
        dt_c = sb("dt_c", [P, 2, DTS])
        d_skip = sb("d_skip", [P, ST])
        dtw = sb("dtw", [P, KT, DTS])
        dtw_hi, dtw_lo = sb("dtw_hi", [P, KT, DTS], f32r), sb("dtw_lo", [P, KT, DTS], f32r)
        zT = sb("zT", [P, ST, N])
        ctmp = sb("ctmp", [P, PADDED])
        kc, vc = sb("kc", [P, KV_W]), sb("vc", [P, KV_W])
        qk_g = sb("qk_g", [P, 2, HD])
        cosA, sinA = sb("cosA", [P, LT, 32]), sb("sinA", [P, LT, 32])
        s0 = sb("s0", [P, NH, HD])
        qkv_at = sb.at
        qkv = sb("qkv", [P, TT, QKV_W])
        sb.at = h_at
        qT, kT = sb("qT", [P, 4, N]), sb("kT", [P, N + PAST])
        probs, pT = sb("probs", [P, 2, N]), sb("pT", [P, 2, N])
        nmax, rsum, rrec = sb("nmax", [P, 4]), sb("rsum", [P, 4]), sb("rrec", [P, 4])
        sb.at = h_at
        G_LEN = LT * (N_LAT + P)
        Gt = [sb(f"G{g}", [P, G_LEN]) for g in range(2)]
        Gp = sb("Gp", [P, 2, P])
        x_tok = sb("x_tok", [P, TT, SSD_W])
        ecum, ce, ct2 = sb("ecum", [P, N_LAT]), sb("ce", [P, N_LAT]), sb("ct2", [P, N_LAT])
        assert sb.at <= h_end
        sb.at = qkv_at
        y_tok = sb("y_tok", [P, TT, SSD_W])
        cum, ncum = sb("cum", [P, TT, DTS]), sb("ncum", [P, TT, DTS])
        dg, dm = tbuf[:, 0, :].rearrange("p (t n) -> p t n", t=TT), tbuf[:, 1, :].rearrange("p (t n) -> p t n", t=TT)
        tot, wst = sb("tot", [P, DTS]), sb("wst", [P, DTS])
        b_tok = sb("b_tok", [P, 2 * HD])
        bw = sb("bw", [P, 2, 2 * HD])
        s_out = sb("s_out", [P, NH, HD])
        E_off = ada_raw[0][:, :].rearrange("p (j n) -> p j n", j=LT)
        M_off = ada_raw[1][:, :].rearrange("p (j n) -> p j n", j=LT)

        sb.at = part_at
        gu_hi, gu_lo = sb("gu_hi", [P, KT, N], f32r), sb("gu_lo", [P, KT, N], f32r)
        silu_g, gu32 = sb("silu_g", [P, N]), sb("gu32", [P, N])

        sb.at = phase_at
        S0 = sb("S0", [P, 2, 2, DV])
        qk = sb("qk", [P, 4, N])
        qg = sb("qg", [P, 2, N_LAT])
        v_tok = sb("v_tok", [P, TT, DV])
        strip = sb("strip", [P, STRIP])
        sc_sb = sb("sc_sb", [P, 2, N_LAT])
        sc_p = sb("sc_p", [P, P])
        ramp = sb("ramp", [P, 2, N_LAT])
        grow = sb("grow", [P, N_LAT])
        kw = sb("kw", [P, 2, DK])
        pcol, wcol = sb("pcol", [P, 2]), sb("wcol", [P, 2])
        acol = sb("acol", [P, 2])
        rgain = sb("rgain", [P, VT])
        cosR, sinR = sb("cosR", [P, N_LAT]), sb("sinR", [P, N_LAT])
        yg_hi, yg_lo = sb("yg_hi", [P, VT, N], f32r), sb("yg_lo", [P, VT, N], f32r)
        yR = qk

        sb.at = phase_at
        y_out = sb("y_out", [P, TT, D])

        acc = ctx.enter_context(nc.psum_tensor("acc", [P, 4, 512], f32))
        mix = ctx.enter_context(nc.psum_tensor("mix", [P, 4, 512], f32))
        accf, mixf = (t[:, :, :].rearrange("p a b -> p (a b)") for t in (acc, mix))
        ADA = mix[:, 3, 256:256 + 192].rearrange("p (l j c) -> p l j c", l=2, c=2)
        S = Sems(nc, ctx)
        block = ctx.enter_context(nc.Block())

        SEGS = [(0, slice(0, N_CTX), slice(0, N_CTX), 0),
                (0, slice(N_CTX, HALF), slice(N_CTX, HALF), 1),
                (1, slice(0, HALF), slice(HALF, N), 1)]
        PARTS = [(slice(0, N_CTX), 0), (slice(N_CTX, N), 1)]
        tok = lambda t: slice(t * P, (t + 1) * P)
        pad = lambda t: slice(0, P) if t == 0 else slice(4 + t * P, 4 + (t + 1) * P)
        LAT = slice(4 + P, 4 + P + N_LAT)
        pair = lambda r: acc[:, 2 * r:2 * r + 2, 0:HALF]
        halves = lambda t: t.rearrange("p (b n) -> p b n", b=2)
        units = [(t, h) for t in range(TT) for h in range(NH)]

        @block.sync
        def _(eng):
            sp = Line(eng, "sp")
            job, ada = [0], [0]

            def kpn(w):
                return w.rearrange("(k p) n -> p k n", p=P)

            def load(dst, src, name):
                k = dst.shape[1]
                for a, b in ((0, k // 2), (k // 2, k)):
                    eng.dma_start(dst[:, a:b, :], src[:, a:b, :]).then_inc(S[name], sp.up(name, 16))

            def slot():
                s = job[0] % 2
                job[0] += 1
                if sp.due(f"w_lo{s}", 1):
                    eng.wait_ge(S[f"w_lo{s}"], sp.now(f"w_lo{s}", 1))
                return s

            def panel(src, cols=W):
                s = slot()
                k = src.shape[1]
                load(raw[s][:, 0:k * cols].rearrange("p (k n) -> p k n", n=cols), src, f"raw_in{s}")

            def gate_up(gate, up, f):
                s = slot()
                v = raw[s][:, :].rearrange("p (k n) -> p k n", n=W)
                for a, w in ((0, gate), (P, up)):
                    eng.dma_start(v[:, :, a:a + P], kpn(w)[:, :, bass.ds(f, P)]).then_inc(S[f"raw_in{s}"], sp.up(f"raw_in{s}", 16))

            def ada_panel(w, n):
                s = ada[0] % 2
                ada[0] += 1
                if sp.due("ada_used", 2):
                    eng.wait_ge(S["ada_used"], sp.now("ada_used", 2))
                load(ada_raw[s][:, :].rearrange("p (k n) -> p k n", n=W), kpn(w)[:, :, bass.ds(n, W)], f"ada_in{s}")

            def small(dst, src):
                eng.dma_start(dst, src).then_inc(S["setup_in"], sp.up("setup_in", 16))

            rows = lambda a, n=P: a.rearrange("(r c) -> r c", c=n)
            for l in range(2):
                small(stg_a[48 * l:48 * l + 48, :], rows(I[f"l{l}_b_ada"]))
                small(stg_b[NM[l]:NM[l] + KT, :], rows(I[f"l{l}_norm_mix"]))
                small(stg_b[NF[l]:NF[l] + KT, :], rows(I[f"l{l}_norm_ffn"]))
            small(stg_b[FIN:FIN + KT, :], rows(I["final_norm"]))
            small(stg_b[COND:COND + KT, :], rows(I["c_ctx"]))
            small(stg_b[COND + KT:COND + 2 * KT, :], I["c"][0, :].rearrange("(r c) -> r c", c=P))
            small(stg_b[CONV_B:CONV_B + XBC_T, :], rows(I["l0_conv_b"]))
            small(stg_b[SSD_G:SSD_G + ST, :], rows(I["l0_ssd_gain"]))
            small(stg_b[CONV_W:CONV_W + TAPS * XBC_T, :], I["l0_conv_w"].rearrange("k (t c) -> (k t) c", c=P))
            for n, dst in enumerate((ident, upto, onward, ones)):
                small(dst[:, :], I["squares"][n, :, :])
            eng.dma_start(x_stage[:, 0, :], I["x_prompt"][0, :, :]).then_inc(S["x_in"], sp.up("x_in", 16))
            eng.dma_start(x_stage[:, 1:TT, :], I["x_sample"][0, :, :].rearrange("(t p) d -> p t d", p=P)).then_inc(S["x_in"], sp.up("x_in", 16))
            w_in, w_ada = kpn(I["l0_w_in"]), I["l0_w_ada"]
            cols = [i * W for i in range(3)] + [OFF_X + i * W for i in range(3)] + [OFF_Z + i * W for i in range(2)]
            for n in range(8):
                ada_panel(w_ada, n * W)
                if n in (1, 3):
                    panel(w_in[:, :, cols[n // 2]:cols[n // 2] + W])
            eng.wait_ge(S["x_T_read"], sp.next("x_T_read", 10))

            def aside(dst, src, slow=False):
                eng.dma_start(dst, src, allow_slow_non_contiguous=slow).then_inc(S["l0_in"], sp.up("l0_in", 16))

            aside(dtw[:, :, :], w_in[:, :, OFF_DT:OFF_DT + DTS])
            aside(kc[:, :], I["cache_k0"][0].rearrange("t h d -> t (h d)"))
            aside(vc[:, :], I["cache_v0"][0].rearrange("t h d -> t (h d)"))
            aside(qk_g[:, 0, :], I["l0_q_gain"].partition_broadcast(P))
            aside(qk_g[:, 1, :], I["l0_k_gain"].partition_broadcast(P))
            aside(dt_c[:, 0, :], I["l0_dt_bias"].rearrange("a b -> (a b)").partition_broadcast(P))
            aside(dt_c[:, 1, :], I["l0_a_log"].rearrange("a b -> (a b)").partition_broadcast(P))
            for b in range(2):
                aside(d_skip[HD * b:HD * b + HD, :],
                      I["l0_d_skip"].rearrange("(t b) -> b t", b=2)[b, :].partition_broadcast(HD), True)
                aside(s0[HD * b:HD * b + HD, :, :], I["state_ssd0"][0, b].rearrange("h n d -> n h d"))
            aside(cosA[:, :, :], I["rope_att"][0])
            aside(sinA[:, :, :], I["rope_att"][1])
            n = 8
            for j in range(8):
                if j >= 2:
                    panel(w_in[:, :, cols[j]:cols[j] + W])
                if j >= 1:
                    for _ in range(2):
                        ada_panel(w_ada, n * W)
                        n += 1
            for _ in range(2):
                ada_panel(w_ada, n * W)
                n += 1
            assert n == ADA_JOBS
            eng.wait_ge(S["new_kv"], sp.next("new_kv"))
            for k, src in enumerate((qkv[:, 0, ATT_W:ATT_W + KV_W], qkv[:, 0, ATT_W + KV_W:QKV_W])):
                eng.dma_start(O[2 + k][0].rearrange("t h d -> t (h d)"), src).then_inc(S["kv_out"], sp.up("kv_out", 16))
            eng.wait_ge(S[sp.last], sp.ended())
            eng.sem_inc(S["kv_gone"], sp.told("kv_gone"))
            for j in range(4):
                panel(kpn(I["l0_w_out"])[:, :, j * W:j * W + W])
            eng.wait_ge(S["s_out_ready"], sp.next("s_out_ready"))
            for b in range(2):
                eng.dma_start(O[4][0, b].rearrange("h n d -> n h d"), s_out[HD * b:HD * b + HD, :, :]).then_inc(S["out"], sp.up("out", 16))
            eng.wait_ge(S["l0_mixed"], sp.next("l0_mixed"))
            for n in range(2):
                ada_panel(I["l1_w_ada"], n * W)

            def ffn(l):
                gate, up, down = (I[f"l{l}_w_{n}"] for n in ("gate", "up", "down"))
                for f0, nf in CHUNKS:
                    per = {"w_lo0": 1, "w_lo1": 1, "raw_in0": 32, "raw_in1": 32}
                    if l == 0:
                        per |= {"ada_used": 2, "ada_in0": 32, "ada_in1": 32}
                    with sp.loop(nf // 2, per) as i:
                        for s in range(2):
                            gate_up(gate, up, (i * 2 + s + f0) * P)
                            if l == 0:
                                ada_panel(I["l1_w_ada"], (i * 2 + s + f0 + 2) * W)
                    for j in range(4):
                        panel(kpn(down)[:, f0:f0 + nf, j * W:j * W + W])

            ffn(0)
            w_in, w_out = kpn(I["l1_w_in"]), I["l1_w_out"]
            per = {"raw_in0": 128, "raw_in1": 128, "w_lo0": 4, "w_lo1": 4}
            with sp.loop(RH, per) as h:
                panel(w_in[:, :, bass.ds(h * DK, W)])
                panel(w_in[:, :, bass.ds(h * DK + D, W)])
                for j in range(2):
                    panel(w_in[:, :, bass.ds(h * DV + j * W + 2 * D, W)])
                for j in range(2):
                    panel(w_in[:, :, bass.ds(h * DV + j * W + 4 * D, W)])
                for j in range(2):
                    panel(w_out.rearrange("(h k p) n -> p (h k) n", p=P, k=VT)[:, bass.ds(h * VT, VT), j * 2 * W:(j + 1) * 2 * W], 2 * W)
            ffn(1)
            eng.wait_ge(S["y_ready"], sp.next("y_ready", 10))
            eng.dma_start(O[0][0], y_out[:, 0, :]).then_inc(S["out"], sp.up("out", 16))
            eng.dma_start(O[1][0].rearrange("(t p) d -> p t d", p=P), y_out[:, 1:TT, :]).then_inc(S["out"], sp.up("out", 16))
            eng.wait_ge(S[sp.last], sp.ended())
            for b in range(2):
                eng.wait_ge(S[f"fs_out{b}"], 32 * RH)

        @block.tensor
        def _(eng):
            pe = Line(eng, "pe")
            job, tile, ada = [0], [0], [0]
            mm = eng.matmul

            def next_tile():
                r = tile[0] % 2
                tile[0] += 1
                if pe.due(f"acc_free{r}", 1):
                    eng.wait_ge(S[f"acc_free{r}"], pe.now(f"acc_free{r}", 1))
                return r

            def next_job():
                s = job[0] % 2
                job[0] += 1
                eng.wait_ge(S[f"w_lo{s}"], pe.next(f"w_lo{s}"))
                return s

            def tile_a(s, xh, xl, kts, col, cols=W, came=None):
                r = next_tile()
                for k in range(kts):
                    if came:
                        eng.wait_ge(S[came], pe.next(came))
                    for n, (w, x) in enumerate(((w_hi[s], xh), (w_hi[s], xl), (w_lo[s], xh))):
                        for b in range(2):
                            last = mm(acc[:, 2 * r + b, 0:HALF], w[:, k * cols + col:k * cols + col + P],
                                      x[:, k, b * HALF:(b + 1) * HALF],
                                      start=(k == 0 and n == 0), stop=(k == kts - 1 and n == 2))
                last.then_inc(S[f"acc_ready{r}"], pe.up(f"acc_ready{r}"))

            def tile_b(s, t, came=None):
                r = next_tile()
                for k in range(KT):
                    if came:
                        eng.wait_ge(S[came], pe.next(came))
                    for n, (x, w) in enumerate(((h_hi, w_hi[s]), (h_hi, w_lo[s]), (h_lo, w_hi[s]))):
                        last = mm(acc[:, 2 * r, 0:W], x[:, k, tok(t)], w[:, k * W:(k + 1) * W],
                                  start=(k == 0 and n == 0), stop=(k == KT - 1 and n == 2))
                last.then_inc(S[f"acc_ready{r}"], pe.up(f"acc_ready{r}"))

            def ada_job(l, n):
                s = ada[0] % 2
                ada[0] += 1
                eng.wait_ge(S[f"ada_in{s}"], pe.next(f"ada_in{s}", 32))
                for c in range(2):
                    for k in range(KT):
                        last = mm(ADA[:, l, bass.ds(n * 2 + c, 1), :].rearrange("p o c -> p (o c)"),
                                  ada_raw[s][:, k * W + c * P:k * W + (c + 1) * P], scond[:, k, :],
                                  start=(k == 0), stop=(k == KT - 1))
                last.then_inc(S["ada_used"], pe.up("ada_used"))

            def rms():
                eng.wait_ge(S["sq_done"], pe.next("sq_done"))
                for t in range(TT):
                    last = mm(mixf[:, t:t + 1], sq_sum[:, tok(t)], ones[:, 0:1], start=True, stop=True)
                last.then_inc(S["stat"], pe.up("stat"))
                eng.wait_ge(S["rinv"], pe.next("rinv"))
                for t in range(TT):
                    last = mm(mixf[:, 512 + t * P:512 + (t + 1) * P],
                              stt[:, 4, t:t + 1].broadcast_to([P, P]), ident[:, :], start=True, stop=True)
                last.then_inc(S["rb"], pe.up("rb"))

            eng.wait_ge(S["setup_in"], pe.next("setup_in", 16 * 16))
            eng.transpose(mix[:, 0, 0:96], stg_a[:, :], ident[0:96, 0:96])
            eng.transpose(mix[:, 0, 96:96 + N_ROWS], stg_b[:, :], ident[0:N_ROWS, 0:N_ROWS]).then_inc(S["vec_T"], pe.up("vec_T"))
            eng.wait_ge(S["x_in"], pe.next("x_in", 32))
            for n in range(2 * TT):
                t, half = divmod(n, 2)
                if pe.due("x_T_read", 2):
                    eng.wait_ge(S["x_T_read"], pe.now("x_T_read", 2))
                for k in range(4):
                    last = eng.transpose(acc[:, n % 2, k * P:(k + 1) * P],
                                         x_stage[:, t, (half * 4 + k) * P:(half * 4 + k + 1) * P], ident[:, :])
                last.then_inc(S["x_T"], pe.up("x_T"))
            eng.wait_ge(S["cond"], pe.next("cond"))
            for n in range(8):
                ada_job(0, n)
            rms()
            eng.wait_ge(S["mod_read"], pe.next("mod_read"))
            eng.wait_ge(S["x_T_read"], pe.now("x_T_read"))
            n = 8
            for j in range(8):
                s = next_job()
                if j < 3:
                    for t in range(TT):
                        tile_b(s, t, "h_ready" if j == 0 and t == 0 else None)
                else:
                    for c in range(2):
                        tile_a(s, h_hi, h_lo, KT, c * P)
                if j == 5:
                    eng.wait_ge(S["dtw_lo"], pe.next("dtw_lo"))
                    r = next_tile()
                    for t in range(TT):
                        for k in range(KT):
                            for m, (x, w) in enumerate(((h_hi, dtw_hi), (h_hi, dtw_lo), (h_lo, dtw_hi))):
                                last = mm(acc[:, 2 * r, t * DTS:(t + 1) * DTS], x[:, k, tok(t)], w[:, k, :],
                                          start=(k == 0 and m == 0), stop=(k == KT - 1 and m == 2))
                    last.then_inc(S[f"acc_ready{r}"], pe.up(f"acc_ready{r}"))
                for _ in range(2):
                    ada_job(0, n)
                    n += 1
            eng.wait_ge(S["acc_free0"], pe.now("acc_free0"))
            eng.wait_ge(S["acc_free1"], pe.now("acc_free1"))
            eng.wait_ge(S["l0_in"], pe.next("l0_in", 16 * 13))
            eng.wait_ge(S["roped"], pe.next("roped"))
            for t in range(TT):
                eng.transpose(accf[:, t * P:(t + 1) * P], qkv[:, t, ATT_W:ATT_W + KV_W], ident[:, :])
            eng.transpose(accf[:, N:N + PAST], kc[:, :], ident[:, :]).then_inc(S["kT_made"], pe.up("kT_made"))
            for t in range(TT):
                if pe.due("qT_sb", 2):
                    eng.wait_ge(S["qT_sb"], pe.now("qT_sb", 2))
                for j in range(4):
                    last = eng.transpose(acc[:, 2 + t % 2, j * P:(j + 1) * P], qkv[:, t, j * P:(j + 1) * P], ident[:, :])
                last.then_inc(S["qT_made"], pe.up("qT_made"))
            eng.wait_ge(S["qT_sb"], pe.now("qT_sb"))
            U = len(units)
            for i in range(U + 2):
                if i < U:
                    t, h = units[i]
                    b, g = i % 2, h // 4
                    if pe.due("exp_done", 2):
                        eng.wait_ge(S["exp_done"], pe.now("exp_done", 2))
                    q = qT[HD * g:HD * g + HD, h % 4, tok(t)]
                    spans = [(0, N_CTX, 0)] if t == 0 else [(0, 512, P), (512, P, P + 512)]
                    for at, n_, k0 in spans:
                        last = mm(mixf[:, 1024 * b + at:1024 * b + at + n_], q, kT[HD * g:HD * g + HD, k0:k0 + n_],
                                  start=True, stop=True)
                    last.then_inc(S["scores"], pe.up("scores"))
                if 1 <= i <= U:
                    t, h = units[i - 1]
                    b = (i - 1) % 2
                    eng.wait_ge(S["exp_done"], i)
                    if pe.due("att_read", 2):
                        eng.wait_ge(S["att_read"], pe.now("att_read", 2))
                    for m in range(1 if t == 0 else TT):
                        last = eng.transpose(accf[:, 1024 * b + m * P:1024 * b + (m + 1) * P],
                                             probs[:, b, m * P:(m + 1) * P], ident[:, :])
                    last.then_inc(S["pT_made"], pe.up("pT_made"))
                if i >= 2:
                    t, h = units[i - 2]
                    b, g = i % 2, h // 4
                    eng.wait_ge(S["pT_sb"], pe.next("pT_sb"))
                    vs = [qkv[:, t_, ATT_W + KV_W + HD * g:ATT_W + KV_W + HD * g + HD] for t_ in ([0] if t == 0 else range(1, TT))]
                    if t:
                        vs.append(vc[:, HD * g:HD * g + HD])
                    for m, v in enumerate(vs):
                        last = mm(accf[:, 1024 * b + 768:1024 * b + 768 + HD], pT[:, b, m * P:(m + 1) * P], v,
                                  start=(m == 0), stop=(m == len(vs) - 1))
                    last.then_inc(S["att_made"], pe.up("att_made"))
            eng.wait_ge(S["att_read"], U)
            eng.wait_ge(S["exp_done"], U)
            eng.wait_ge(S["a_ready"], pe.next("a_ready"))
            for t in range(TT):
                for d in range(2):
                    tri = (upto, onward)[d]
                    others = [] if t == 0 else (range(1, t) if d == 0 else range(t + 1, TT))
                    parts = [(ones, t_) for t_ in others] + [(tri, t)]
                    for m, (w, t_) in enumerate(parts):
                        last = mm(mixf[:, t * DTS + NH * d:t * DTS + NH * d + NH], w[:, :], a_tok[:, t_, NH * d:NH * d + NH],
                                  start=(m == 0), stop=(m == len(parts) - 1))
            last.then_inc(S["cum_made"], pe.up("cum_made"))
            eng.wait_ge(S["conv_ready"], pe.next("conv_ready"))
            for t in range(TT):
                if pe.due("xt_read", 2):
                    eng.wait_ge(S["xt_read"], pe.now("xt_read", 2))
                for j in range(ST):
                    last = eng.transpose(acc[:, t % 2, j * P:(j + 1) * P], conv[:, j, pad(t)], ident[:, :])
                last.then_inc(S["xt_made"], pe.up("xt_made"))
            eng.transpose(acc[:, 2, 0:P], conv[:, ST, pad(0)], ident[:, :]).then_inc(S["bt_made"], pe.up("bt_made"))
            for g in range(2):
                B, C = (conv[HD * g:HD * g + HD, ST + m, :] for m in range(2))
                for J in range(LT):
                    n = g * (LT + 1) + J
                    if pe.due("cb_read", 2):
                        eng.wait_ge(S["cb_read"], pe.now("cb_read", 2))
                    mm(mix[:, 1 + n % 2, :], B[:, pad(J + 1)], C[:, LAT], start=True, stop=True).then_inc(S["cb_made"], pe.up("cb_made"))
                n += 1
                if pe.due("cb_read", 2):
                    eng.wait_ge(S["cb_read"], pe.now("cb_read", 2))
                mm(mix[:, 1 + n % 2, 0:P], B[:, pad(0)], C[:, pad(0)], start=True, stop=True).then_inc(S["cb_made"], pe.up("cb_made"))
            eng.wait_ge(S["cum_read"], pe.next("cum_read"))
            eng.wait_ge(S["xt_read"], TT)
            eng.wait_ge(S["bt_read"], 1)
            eng.wait_ge(S["cb_read"], 2 * (LT + 1))
            for h in range(NH + 1):
                if h < NH:
                    if pe.due("rows_read", 1):
                        eng.wait_ge(S["rows_read"], pe.now("rows_read", 1))
                    for d in range(2):
                        for t in range(TT):
                            c = cum[:, t, NH * d + h:NH * d + h + 1].broadcast_to([P, P])
                            last = mm(accf[:, 1024 * d + t * P:1024 * d + (t + 1) * P], c, ident[:, :], start=True, stop=True)
                    last.then_inc(S["rows_made"], pe.up("rows_made"))
                if h >= 1:
                    g = h - 1
                    eng.wait_ge(S["m_ready"], pe.next("m_ready"))
                    if pe.due("y_read", 2):
                        eng.wait_ge(S["y_read"], pe.now("y_read", 2))
                    cols = slice(g * HD, (g + 1) * HD)
                    bank = mix[:, g % 2, 0:TT * HD]
                    mm(bank[:, 0:HD], dg[:, 0, :], x_tok[:, 0, cols], start=True, stop=True)
                    for I_ in range(LT):
                        o = bank[:, (I_ + 1) * HD:(I_ + 2) * HD]
                        for J in range(LT):
                            m_ = dg[:, I_ + 1, :] if J == I_ else M_off[:, J, I_ * P:(I_ + 1) * P]
                            mm(o, m_, x_tok[:, J + 1, cols], start=(J == 0), stop=False)
                        last = mm(o, ce[:, I_ * P:(I_ + 1) * P], s0[:, g, :], start=False, stop=True)
                    last.then_inc(S["y_made"], pe.up("y_made"))
            for h in range(NH):
                eng.wait_ge(S["bw_ready"], pe.next("bw_ready"))
                mm(mix[:, 2, h * HD:(h + 1) * HD], bw[:, h % 2, :], x_tok[:, 0, h * HD:(h + 1) * HD], start=True, stop=True).then_inc(S["fs_made"], pe.up("fs_made"))
            eng.wait_ge(S["y_read"], NH)
            for t in range(TT):
                if pe.due("yT_read", 2):
                    eng.wait_ge(S["yT_read"], pe.now("yT_read", 2))
                for j in range(ST):
                    last = eng.transpose(acc[:, t % 2, j * P:(j + 1) * P], y_tok[:, t, j * P:(j + 1) * P], ident[:, :])
                last.then_inc(S["yT_made"], pe.up("yT_made"))
            eng.wait_ge(S["s_out_ready"], 1)
            rms()
            for t in range(TT):
                if pe.due("aT_read", 2):
                    eng.wait_ge(S["aT_read"], pe.now("aT_read", 2))
                for j in range(ST):
                    last = eng.transpose(acc[:, 2 + t % 2, j * P:(j + 1) * P], att_tok[:, t, j * P:(j + 1) * P], ident[:, :])
                last.then_inc(S["aT_made"], pe.up("aT_made"))
            eng.wait_ge(S["yT_read"], TT)
            eng.wait_ge(S["aT_read"], TT)
            for j in range(4):
                s = next_job()
                if j == 0:
                    eng.wait_ge(S["h_ready"], pe.next("h_ready", TT + ST))
                tile_a(s, h_hi, h_lo, KT, 0)
                tile_a(s, h_hi, h_lo, KT, P)
                if j < 2:
                    if j == 0:
                        eng.wait_ge(S["mod_read"], pe.next("mod_read"))
                    ada_job(1, j)

            def ffn(l):
                rms()
                if l == 0:
                    pass
                first = True
                for f0, nf in CHUNKS:
                    per = {"w_lo0": 1, "w_lo1": 1, "acc_free0": 2, "acc_free1": 2, "acc_ready0": 2, "acc_ready1": 2}
                    if l == 0:
                        per |= {"ada_in0": 32, "ada_in1": 32, "ada_used": 2}
                    if first:
                        for k in range(KT):
                            eng.wait_ge(S["h_ready"], pe.next("h_ready"))
                        first = False
                    with pe.loop(nf // 2, per) as i:
                        for s_ in range(2):
                            s = next_job()
                            tile_a(s, h_hi, h_lo, KT, 0)
                            tile_a(s, h_hi, h_lo, KT, P)
                            if l == 0:
                                ada_job(1, i * 2 + s_ + f0 + 2)
                    for j in range(4):
                        s = next_job()
                        tile_a(s, gu_hi, gu_lo, nf, 0, came="gu_ready" if j == 0 else None)
                        tile_a(s, gu_hi, gu_lo, nf, P)

            ffn(0)
            rms()
            for k in range(KT):
                eng.wait_ge(S["h_ready"], pe.next("h_ready"))
            per = {"w_lo0": 4, "w_lo1": 4, "acc_free0": 13, "acc_free1": 13, "acc_ready0": 13, "acc_ready1": 13,
                   "rope_done": 1, "kp_made": 1, "kw_ready": 1, "head_in": 16 * 8, "score_made": 5, "sc_ready": 5,
                   "y_part": 5, "qg_ready": 2, "state_done": 2, "v_in": 1, "fs_made1": 4, "fs_read": 4, "yr_read": 1,
                   "sq_done": 1, "stat": 1, "rinv": 1, "rb": 1, "yg_ready": 4}
            with pe.loop(RH, per):
                for j in range(2):
                    s = next_job()
                    for c in range(2):
                        tile_a(s, h_hi, h_lo, KT, c * P)
                for j in range(2):
                    s = next_job()
                    for t in range(TT):
                        tile_b(s, t)
                eng.wait_ge(S["acc_free0"], pe.now("acc_free0"))
                eng.wait_ge(S["acc_free1"], pe.now("acc_free1"))
                eng.wait_ge(S["rope_done"], pe.next("rope_done"))
                for k in range(2):
                    last = eng.transpose(mix[:, 0, k * P:(k + 1) * P], qk[:, 2 + k, 0:P], ident[:, :])
                last.then_inc(S["kp_made"], pe.up("kp_made"))

                def score(J):
                    n = N_LAT if J < LT else N_CTX
                    i0, j0 = (N_CTX, (J + 1) * P) if J < LT else (0, 0)
                    for k in range(2):
                        last = mm(mix[:, 1 + J % 2, 0:n], qk[:, 2 + k, j0:j0 + P], qk[:, k, i0:i0 + n],
                                  start=(k == 0), stop=(k == 1))
                    last.then_inc(S["score_made"], pe.up("score_made"))

                def states(b):
                    eng.wait_ge(S["qg_ready"], pe.next("qg_ready"))
                    for v in range(VT):
                        for k in range(2):
                            last = mm(acc[:, v, :], S0[:, b, k, v * P:(v + 1) * P], qg[:, k, :],
                                      start=(b == 0 and k == 0), stop=(b == 1 and k == 1))
                    last.then_inc(S["state_done"], pe.up("state_done"))

                score(0)
                score(1)
                eng.wait_ge(S["head_in"], pe.next("head_in", 16 * 8))
                states(0)
                eng.wait_ge(S["v_in"], pe.next("v_in"))
                for J in range(LT + 1):
                    eng.wait_ge(S["sc_ready"], pe.next("sc_ready"))
                    if J == LT:
                        eng.wait_ge(S["kw_ready"], pe.next("kw_ready"))
                    for v in range(VT):
                        if J < LT:
                            last = mm(acc[:, v, :], v_tok[:, J + 1, v * P:(v + 1) * P], sc_sb[:, J % 2, :], start=False, stop=False)
                        else:
                            last = mm(mix[:, 0, v * P:(v + 1) * P], v_tok[:, 0, v * P:(v + 1) * P], sc_p[:, :], start=True, stop=True)
                    last.then_inc(S["y_part"], pe.up("y_part"))
                    if J + 2 <= LT:
                        score(J + 2)
                states(1)
                for n in range(4):
                    b, k = divmod(n, 2)
                    if n >= 2:
                        eng.wait_ge(S["fs_read"], pe.next("fs_read"))
                    mm(mix[:, 1 + n % 2, :], kw[:, b, k * P:(k + 1) * P], v_tok[:, 0, :], start=True, stop=True).then_inc(S["fs_made1"], pe.up("fs_made1"))
                eng.wait_ge(S["fs_read"], pe.next("fs_read", 2))
                eng.wait_ge(S["yr_read"], pe.next("yr_read"))
                s = next_job()
                for c in range(2):
                    tile_a(s, h_hi, h_lo, KT, c * P)
                rms()
                s = next_job()
                for c in range(2):
                    tile_a(s, h_hi, h_lo, KT, c * P)
                for j in range(2):
                    s = next_job()
                    for c in range(4):
                        tile_a(s, yg_hi, yg_lo, VT, c * P, 2 * W, came="yg_ready" if j == c == 0 else None)
            ffn(1)
            rms()
            for t in range(TT):
                for half in range(2):
                    n = 2 * t + half
                    if n == 0:
                        eng.wait_ge(S["final_ready"], pe.next("final_ready"))
                    if pe.due("y_ready", 2):
                        eng.wait_ge(S["y_ready"], pe.now("y_ready", 2))
                    for k in range(4):
                        last = eng.transpose(acc[:, n % 2, k * P:(k + 1) * P], xT[:, half * 4 + k, tok(t)], ident[:, :])
                    last.then_inc(S["out_T"], pe.up("out_T"))

        @block.scalar
        def _(eng):
            ac = Line(eng, "act")
            act = eng.activation
            job, tile = [0], [0]

            def split_hi():
                s = job[0] % 2
                job[0] += 1
                eng.wait_ge(S[f"raw_in{s}"], ac.next(f"raw_in{s}", 32))
                act(w_hi[s][:, :], raw[s][:, :], ACT.Copy).then_inc(S[f"w_hi{s}"], ac.up(f"w_hi{s}"))

            def tile_of():
                r = tile[0] % 2
                tile[0] += 1
                eng.wait_ge(S[f"acc_ready{r}"], ac.next(f"acc_ready{r}"))
                return r

            def pass_tiles(n):
                for _ in range(n - 1):
                    ac.skip(f"acc_ready{tile[0] % 2}")
                    tile[0] += 1
                tile_of()

            def root(n=TT):
                eng.wait_ge(S["mean"], ac.next("mean"))
                act(stt[:, 1, 0:n], stt[:, 0, 0:n], ACT.Sqrt).then_inc(S["root"], ac.up("root"))

            def modulate(l, m):
                for k in range(KT):
                    eng.wait_ge(S["normed"], ac.next("normed"))
                    for cols, c in PARTS:
                        ins = act(h_hi[:, k, cols], tbuf[:, k % 2, cols], ACT.Identity,
                                  bias=mod[l][:, SH[m] + k, c:c + 1], scale=gain[l][m][:, k, c:c + 1])
                    ins.then_inc(S["h_hi"], ac.up("h_hi"))

            eng.wait_ge(S["vec_read"], ac.next("vec_read"))
            act(scond[:, :, :].rearrange("p k c -> p c k"),
                       vec[:, COND:COND + 2 * KT].rearrange("p (c k) -> p c k", c=2), ACT.Silu).then_inc(S["cond"], ac.up("cond"))
            split_hi()
            split_hi()
            root()
            eng.wait_ge(S["gain_ready"], ac.next("gain_ready"))
            modulate(0, 0)
            eng.wait_ge(S["l0_in"], ac.next("l0_in", 16 * 13))
            act(dtw_hi[:, :, :], dtw[:, :, :], ACT.Copy).then_inc(S["dtw_hi"], ac.up("dtw_hi"))
            for j in range(8):
                if j < 3:
                    for t in range(TT):
                        r = tile_of()
                        dst, src = qkv[:, t, j * W:(j + 1) * W], acc[:, 2 * r, 0:W]
                        if j < 2:
                            dst = qkv[:, t, 0:ATT_W].rearrange("p (i g d) -> p i g d", g=2, d=HD)[:, :, j, :]
                            src = src.rearrange("p (i d) -> p i d", d=HD)
                        act(dst, src, ACT.Copy).then_inc(S["act"], ac.up("act"))
                        eng.wait_ge(S[ac.last], ac.ended())
                        eng.sem_inc(S[f"acc_free{r}"], ac.told(f"acc_free{r}"))
                    if j == 2:
                        eng.wait_ge(S[ac.last], ac.ended())
                        eng.sem_inc(S["qkv_in"], ac.told("qkv_in"))
                else:
                    for c in range(2):
                        r = tile_of()
                        i = (j - 3) * 2 + c
                        if j < 6:
                            for b, src, dst, _ in SEGS:
                                o = 2 if dst.start == 0 else 6
                                ins = act(xpad[:, i, dst.start + o:dst.stop + o], acc[:, 2 * r + b, src], ACT.Copy)
                            ins.then_inc(S["act"], ac.up("act"))
                            eng.wait_ge(S[ac.last], ac.ended())
                            eng.sem_inc(S[f"acc_free{r}"], ac.told(f"acc_free{r}"))
                            eng.wait_ge(S[ac.last], ac.ended())
                            eng.sem_inc(S["xb_in"], ac.told("xb_in"))
                        else:
                            act(halves(zT[:, i - 6, :]), pair(r), ACT.Silu).then_inc(S["act"], ac.up("act"))
                            eng.wait_ge(S[ac.last], ac.ended())
                            eng.sem_inc(S[f"acc_free{r}"], ac.told(f"acc_free{r}"))
                if j == 5:
                    r = tile_of()
                    act(dt_tok[:, :, :].rearrange("p t c -> p (t c)"), acc[:, 2 * r, 0:TT * DTS], ACT.Copy).then_inc(S["act"], ac.up("act"))
                    eng.wait_ge(S[ac.last], ac.ended())
                    eng.sem_inc(S[f"acc_free{r}"], ac.told(f"acc_free{r}"))
                    eng.wait_ge(S[ac.last], ac.ended())
                    eng.sem_inc(S["dt_in"], ac.told("dt_in"))
                split_hi()
                if j == 3:
                    root(TT * 10)
            eng.wait_ge(S["dt_abs"], ac.next("dt_abs"))
            act(dt_t[1][:, :, :], dt_t[1][:, :, :], ACT.Exp, scale=-1.0).then_inc(S["dt_exp"], ac.up("dt_exp"))
            eng.wait_ge(S["dt_u"], ac.next("dt_u"))
            act(dt_t[3][:, :, :], dt_t[0][:, :, :], ACT.Ln)
            act(dt_c[:, 1, :], dt_c[:, 1, :], ACT.Exp).then_inc(S["dt_ln"], ac.up("dt_ln"))
            eng.wait_ge(S["kT_made"], ac.next("kT_made"))
            act(kT[:, :], accf[:, 0:N + PAST], ACT.Copy).then_inc(S["act"], ac.up("act"))
            for t in range(TT):
                eng.wait_ge(S["qT_made"], ac.next("qT_made"))
                act(qT[:, :, tok(t)], acc[:, 2 + t % 2, :].rearrange("p (j n) -> p j n", j=4), ACT.Copy).then_inc(S["qT_sb"], ac.up("qT_sb"))
            for u, (t, h) in enumerate(units):
                b = u % 2
                n = N_CTX if t == 0 else N
                eng.wait_ge(S["max_ready"], ac.next("max_ready"))
                if ac.due("pT_made", 2):
                    eng.wait_ge(S["pT_made"], ac.now("pT_made", 2))
                act(probs[:, b, 0:n], mixf[:, 1024 * b:1024 * b + n], ACT.Exp, bias=nmax[:, u % 4:u % 4 + 1],
                           scale=ATT_SCALE, accum_out=rsum[:, u % 4:u % 4 + 1]).then_inc(S["exp_done"], ac.up("exp_done"))
            for i in range(XBC_T):
                eng.wait_ge(S["conv_raw"], ac.next("conv_raw"))
                for cols in (slice(0, N_CTX), LAT):
                    ins = act(conv[:, i, cols], conv[:, i, cols], ACT.Silu, bias=vec[:, CONV_B + i:CONV_B + i + 1])
            ins.then_inc(S["conv_ready"], ac.up("conv_ready"))
            eng.wait_ge(S["cum_read"], ac.next("cum_read"))
            for h in range(NH):
                eng.wait_ge(S["arg_ready"], ac.next("arg_ready"))
                act(tbuf[:, 0, :], tbuf[:, 0, :], ACT.Exp).then_inc(S["diag_exp"], ac.up("diag_exp"))
                if ac.due("m_ready", 1):
                    eng.wait_ge(S["m_ready"], ac.now("m_ready", 1))
                for J in range(LT):
                    if J < LT - 1:
                        act(E_off[:, J, (J + 1) * P:], accf[:, (J + 2) * P:N], ACT.Exp, bias=ncum[:, J + 1, h:h + 1])
                    if J:
                        act(E_off[:, J, 0:J * P], accf[:, 1024 + P:1024 + (J + 1) * P], ACT.Exp,
                            bias=ncum[:, J + 1, NH + h:NH + h + 1])
                for b in range(2):
                    ins = act(ecum[HD * b:HD * b + HD, :], accf[HD * b:HD * b + HD, 1024 * b + P:1024 * b + N], ACT.Exp)
                ins.then_inc(S["rows_read"], ac.up("rows_read"))
            eng.wait_ge(S["wst_arg"], ac.next("wst_arg"))
            act(wst[:, :], wst[:, :], ACT.Exp).then_inc(S["wst_exp"], ac.up("wst_exp"))
            root()
            for t in range(TT):
                eng.wait_ge(S["aT_made"], ac.next("aT_made"))
                act(h_hi[:, 0:ST, tok(t)], acc[:, 2 + t % 2, :].rearrange("p (j n) -> p j n", j=4), ACT.Copy).then_inc(S["h_hi"], ac.up("h_hi"))
            for j in range(ST):
                eng.wait_ge(S["y32_ready"], ac.next("y32_ready"))
                act(h_hi[:, ST + j, :], h32[:, :], ACT.Copy).then_inc(S["h_hi"], ac.up("h_hi"))
            for j in range(4):
                pass_tiles(2)
                split_hi()

            def ffn(l):
                root()
                if l == 0:
                    eng.wait_ge(S["gain_ready"], ac.next("gain_ready"))
                modulate(l, 1)
                for f0, nf in CHUNKS:
                    per = {"acc_ready0": 2, "acc_ready1": 2, "acc_free0": 2, "silu_ready": 2, "gu32_ready": 2, "gu_hi": 2,
                           "gu_ready": 2, "raw_in0": 32, "raw_in1": 32, "w_hi0": 1, "w_hi1": 1, "act": 2}
                    with ac.loop(nf // 2, per) as i:
                        for s in range(2):
                            r = tile_of()
                            act(halves(silu_g[:, :]), pair(r), ACT.Silu).then_inc(S["act"], ac.up("act"))
                            eng.wait_ge(S[ac.last], ac.ended())
                            eng.sem_inc(S[f"acc_free{r}"], ac.told(f"acc_free{r}"))
                            eng.wait_ge(S[ac.last], ac.ended())
                            eng.sem_inc(S["silu_ready"], ac.told("silu_ready"))
                            tile_of()
                            split_hi()
                            eng.wait_ge(S["gu32_ready"], ac.next("gu32_ready"))
                            act(gu_hi[:, bass.ds(i * 2 + s, 1), :].rearrange("p o n -> p (o n)"), gu32[:, :], ACT.Copy).then_inc(S["gu_hi"], ac.up("gu_hi"))
                    for j in range(4):
                        pass_tiles(2)
                        if not (l == 1 and f0 == CHUNKS[-1][0] and j >= 2):
                            split_hi()

            ffn(0)
            root()
            eng.wait_ge(S["gain_ready"], ac.next("gain_ready"))
            modulate(1, 0)
            per = {"acc_ready0": 13, "acc_ready1": 13, "acc_free0": 9, "acc_free1": 9, "raw_in0": 128, "raw_in1": 128,
                   "w_hi0": 4, "w_hi1": 4, "qk_in": 1, "v_in": 1, "acol_ready": 1, "head_in": 128, "decay_exp": 1, "arg1_ready": 1, "strip_exp": 1,
                   "grow_used": 2, "grow_ready": 2, "wcol_ready": 1, "mean": 1, "root": 1, "z32_ready": 4, "yg_hi": 4, "yg_ready": 4,
                   "g_in": 4, "fs_made1": 4, "fs_read": 4, "act": 18}
            with ac.loop(RH, per):
                eng.wait_ge(S["head_in"], ac.next("head_in", 128))
                act(acol[:, :], acol[:, :], ACT.Exp).then_inc(S["decay_exp"], ac.up("decay_exp"))
                for j in range(2):
                    for c in range(2):
                        r = tile_of()
                        act(halves(qk[:, 2 * j + c, :]), pair(r), ACT.Copy, scale=1.0 if j == 0 else K_SCALE).then_inc(S["act"], ac.up("act"))
                        eng.wait_ge(S[ac.last], ac.ended())
                        eng.sem_inc(S[f"acc_free{r}"], ac.told(f"acc_free{r}"))
                    split_hi()
                eng.wait_ge(S[ac.last], ac.ended())
                eng.sem_inc(S["qk_in"], ac.told("qk_in"))
                eng.wait_ge(S["arg1_ready"], ac.next("arg1_ready"))
                act(strip[:, :], strip[:, :], ACT.Exp).then_inc(S["strip_exp"], ac.up("strip_exp"))
                act(grow[:, :], ramp[:, 0, :], ACT.Exp, scale=acol[:, 0:1]).then_inc(S["grow_ready"], ac.up("grow_ready"))
                for b in range(2):
                    ins = act(wcol[:, b:b + 1], pcol[:, b:b + 1], ACT.Exp, scale=acol[:, b:b + 1])
                ins.then_inc(S["wcol_ready"], ac.up("wcol_ready"))
                for j in range(2):
                    for t in range(TT):
                        r = tile_of()
                        act(v_tok[:, t, j * W:(j + 1) * W], acc[:, 2 * r, 0:W], ACT.Copy).then_inc(S["act"], ac.up("act"))
                        eng.wait_ge(S[ac.last], ac.ended())
                        eng.sem_inc(S[f"acc_free{r}"], ac.told(f"acc_free{r}"))
                    split_hi()
                eng.wait_ge(S[ac.last], ac.ended())
                eng.sem_inc(S["v_in"], ac.told("v_in"))
                eng.wait_ge(S["grow_used"], ac.next("grow_used"))
                act(grow[:, :], ramp[:, 1, :], ACT.Exp, scale=acol[:, 1:2]).then_inc(S["grow_ready"], ac.up("grow_ready"))
                eng.wait_ge(S["grow_used"], ac.next("grow_used"))
                for j in range(2):
                    for c in range(2):
                        r = tile_of()
                        v = 2 * j + c
                        if v >= 2:
                            eng.wait_ge(S["yg_ready"], ac.next("yg_ready"))
                        act(halves(tbuf[:, v % 2, :]), pair(r), ACT.Silu).then_inc(S["act"], ac.up("act"))
                        eng.wait_ge(S[ac.last], ac.ended())
                        eng.sem_inc(S[f"acc_free{r}"], ac.told(f"acc_free{r}"))
                        eng.wait_ge(S[ac.last], ac.ended())
                        eng.sem_inc(S["g_in"], ac.told("g_in"))
                    split_hi()
                    if j == 0:
                        root()
                    for c in range(2):
                        eng.wait_ge(S["z32_ready"], ac.next("z32_ready"))
                        act(yg_hi[:, 2 * j + c, :], h32[:, :], ACT.Copy).then_inc(S["yg_hi"], ac.up("yg_hi"))
                eng.wait_ge(S["yg_ready"], ac.next("yg_ready", 2))
                for j in range(2):
                    pass_tiles(4)
                    split_hi()
            ffn(1)
            root()

        @block.vector
        def _(eng):
            v = Line(eng, "dve")
            tt, ts, st3 = eng.tensor_tensor, eng.tensor_scalar, eng.scalar_tensor_tensor
            job, tile = [0], [0]

            def split_lo():
                s = job[0] % 2
                job[0] += 1
                eng.wait_ge(S[f"w_hi{s}"], v.next(f"w_hi{s}"))
                tt(w_lo[s][:, :], raw[s][:, :], w_hi[s][:, :].bitcast(f32), ALU.subtract).then_inc(S[f"w_lo{s}"], v.up(f"w_lo{s}"))

            def pass_tiles(n):
                for _ in range(n):
                    v.skip(f"acc_ready{tile[0] % 2}")
                    tile[0] += 1

            def tile_of():
                r = tile[0] % 2
                tile[0] += 1
                eng.wait_ge(S[f"acc_ready{r}"], v.next(f"acc_ready{r}"))
                return r

            def square_in(src, first):
                if first:
                    tt(sq_sum[:, :], src, src, ALU.mult).then_inc(S["dve"], v.up("dve"))
                    eng.wait_ge(S[v.last], v.ended())
                else:
                    tt(sq[:, :], src, src, ALU.mult).then_inc(S["dve"], v.up("dve"))
                    eng.wait_ge(S[v.last], v.ended())
                    tt(sq_sum[:, :], sq_sum[:, :], sq[:, :], ALU.add).then_inc(S["dve"], v.up("dve"))
                    eng.wait_ge(S[v.last], v.ended())

            def inverse_root(n, name="dve"):
                m, r, y, t, out = (stt[:, i, 0:n] for i in range(5))
                eng.wait_ge(S["root"], v.next("root"))
                eng.reciprocal(y, r).then_inc(S["dve"], v.up("dve"))
                eng.wait_ge(S[v.last], v.ended())
                tt(t, y, y, ALU.mult).then_inc(S["dve"], v.up("dve"))
                eng.wait_ge(S[v.last], v.ended())
                tt(t, t, m, ALU.mult).then_inc(S["dve"], v.up("dve"))
                eng.wait_ge(S[v.last], v.ended())
                ts(t, t, -0.5, 1.5, ALU.mult, ALU.add).then_inc(S["dve"], v.up("dve"))
                eng.wait_ge(S[v.last], v.ended())
                tt(out, y, t, ALU.mult).then_inc(S[name], v.up(name))

            def rms(width):
                eng.wait_ge(S[v.last], v.ended())
                eng.sem_inc(S["sq_done"], v.told("sq_done"))
                eng.wait_ge(S["stat"], v.next("stat"))
                ts(stt[:, 0, 0:TT], mixf[:, 0:TT], 1.0 / width, EPS, ALU.mult, ALU.add).then_inc(S["mean"], v.up("mean"))
                inverse_root(TT, "rinv")
                eng.wait_ge(S["rb"], v.next("rb"))
                eng.tensor_copy(rB[:, :], mixf[:, 512:512 + N]).then_inc(S["rb_done"], v.up("rb_done"))
                eng.wait_ge(S[v.last], v.ended())

            def modulate(l, m):
                for k in range(KT):
                    eng.wait_ge(S["normed"], v.next("normed"))
                    for cols, c in PARTS:
                        ins = ts(h32[:, cols], tbuf[:, k % 2, cols], gain[l][m][:, k, c:c + 1],
                                 mod[l][:, SH[m] + k, c:c + 1], ALU.mult, ALU.add)
                    ins.then_inc(S["dve"], v.up("dve"))
                    eng.wait_ge(S[v.last], v.ended())
                    eng.wait_ge(S["h_hi"], v.next("h_hi"))
                    tt(h_lo[:, k, :], h32[:, :], h_hi[:, k, :].bitcast(f32), ALU.subtract).then_inc(S["h_ready"], v.up("h_ready"))
                    eng.wait_ge(S[v.last], v.ended())

            def mods(l, a, b):
                tt(mod[l][:, a:b, :], ADA[:, l, a:b, :],
                         b_ada[:, l, a:b].unsqueeze(2).broadcast_to([P, b - a, 2]), ALU.add).then_inc(S["mod_read"], v.up("mod_read"))
                eng.wait_ge(S[v.last], v.ended())

            def gains(l, m):
                row = (NM, NF)[m][l]
                for c in range(2):
                    ins = st3(gain[l][m][:, :, c], mod[l][:, SC[m]:SC[m] + KT, c], 1.0, vec[:, row:row + KT], ALU.add, ALU.mult)
                return ins

            def into_x(l, m, d):
                r = tile_of()
                for b, src, dst, c in SEGS:
                    ins = st3(xT[:, d, dst], acc[:, 2 * r + b, src], mod[l][:, GA[m] + d, c:c + 1], xT[:, d, dst], ALU.mult, ALU.add)
                ins.then_inc(S["dve"], v.up("dve"))
                eng.wait_ge(S[v.last], v.ended())
                eng.sem_inc(S[f"acc_free{r}"], v.told(f"acc_free{r}"))
                eng.wait_ge(S[v.last], v.ended())
                square_in(xT[:, d, :], d == 0)

            eng.wait_ge(S["vec_T"], v.next("vec_T"))
            eng.tensor_copy(b_ada[:, :, :].rearrange("p l j -> p (l j)"), mix[:, 0, 0:96])
            eng.tensor_copy(vec[:, :], mix[:, 0, 96:96 + N_ROWS]).then_inc(S["vec_read"], v.up("vec_read"))
            for n in range(2 * TT):
                t, half = divmod(n, 2)
                eng.wait_ge(S["x_T"], v.next("x_T"))
                eng.tensor_copy(xT[:, half * 4:half * 4 + 4, tok(t)], acc[:, n % 2, :].rearrange("p (k n) -> p k n", k=4)).then_inc(S["x_T_read"], v.up("x_T_read"))
            eng.wait_ge(S[v.last], v.ended())
            for k in range(KT):
                square_in(xT[:, k, :], k == 0)
            split_lo()
            split_lo()
            v.took["ada_used"] = 0
            eng.wait_ge(S["ada_used"], v.next("ada_used", 8))
            mods(0, 0, 16)
            gains(0, 0).then_inc(S["gain_ready"], v.up("gain_ready"))
            rms(D)
            modulate(0, 0)
            eng.wait_ge(S["dtw_hi"], v.next("dtw_hi"))
            tt(dtw_lo[:, :, :], dtw[:, :, :], dtw_hi[:, :, :].bitcast(f32), ALU.subtract).then_inc(S["dtw_lo"], v.up("dtw_lo"))
            heads = lambda a: a.rearrange("p (h d) -> p h d", d=HD)
            for j in range(8):
                pass_tiles((TT, TT, TT, 2, 2, 3, 2, 2)[j])
                split_lo()
                if j == 2:
                    eng.wait_ge(S["qkv_in"], v.next("qkv_in"))
                    for t in range(TT):
                        tt(sq[:, :], qkv[:, t, 0:N], qkv[:, t, 0:N], ALU.mult).then_inc(S["dve"], v.up("dve"))
                        eng.wait_ge(S[v.last], v.ended())
                        eng.tensor_reduce(stt[:, 3, t * 10:(t + 1) * 10], heads(sq[:, :]), X, ALU.add).then_inc(S["dve"], v.up("dve"))
                        eng.wait_ge(S[v.last], v.ended())
                    ts(stt[:, 0, :], stt[:, 3, :], 1.0 / HD, EPS, ALU.mult, ALU.add).then_inc(S["mean"], v.up("mean"))
                    inverse_root(TT * 10)
                    eng.wait_ge(S[v.last], v.ended())
                    for t in range(TT):
                        x = heads(qkv[:, t, 0:N])
                        tt(x, x, stt[:, 4, t * 10:(t + 1) * 10].unsqueeze(2).broadcast_to([P, 10, HD]), ALU.mult).then_inc(S["dve"], v.up("dve"))
                        eng.wait_ge(S[v.last], v.ended())
                        tt(x[:, 0:NH, :], x[:, 0:NH, :], qk_g[:, 0, :].unsqueeze(1).broadcast_to([P, NH, HD]), ALU.mult)
                        ins = tt(x[:, NH:, :], x[:, NH:, :], qk_g[:, 1, :].unsqueeze(1).broadcast_to([P, NKV, HD]), ALU.mult)
                        ins.then_inc(S["new_kv" if t == 0 else "dve"], v.up("new_kv" if t == 0 else "dve"))
                        eng.wait_ge(S[v.last], v.ended())
                        if t:
                            a, b = x[:, :, 0:32], x[:, :, 32:HD]
                            co, si = (c[:, t - 1, :].unsqueeze(1).broadcast_to([P, 10, 32]) for c in (cosA, sinA))
                            r = [tbuf[:, i // 2, (i % 2) * 320:(i % 2 + 1) * 320].rearrange("p (h d) -> p h d", d=32) for i in range(4)]
                            for o, p_, q_ in zip(r, (a, b, b, a), (co, si, co, si)):
                                ins = tt(o, p_, q_, ALU.mult)
                            ins.then_inc(S["dve"], v.up("dve"))
                            eng.wait_ge(S[v.last], v.ended())
                            tt(a, r[0], r[1], ALU.subtract)
                            ins = tt(b, r[2], r[3], ALU.add)
                            ins.then_inc(S["roped" if t == TT - 1 else "dve"], v.up("roped" if t == TT - 1 else "dve"))
                            eng.wait_ge(S[v.last], v.ended())
                if j == 5:
                    eng.wait_ge(S["dt_in"], v.next("dt_in"))
                    tt(dt_tok[:, :, :], dt_tok[:, :, :], dt_c[:, 0, :].unsqueeze(1).broadcast_to([P, TT, DTS]), ALU.add).then_inc(S["dve"], v.up("dve"))
                    eng.wait_ge(S[v.last], v.ended())
                    st3(dt_t[1][:, :, :], dt_tok[:, :, :], -1.0, dt_tok[:, :, :], ALU.mult, ALU.max).then_inc(S["dt_abs"], v.up("dt_abs"))
                    eng.wait_ge(S[v.last], v.ended())
                    ts(dt_tok[:, :, :], dt_tok[:, :, :], 0.0, None, ALU.max).then_inc(S["dve"], v.up("dve"))
            eng.wait_ge(S["ada_used"], v.next("ada_used", 16))
            mods(0, 16, 48)
            gains(0, 1).then_inc(S["gain_ready"], v.up("gain_ready"))
            eng.wait_ge(S["dt_exp"], v.next("dt_exp"))
            e, u, c = (t[:, :, :] for t in (dt_t[1], dt_t[0], dt_t[2]))
            ts(u, e, 1.0, None, ALU.add).then_inc(S["dt_u"], v.up("dt_u"))
            eng.wait_ge(S[v.last], v.ended())
            ts(c, u, -1.0, None, ALU.add).then_inc(S["dve"], v.up("dve"))
            eng.wait_ge(S[v.last], v.ended())
            tt(c, e, c, ALU.subtract).then_inc(S["dve"], v.up("dve"))
            eng.wait_ge(S[v.last], v.ended())
            eng.reciprocal(e, u).then_inc(S["dve"], v.up("dve"))
            eng.wait_ge(S[v.last], v.ended())
            tt(c, c, e, ALU.mult).then_inc(S["dve"], v.up("dve"))
            eng.wait_ge(S[v.last], v.ended())
            eng.wait_ge(S["dt_ln"], v.next("dt_ln"))
            tt(dt_tok[:, :, :], dt_tok[:, :, :], c, ALU.add).then_inc(S["dve"], v.up("dve"))
            eng.wait_ge(S[v.last], v.ended())
            tt(dt_tok[:, :, :], dt_tok[:, :, :], dt_t[3][:, :, :], ALU.add).then_inc(S["dve"], v.up("dve"))
            eng.wait_ge(S[v.last], v.ended())
            tt(a_tok[:, :, :], dt_tok[:, :, :], dt_c[:, 1, :].unsqueeze(1).broadcast_to([P, TT, DTS]), ALU.mult).then_inc(S["dve"], v.up("dve"))
            eng.wait_ge(S[v.last], v.ended())
            ts(a_tok[:, :, :], a_tok[:, :, :], -1.0, None, ALU.mult).then_inc(S["a_ready"], v.up("a_ready"))
            U = len(units)
            for i in range(U + 2):
                if i < U:
                    t, h = units[i]
                    n = N_CTX if t == 0 else N
                    eng.wait_ge(S["scores"], v.next("scores"))
                    if v.due("exp_done", 4):
                        eng.wait_ge(S["exp_done"], v.now("exp_done", 4))
                    eng.tensor_reduce(nmax[:, i % 4:i % 4 + 1], mixf[:, 1024 * (i % 2):1024 * (i % 2) + n], X, ALU.max).then_inc(S["dve"], v.up("dve"))
                    eng.wait_ge(S[v.last], v.ended())
                    ts(nmax[:, i % 4:i % 4 + 1], nmax[:, i % 4:i % 4 + 1], -ATT_SCALE, None, ALU.mult).then_inc(S["max_ready"], v.up("max_ready"))
                if 1 <= i <= U:
                    t, h = units[i - 1]
                    n = N_CTX if t == 0 else N
                    b = (i - 1) % 2
                    eng.wait_ge(S["pT_made"], v.next("pT_made"))
                    if v.due("att_made", 2):
                        eng.wait_ge(S["att_made"], v.now("att_made", 2))
                    eng.tensor_copy(pT[:, b, 0:n], accf[:, 1024 * b:1024 * b + n]).then_inc(S["pT_sb"], v.up("pT_sb"))
                if i >= 2:
                    t, h = units[i - 2]
                    u, b = i - 2, i % 2
                    eng.reciprocal(rrec[:, u % 4:u % 4 + 1], rsum[:, u % 4:u % 4 + 1]).then_inc(S["dve"], v.up("dve"))
                    eng.wait_ge(S[v.last], v.ended())
                    eng.wait_ge(S["att_made"], u + 1)
                    ts(att_tok[:, t, h * HD:(h + 1) * HD], accf[:, 1024 * b + 768:1024 * b + 768 + HD],
                             rrec[:, u % 4:u % 4 + 1], None, ALU.mult).then_inc(S["att_read"], v.up("att_read"))
            eng.wait_ge(S["kv_gone"], 1)
            eng.wait_ge(S["cum_made"], v.next("cum_made"))
            both = mixf[:, 0:TT * DTS].rearrange("p (t c) -> p t c", c=DTS)
            eng.tensor_copy(cum[:, :, :], both)
            ts(ncum[:, :, :], both, -1.0, None, ALU.mult).then_inc(S["cum_read"], v.up("cum_read"))
            eng.wait_ge(S[v.last], v.ended())
            for t in range(TT):
                eng.wait_ge(S["xt_made"], v.next("xt_made"))
                eng.tensor_copy(x_tok[:, t, :], acc[:, t % 2, :]).then_inc(S["xt_read"], v.up("xt_read"))
            eng.wait_ge(S["bt_made"], v.next("bt_made"))
            eng.tensor_copy(b_tok[:, :], acc[:, 2, 0:P]).then_inc(S["bt_read"], v.up("bt_read"))
            for g in range(2):
                for J in range(LT + 1):
                    n = g * (LT + 1) + J
                    eng.wait_ge(S["cb_made"], v.next("cb_made"))
                    if J < LT:
                        eng.tensor_copy(Gt[g][:, J * N_LAT:(J + 1) * N_LAT], mix[:, 1 + n % 2, :]).then_inc(S["cb_read"], v.up("cb_read"))
                    else:
                        eng.tensor_copy(Gp[:, g, :], mix[:, 1 + n % 2, 0:P]).then_inc(S["cb_read"], v.up("cb_read"))
            eng.wait_ge(S["conv_ready"], v.next("conv_ready"))
            f, w = (lambda h, t: ncum[:, t, h:h + 1]), (lambda h, t: dt_tok[:, t, h:h + 1])

            def y_in(h):
                eng.wait_ge(S["y_made"], v.next("y_made"))
                eng.tensor_copy(y_tok[:, :, h * HD:(h + 1) * HD], mix[:, h % 2, 0:TT * HD].rearrange("p (t d) -> p t d", d=HD)).then_inc(S["y_read"], v.up("y_read"))

            for h in range(NH):
                g = h // 4
                eng.wait_ge(S["rows_made"], v.next("rows_made"))
                if h:
                    y_in(h - 1)
                if h % 4 == 0:
                    for b in range(2):
                        ins = eng.tensor_copy(ct2[HD * b:HD * b + HD, :], conv[HD * g:HD * g + HD, ST + 1, LAT])
                    ins.then_inc(S["dve"], v.up("dve"))
                eng.tensor_copy(tot[:, h:h + 1], accf[:, P - 1:P])
                eng.tensor_copy(tot[:, NH + h:NH + h + 1], accf[:, 1024:1025]).then_inc(S["dve"], v.up("dve"))
                for t in range(TT):
                    ins = ts(dm[:, t, :], accf[:, 1024 + t * P:1024 + (t + 1) * P], f(NH + h, t), None, ALU.add)
                ins.then_inc(S["dve"], v.up("dve"))
                eng.wait_ge(S[v.last], v.ended())
                for t in range(TT):
                    ins = st3(dg[:, t, :], accf[:, t * P:(t + 1) * P], f(h, t), dm[:, t, :], ALU.add, ALU.min)
                ins.then_inc(S["arg_ready"], v.up("arg_ready"))
                eng.wait_ge(S[v.last], v.ended())
                for t in range(TT):
                    ins = ts(dm[:, t, :], upto[:, :], w(h, t), None, ALU.mult)
                ins.then_inc(S["dve"], v.up("dve"))
                eng.wait_ge(S[v.last], v.ended())
                for t in range(TT):
                    ins = st3(dm[:, t, :], onward[:, :], w(NH + h, t), dm[:, t, :], ALU.mult, ALU.add)
                ins.then_inc(S["dve"], v.up("dve"))
                eng.wait_ge(S[v.last], v.ended())
                diag = Gt[g][:, :].rearrange("p (j c) -> p j c", j=LT)[:, :, 0:P]
                tt(dm[:, 0, :], dm[:, 0, :], Gp[:, g, :], ALU.mult)
                tt(dm[:, 1:, :], dm[:, 1:, :], diag, ALU.mult).then_inc(S["dve"], v.up("dve"))
                eng.wait_ge(S[v.last], v.ended())
                eng.wait_ge(S["diag_exp"], v.next("diag_exp"))
                tt(dg, dg, dm, ALU.mult)
                eng.wait_ge(S["rows_read"], v.next("rows_read"))
                for J in range(LT):
                    if J < LT - 1:
                        c = slice((J + 1) * P, N_LAT)
                        st3(M_off[:, J, c], E_off[:, J, c], w(h, J + 1), Gt[g][:, J * N_LAT + c.start:J * N_LAT + c.stop], ALU.mult, ALU.mult)
                    if J:
                        c = slice(0, J * P)
                        st3(M_off[:, J, c], E_off[:, J, c], w(NH + h, J + 1), Gt[g][:, J * N_LAT:J * N_LAT + c.stop], ALU.mult, ALU.mult)
                tt(ce[:, :], ecum[:, :], ct2[:, :], ALU.mult).then_inc(S["m_ready"], v.up("m_ready"))
            y_in(NH - 1)
            tt(wst[:, :], tot[:, :], ncum[:, 0, :], ALU.add).then_inc(S["wst_arg"], v.up("wst_arg"))
            eng.wait_ge(S["wst_exp"], v.next("wst_exp"))
            tt(wst[:, :], wst[:, :], dt_tok[:, 0, :], ALU.mult).then_inc(S["dve"], v.up("dve"))
            eng.wait_ge(S[v.last], v.ended())
            for h in range(NH):
                g = h // 4
                if v.due("fs_made", 2):
                    eng.wait_ge(S["fs_made"], v.now("fs_made", 2))
                for b in range(2):
                    ins = ts(bw[:, h % 2, b * HD:(b + 1) * HD], b_tok[:, g * HD:(g + 1) * HD], wst[:, b * NH + h:b * NH + h + 1], None, ALU.mult)
                ins.then_inc(S["bw_ready"], v.up("bw_ready"))
            eng.wait_ge(S["fs_made"], NH)
            eng.tensor_copy(s_out[:, :, :].rearrange("p h d -> p (h d)"), mix[:, 2, :]).then_inc(S["s_out_ready"], v.up("s_out_ready"))
            for t in range(TT):
                eng.wait_ge(S["yT_made"], v.next("yT_made"))
                for j in range(ST):
                    ins = st3(conv[:, j, pad(t)], conv[:, j, pad(t)], d_skip[:, j:j + 1], acc[:, t % 2, j * P:(j + 1) * P], ALU.mult, ALU.add)
                ins.then_inc(S["yT_read"], v.up("yT_read"))
            eng.wait_ge(S[v.last], v.ended())
            for j in range(ST):
                tt(zT[:, j, 0:N_CTX], zT[:, j, 0:N_CTX], conv[:, j, 0:N_CTX], ALU.mult)
                tt(zT[:, j, N_CTX:], zT[:, j, N_CTX:], conv[:, j, LAT], ALU.mult).then_inc(S["dve"], v.up("dve"))
                eng.wait_ge(S[v.last], v.ended())
                square_in(zT[:, j, :], j == 0)
            rms(SSD_W)
            for t in range(TT):
                eng.wait_ge(S["aT_made"], v.next("aT_made"))
                eng.wait_ge(S["h_hi"], v.next("h_hi"))
                tt(h_lo[:, 0:ST, tok(t)], acc[:, 2 + t % 2, :].rearrange("p (j n) -> p j n", j=4), h_hi[:, 0:ST, tok(t)].bitcast(f32), ALU.subtract).then_inc(S["aT_read"], v.up("aT_read"))
            for t in range(TT):
                eng.wait_ge(S[v.last], v.ended())
                eng.sem_inc(S["h_ready"], v.told("h_ready"))
            for j in range(ST):
                st3(h32[:, :], zT[:, j, :], vec[:, SSD_G + j:SSD_G + j + 1], rB[:, :], ALU.mult, ALU.mult).then_inc(S["y32_ready"], v.up("y32_ready"))
                eng.wait_ge(S[v.last], v.ended())
                eng.wait_ge(S["h_hi"], v.next("h_hi"))
                tt(h_lo[:, ST + j, :], h32[:, :], h_hi[:, ST + j, :].bitcast(f32), ALU.subtract).then_inc(S["h_ready"], v.up("h_ready"))
                eng.wait_ge(S[v.last], v.ended())
            eng.wait_ge(S[v.last], v.ended())
            eng.sem_inc(S["l0_mixed"], v.told("l0_mixed"))
            for j in range(4):
                for c in range(2):
                    into_x(0, 0, 2 * j + c)
                split_lo()

            def ffn(l):
                rms(D)
                modulate(l, 1)
                for f0, nf in CHUNKS:
                    per = {"acc_ready0": 2, "acc_ready1": 2, "acc_free1": 2, "silu_ready": 2, "gu32_ready": 2, "gu_hi": 2,
                           "gu_ready": 2, "w_hi0": 1, "w_hi1": 1, "w_lo0": 1, "w_lo1": 1, "dve": 2}
                    with v.loop(nf // 2, per) as i:
                        for s in range(2):
                            pass_tiles(1)
                            eng.wait_ge(S["silu_ready"], v.next("silu_ready"))
                            r = tile_of()
                            tt(halves(gu32[:, :]), halves(silu_g[:, :]), pair(r), ALU.mult).then_inc(S["dve"], v.up("dve"))
                            eng.wait_ge(S[v.last], v.ended())
                            eng.sem_inc(S[f"acc_free{r}"], v.told(f"acc_free{r}"))
                            eng.wait_ge(S[v.last], v.ended())
                            eng.sem_inc(S["gu32_ready"], v.told("gu32_ready"))
                            split_lo()
                            eng.wait_ge(S["gu_hi"], v.next("gu_hi"))
                            f_ = bass.ds(i * 2 + s, 1)
                            one = lambda a: a[:, f_, :].rearrange("p o n -> p (o n)")
                            tt(one(gu_lo), gu32[:, :], one(gu_hi).bitcast(f32), ALU.subtract).then_inc(S["gu_ready"], v.up("gu_ready"))
                            eng.wait_ge(S[v.last], v.ended())
                    for j in range(4):
                        for c in range(2):
                            into_x(l, 1, 2 * j + c)
                        if not (l == 1 and f0 == CHUNKS[-1][0] and j >= 2):
                            split_lo()

            ffn(0)
            eng.wait_ge(S[v.last], v.ended())
            eng.sem_inc(S["ffn_over"], v.told("ffn_over"))
            eng.wait_ge(S["ada_used"], v.next("ada_used", 24))
            mods(1, 0, 48)
            gains(1, 0)
            gains(1, 1).then_inc(S["gain_ready"], v.up("gain_ready"))
            rms(D)
            modulate(1, 0)
            eng.wait_ge(S["l1_in"], v.next("l1_in", 16 * 5))
            eng.wait_ge(S[v.last], v.ended())
            eng.sem_inc(S["head_used"], v.told("head_used"))
            per = {"acc_ready0": 13, "acc_ready1": 13, "acc_free0": 4, "acc_free1": 4, "w_hi0": 4, "w_hi1": 4, "w_lo0": 4, "w_lo1": 4,
                   "head_in": 128, "decay_exp": 1, "arg1_ready": 1, "strip_exp": 1, "grow_ready": 2, "grow_used": 2, "wcol_ready": 1,
                   "qk_in": 1, "rope_done": 1, "kp_made": 1, "kw_ready": 1, "score_made": 5, "sc_ready": 5, "y_part": 5,
                   "qg_ready": 2, "state_done": 2, "fs_made1": 4, "fs_ready": 4, "fs_read": 4, "fs_out0": 32, "fs_out1": 32, "yr_read": 1,
                   "sq_done": 1, "stat": 1, "mean": 1, "root": 1, "rinv": 1, "rb": 1, "rb_done": 1,
                   "g_in": 4, "z32_ready": 4, "yg_hi": 4, "yg_ready": 4, "head_used": 1}
            own = [0]
            DVE_PER = 45
            per["dve"] = DVE_PER
            flat = lambda a: a.rearrange("p a n -> p (a n)")
            with v.loop(RH, per):
                eng.wait_ge(S["head_in"], v.next("head_in", 128))
                eng.wait_ge(S["decay_exp"], v.next("decay_exp"))
                ts(acol[:, :], acol[:, :], -1.0, None, ALU.mult).then_inc(S["dve"], v.up("dve"))
                eng.wait_ge(S[v.last], v.ended())
                tmp = flat(sc_sb[:, :, :])[:, 0:STRIP]
                ts(tmp, strip[:, :], 0.0, acol[:, 0:1], ALU.max, ALU.mult).then_inc(S["dve"], v.up("dve"))
                eng.wait_ge(S[v.last], v.ended())
                ts(strip[:, :], strip[:, :], -1.0, 0.0, ALU.mult, ALU.max).then_inc(S["dve"], v.up("dve"))
                eng.wait_ge(S[v.last], v.ended())
                st3(strip[:, :], strip[:, :], acol[:, 1:2], tmp, ALU.mult, ALU.add).then_inc(S["arg1_ready"], v.up("arg1_ready"))
                for j in range(2):
                    pass_tiles(2)
                    split_lo()
                eng.wait_ge(S["qk_in"], v.next("qk_in"))
                for m in range(2):
                    a, b = qk[:, 2 * m, N_CTX:], qk[:, 2 * m + 1, N_CTX:]
                    r = [tbuf[:, 0, 0:N_LAT], tbuf[:, 1, 0:N_LAT], h32[:, 0:N_LAT], sq[:, 0:N_LAT]]
                    for o, p_, q_ in zip(r, (a, b, b, a), (cosR, sinR, cosR, sinR)):
                        ins = tt(o, p_, q_[:, :], ALU.mult)
                    ins.then_inc(S["dve"], v.up("dve"))
                    eng.wait_ge(S[v.last], v.ended())
                    tt(a, r[0], r[1], ALU.subtract)
                    tt(b, r[2], r[3], ALU.add).then_inc(S["rope_done" if m else "dve"], v.up("rope_done" if m else "dve"))
                    eng.wait_ge(S[v.last], v.ended())
                eng.wait_ge(S["strip_exp"], v.next("strip_exp"))
                tt(strip[:, (LT - 1) * P:LT * P], strip[:, (LT - 1) * P:LT * P], ident[:, :], ALU.add).then_inc(S["dve"], v.up("dve"))
                eng.wait_ge(S[v.last], v.ended())

                def decayed(b):
                    eng.wait_ge(S["grow_ready"], v.next("grow_ready"))
                    ins = tt(qg[:, :, :], qk[:, 0:2, N_CTX:], grow[:, :].unsqueeze(1).broadcast_to([P, 2, N_LAT]), ALU.mult)
                    ins.then_inc(S["qg_ready"], v.up("qg_ready"))
                    eng.wait_ge(S[v.last], v.ended())
                    eng.sem_inc(S["grow_used"], v.told("grow_used"))

                decayed(0)
                for j in range(2):
                    pass_tiles(TT)
                    split_lo()
                eng.wait_ge(S["kp_made"], v.next("kp_made"))
                eng.wait_ge(S["wcol_ready"], v.next("wcol_ready"))
                for b in range(2):
                    ins = ts(kw[:, b, :], mix[:, 0, 0:DK], wcol[:, b:b + 1], None, ALU.mult)
                ins.then_inc(S["kw_ready"], v.up("kw_ready"))
                for J in range(LT + 1):
                    eng.wait_ge(S["score_made"], v.next("score_made"))
                    if J == 0:
                        eng.wait_ge(S[v.last], v.ended())
                    if 2 <= J:
                        eng.wait_ge(S["y_part"], v.next("y_part"))
                    if J < LT:
                        tt(sc_sb[:, J % 2, :], mix[:, 1 + J % 2, :], strip[:, (LT - 1 - J) * P:(LT - 1 - J) * P + N_LAT], ALU.mult).then_inc(S["sc_ready"], v.up("sc_ready"))
                    else:
                        tt(sc_p[:, :], mix[:, 1 + J % 2, 0:P], strip[:, (LT - 1) * P:LT * P], ALU.mult).then_inc(S["sc_ready"], v.up("sc_ready"))
                eng.wait_ge(S["state_done"], v.next("state_done"))
                decayed(1)
                eng.wait_ge(S["y_part"], v.next("y_part", 2))
                eng.wait_ge(S["state_done"], v.next("state_done"))
                eng.tensor_copy(yR[:, :, 0:N_CTX], mix[:, 0, :].rearrange("p (a n) -> p a n", a=VT))
                eng.tensor_copy(yR[:, :, N_CTX:], acc[:, :, :]).then_inc(S["yr_read"], v.up("yr_read"))
                eng.wait_ge(S[v.last], v.ended())
                for n in range(4):
                    eng.wait_ge(S["fs_made1"], v.next("fs_made1"))
                    if n >= 2:
                        eng.wait_ge(S[f"fs_out{n % 2}"], v.next(f"fs_out{n % 2}", 16))
                    eng.tensor_copy(sc_sb[:, n % 2, :], mix[:, 1 + n % 2, :]).then_inc(S["fs_ready"], v.up("fs_ready"))
                    eng.wait_ge(S[v.last], v.ended())
                    eng.sem_inc(S["fs_read"], v.told("fs_read"))
                for j in range(VT):
                    square_in(yR[:, j, :], j == 0)
                pass_tiles(2)
                split_lo()
                rms(DV)
                for j in range(VT):
                    st3(yR[:, j, :], yR[:, j, :], rgain[:, j:j + 1], rB[:, :], ALU.mult, ALU.mult).then_inc(S["dve"], v.up("dve"))
                    eng.wait_ge(S[v.last], v.ended())
                for b in range(2):
                    eng.wait_ge(S[f"fs_out{b}"], v.next(f"fs_out{b}", 16))
                eng.wait_ge(S[v.last], v.ended())
                eng.sem_inc(S["head_used"], v.told("head_used"))
                for j in range(2):
                    if j:
                        pass_tiles(2)
                        split_lo()
                    for c in range(2):
                        n = 2 * j + c
                        eng.wait_ge(S["g_in"], v.next("g_in"))
                        tt(h32[:, :], tbuf[:, n % 2, :], yR[:, n, :], ALU.mult).then_inc(S["z32_ready"], v.up("z32_ready"))
                        eng.wait_ge(S[v.last], v.ended())
                        eng.wait_ge(S["yg_hi"], v.next("yg_hi"))
                        tt(yg_lo[:, n, :], h32[:, :], yg_hi[:, n, :].bitcast(f32), ALU.subtract).then_inc(S["yg_ready"], v.up("yg_ready"))
                        eng.wait_ge(S[v.last], v.ended())
                for j in range(2):
                    for c in range(4):
                        into_x(1, 0, 4 * j + c)
                    split_lo()
            ffn(1)
            rms(D)
            for k in range(KT):
                ins = st3(xT[:, k, :], xT[:, k, :], vec[:, FIN + k:FIN + k + 1], rB[:, :], ALU.mult, ALU.mult)
            ins.then_inc(S["final_ready"], v.up("final_ready"))
            for t in range(TT):
                for half in range(2):
                    eng.wait_ge(S["out_T"], v.next("out_T"))
                    eng.tensor_copy(y_out[:, t, half * 512:(half + 1) * 512], acc[:, half, :]).then_inc(S["y_ready"], v.up("y_ready"))

        @block.gpsimd
        def _(eng):
            po = Line(eng, "pool")
            tt, ts = eng.tensor_tensor, eng.tensor_scalar

            def norm():
                eng.wait_ge(S["rb_done"], po.next("rb_done"))
                for k in range(KT):
                    if k >= 2:
                        eng.wait_ge(S["h_ready"], po.next("h_ready"))
                    tt(tbuf[:, k % 2, :], xT[:, k, :], rB[:, :], ALU.mult).then_inc(S["normed"], po.up("normed"))
                eng.wait_ge(S["h_ready"], po.next("h_ready", 2))

            norm()
            for cols in (slice(0, 2), slice(2 + P, 6 + P), slice(PADDED - 2, PADDED)):
                ins = eng.memset(xpad[:, :, cols], 0.0)
            ins.then_inc(S["pool"], po.up("pool"))
            eng.wait_ge(S[po.last], po.ended())
            n = PADDED - 4
            for i in range(XBC_T):
                eng.wait_ge(S["xb_in"], po.next("xb_in"))
                for k in range(TAPS):
                    tap = vec[:, CONV_W + k * XBC_T + i:CONV_W + k * XBC_T + i + 1]
                    out = conv[:, i, 0:n] if k == 0 else ctmp[:, 0:n]
                    ts(out, xpad[:, i, k:k + n], tap, None, ALU.mult).then_inc(S["pool"], po.up("pool"))
                    eng.wait_ge(S[po.last], po.ended())
                    if k:
                        tt(conv[:, i, 0:n], conv[:, i, 0:n], ctmp[:, 0:n], ALU.add).then_inc(S["conv_raw" if k == TAPS - 1 else "pool"], po.up("conv_raw" if k == TAPS - 1 else "pool"))
                        eng.wait_ge(S[po.last], po.ended())
            po.skip("rb_done")
            po.skip("h_ready", TT + ST)
            norm()
            eng.wait_ge(S["ffn_over"], po.next("ffn_over"))
            for dst, src in ([(cosR[:, :], I["rope_ret"][0]), (sinR[:, :], I["rope_ret"][1]), (pcol[:, :], I["places"])]
                             + [(ramp[:, b, :], I["ramps"][b, :].partition_broadcast(P)) for b in range(2)]):
                eng.dma_start(dst, src).then_inc(S["l1_in"], po.up("l1_in", 16))
            norm()
            per = {"head_used": 1, "head_in": 16 * 8, "fs_ready": 4, "fs_out0": 32, "fs_out1": 32, "rb_done": 1}
            with po.loop(RH, per) as h:
                eng.wait_ge(S["head_used"], po.next("head_used"))
                eng.sem_inc(S["pool_go"], 1)
                o = bass.ds(h, 1)
                one = lambda a: a.rearrange("o p d -> p (o d)")
                eng.dma_start(strip[:, :], I["offsets"]).then_inc(S["head_in"], po.up("head_in", 16))
                eng.dma_start(rgain[:, :], I["l1_ret_gain"][bass.ds(h * DV, DV)].rearrange("(t p) -> p t", p=P),
                                     allow_slow_non_contiguous=True).then_inc(S["head_in"], po.up("head_in", 16))
                for b in range(2):
                    eng.dma_start(acol[:, b:b + 1], I["l1_decay"][b, o].partition_broadcast(P)).then_inc(S["head_in"], po.up("head_in", 16))
                    for k in range(2):
                        eng.dma_start(S0[:, b, k, :], one(I["state_ret1"][0, b, o, k * P:(k + 1) * P, :])).then_inc(S["head_in"], po.up("head_in", 16))
                for n in range(4):
                    b, k = divmod(n, 2)
                    eng.wait_ge(S["fs_ready"], po.next("fs_ready"))
                    eng.sem_inc(S["pool_go"], 1)
                    eng.dma_start(one(O[5][0, b, o, k * P:(k + 1) * P, :]), sc_sb[:, n % 2, :]).then_inc(S[f"fs_out{n % 2}"], po.up(f"fs_out{n % 2}", 16))
                po.skip("rb_done")
            norm()
            for b in range(2):
                eng.wait_ge(S[f"fs_out{b}"], 32 * RH)


_INS = ["x_prompt", "x_sample", "c", "cache_k0", "cache_v0", "state_ssd0", "state_ret1", "c_ctx",
        "l0_w_ada", "l0_b_ada", "l0_norm_mix", "l0_norm_ffn", "l0_w_in", "l0_w_out", "l0_q_gain", "l0_k_gain",
        "l0_conv_w", "l0_conv_b", "l0_dt_bias", "l0_a_log", "l0_d_skip", "l0_ssd_gain",
        "l0_w_gate", "l0_w_up", "l0_w_down", "l1_w_ada", "l1_b_ada", "l1_norm_mix", "l1_norm_ffn",
        "l1_w_in", "l1_w_out", "l1_decay", "l1_ret_gain", "l1_w_gate", "l1_w_up", "l1_w_down", "final_norm"]
_OUTS = [(1, N_CTX, D), (1, N_LAT, D), (1, N_CTX, NKV, HD), (1, N_CTX, NKV, HD),
         (1, 2, NH, HD, HD), (1, 2, RH, DK, DV)]


def _constants():
    import numpy as np

    i = np.arange(P)
    squares = np.stack([np.eye(P), i[:, None] <= i[None, :], i[:, None] >= i[None, :], np.ones((P, P))])
    n = np.arange(N_LAT)
    row, col = (n // GRID_W).astype(np.float32), (n % GRID_W).astype(np.float32)

    def rope(dim):
        f = dim // 4
        inv = np.float32(10000.0) ** (-np.arange(f, dtype=np.float32) / np.float32(f))
        ang = np.concatenate([row[:, None] * inv, col[:, None] * inv], axis=1).astype(np.float32)
        return np.stack([np.cos(ang.astype(np.float64)), np.sin(ang.astype(np.float64))])

    att = rope(HD).reshape(2, LT, P, HD // 2).transpose(0, 2, 1, 3)
    ret = rope(DK).transpose(0, 2, 1)
    offsets = (np.arange(STRIP)[None, :] - (LT - 1) * P) - i[:, None]
    ramps = np.stack([n + 1, N_LAT - n])
    places = np.stack([P - 1 - i, i], axis=1)
    f = lambda a: np.ascontiguousarray(a, dtype=np.float32)
    return {"squares": f(squares), "rope_att": f(att), "rope_ret": f(ret), "offsets": f(offsets),
            "ramps": f(ramps), "places": f(places)}


def kernel(**inputs):
    import numpy as _np
    import concourse.bacc as _bacc
    from concourse import mybir as _mybir
    from concourse.bass_utils import run_bass_kernel_spmd as _run

    nc = _bacc.Bacc("TRN2", target_bir_lowering=False, num_devices=1)
    arrays, ins, outs = {}, {}, []
    given = {name: _np.ascontiguousarray(inputs[name]) for name in _INS}
    for name, a in {**given, **_constants()}.items():
        arrays[f"in_{name}_dram"] = a
        ins[name] = nc.dram_tensor(f"in_{name}_dram", a.shape, _mybir.dt.from_np(a.dtype), kind="ExternalInput").ap()
    for i, shape in enumerate(_OUTS):
        outs.append(nc.dram_tensor(f"out_{i}_dram", shape, _mybir.dt.float32, kind="ExternalOutput").ap())
    trunk_kernel(nc, ins, outs)
    r = _run(nc, [arrays], core_ids=[0])
    return tuple(r.results[0][f"out_{i}_dram"] for i in range(len(_OUTS)))
```

```python
import concourse.bass as bass
from concourse import mybir
from contextlib import ExitStack, contextmanager

P = 128
D = 1024
KT = D // P
N_CTX = 128
N_LAT = 512
N = N_CTX + N_LAT
TT = N // P
GRID_W = 64
LT = N_LAT // P
HALF = N // 2
PAST = 128
EPS = 1e-6
HD = 64
NH = 8
NKV = 2
ATT_W = NH * HD
KV_W = NKV * HD
QKV_W = ATT_W + 2 * KV_W
SSD_W = NH * HD
ST = SSD_W // P
XBC_T = ST + 2
TAPS = 5
PADDED = N + 8
RH = 4
DK = 256
DV = 512
VT = DV // P
STRIP = N_LAT + (LT - 1) * P
D_FF = 2816
FT = D_FF // P
CHUNKS = [(0, 8), (8, 8), (16, 6)]
W = 256
SLOT = KT * W
OFF_Z = QKV_W
OFF_X = OFF_Z + SSD_W
OFF_DT = OFF_X + XBC_T * P
DTS = 2 * NH
ATT_SCALE = HD ** -0.5
K_SCALE = DK ** -0.5
ADA_JOBS = 6 * D // W
NM, NF, FIN, COND, CONV_B, SSD_G, CONV_W = (0, 16), (8, 24), 32, 40, 56, 62, 66
N_ROWS = 96
SH, SC, GA = (0, 24), (8, 32), (16, 40)


class Line:

    def __init__(self, eng, own):
        self.e, self.last = eng, own
        self.made, self.took, self.turn, self.per = {}, {}, None, {}

    def value(self, name, n):
        return n if self.turn is None else n + self.turn * self.per.get(name, 0)

    def up(self, name, k=1):
        self.last = name
        return self.told(name, k)

    def told(self, name, k=1):
        self.made[name] = self.made.get(name, 0) + k
        return k

    def ended(self):
        return self.value(self.last, self.made[self.last])

    def next(self, name, k=1):
        self.took[name] = self.took.get(name, 0) + k
        return self.value(name, self.took[name])

    def due(self, name, behind):
        self.next(name)
        assert self.turn is None or self.took[name] > behind, name
        return self.took[name] > behind

    def now(self, name, behind=0):
        return self.value(name, self.took[name] - behind)

    def skip(self, name, k=1):
        self.took[name] = self.took.get(name, 0) + k

    @contextmanager
    def loop(self, turns, per):
        made, took = dict(self.made), dict(self.took)
        with self.e.Fori(0, turns) as i:
            self.turn, self.per = i, per
            yield i
        self.turn = None
        for now, was in ((self.made, made), (self.took, took)):
            for name in now:
                grown = now[name] - was.get(name, 0)
                assert grown in (0, per.get(name, 0)), (name, grown, per)
                now[name] += grown * (turns - 1)


class Sems(dict):

    def __init__(self, nc, ctx):
        super().__init__()
        self.nc, self.ctx = nc, ctx

    def __missing__(self, name):
        self[name] = self.ctx.enter_context(self.nc.semaphore(name))
        return self[name]


class Floor:

    def __init__(self, nc):
        self.nc, self.at, self.top = nc, (nc.sbuf_base + 31) // 32 * 32, nc.sbuf_usable_end

    def __call__(self, name, shape, dt=mybir.dt.float32):
        size = 4
        for n in shape[1:]:
            size *= n
        t = self.nc.alloc_sbuf_tensor_at(name, shape, dt, offset=self.at)
        self.at += (size + 31) // 32 * 32
        assert self.at <= self.top, (name, self.at, self.top)
        return t


def trunk_kernel(nc, I, O):
    f32, f32r = mybir.dt.float32, mybir.dt.float32r
    ALU, ACT = mybir.AluOpType, mybir.ActivationFunctionType
    X = mybir.AxisListType.X
    ctx = ExitStack()
    with ctx:
        sb = Floor(nc)
        xT = sb("xT", [P, KT, N])
        h_at = sb.at
        h_hi, h_lo = sb("h_hi", [P, KT, N], f32r), sb("h_lo", [P, KT, N], f32r)
        h_end = sb.at
        raw = [sb(f"raw{s}", [P, SLOT]) for s in range(2)]
        w_hi = [sb(f"w_hi{s}", [P, SLOT], f32r) for s in range(2)]
        w_lo = [sb(f"w_lo{s}", [P, SLOT], f32r) for s in range(2)]
        ident, upto, onward, ones = (sb(n, [P, P]) for n in ("ident", "upto", "onward", "ones"))
        b_ada = sb("b_ada", [P, 2, 48])
        vec = sb("vec", [P, N_ROWS])
        scond = sb("scond", [P, KT, 2])
        mod = [sb(f"mod{l}", [P, 48, 2]) for l in range(2)]
        ada_row = sb("ada_row", [2, W])
        gain = [[sb(f"gain{l}{m}", [P, KT, 2]) for m in range(2)] for l in range(2)]
        sq, sq_sum = sb("sq", [P, N]), sb("sq_sum", [P, N])
        stt = sb("stt", [P, 5, TT * 10])
        tbuf = sb("tbuf", [P, 2, N])
        h32 = sb("h32", [P, N])
        nbuf = (tbuf[:, 0, :], tbuf[:, 1, :], h32, sq)
        phase_at = sb.at

        ada_raw = [sb(f"ada_raw{s}", [P, SLOT]) for s in range(2)]
        part_at = sb.at
        x_stage = sb("x_stage", [P, TT, D])
        stg_a, stg_b = sb("stg_a", [96, P]), sb("stg_b", [N_ROWS, P])
        sb.at = part_at
        conv = sb("conv", [P, XBC_T, PADDED])
        sb.at = part_at + 2 * 4 * PADDED
        xpad = sb("xpad", [P, XBC_T, PADDED])
        att_tok = sb("att_tok", [P, TT, ATT_W])
        dt_tok, a_tok = sb("dt_tok", [P, TT, DTS]), sb("a_tok", [P, TT, DTS])
        dt_t = [tbuf[:, 1, i * TT * DTS:(i + 1) * TT * DTS].rearrange("p (t c) -> p t c", c=DTS) for i in range(4)]
        dt_c = sb("dt_c", [P, 2, DTS])
        d_skip = sb("d_skip", [P, ST])
        dtw = sb("dtw", [P, KT, DTS])
        dtw_hi, dtw_lo = sb("dtw_hi", [P, KT, DTS], f32r), sb("dtw_lo", [P, KT, DTS], f32r)
        zT = sb("zT", [P, ST, N])
        kc, vc = sb("kc", [P, KV_W]), sb("vc", [P, KV_W])
        qk_g = sb("qk_g", [P, 2, HD])
        cosA, sinA = sb("cosA", [P, LT, 32]), sb("sinA", [P, LT, 32])
        s0 = sb("s0", [P, NH, HD])
        qkv_at = sb.at
        qkv = sb("qkv", [P, TT, QKV_W])
        sb.at = h_at
        first_raw = [sb(f"first_raw{s}", [P, SLOT]) for s in range(5)]
        first_slots = ada_raw + first_raw
        sb.at = h_at
        qT, kT = sb("qT", [P, 4, N]), sb("kT", [P, N + PAST])
        probs, pT = sb("probs", [P, 2, N]), sb("pT", [P, 2, N])
        nmax, rsum, rrec = sb("nmax", [P, 4]), sb("rsum", [P, 4]), sb("rrec", [P, 4])
        sb.at = h_at
        G_LEN = LT * (N_LAT + P)
        Gt = [sb(f"G{g}", [P, G_LEN]) for g in range(2)]
        Gp = sb("Gp", [P, 2, P])
        x_tok = sb("x_tok", [P, TT, SSD_W])
        ecum, ce, ct2 = sb("ecum", [P, N_LAT]), sb("ce", [P, N_LAT]), sb("ct2", [P, N_LAT])
        assert sb.at <= h_end
        sb.at = qkv_at
        y_tok = sb("y_tok", [P, TT, SSD_W])
        cum, ncum = sb("cum", [P, TT, DTS]), sb("ncum", [P, TT, DTS])
        dgs = [a.rearrange("p (t n) -> p t n", t=TT) for a in (tbuf[:, 0, :], sq[:, :])]
        dm = tbuf[:, 1, :].rearrange("p (t n) -> p t n", t=TT)
        tot, wst = sb("tot", [P, DTS]), sb("wst", [P, DTS])
        b_tok = sb("b_tok", [P, 2 * HD])
        bw = sb("bw", [P, 2, 2 * HD])
        s_out = sb("s_out", [P, NH, HD])
        E_off = ada_raw[0][:, :].rearrange("p (j n) -> p j n", j=LT)
        M_off = ada_raw[1][:, :].rearrange("p (j n) -> p j n", j=LT)

        sb.at = part_at
        gu_hi, gu_lo = sb("gu_hi", [P, KT, N], f32r), sb("gu_lo", [P, KT, N], f32r)
        silu_g, gu32 = sb("silu_g", [P, N]), sb("gu32", [P, N])

        sb.at = phase_at
        S0 = sb("S0", [P, 2, 2, DV])
        qk = sb("qk", [P, 4, N])
        qg = sb("qg", [P, 2, N_LAT])
        v_tok = sb("v_tok", [P, TT, DV])
        strip = sb("strip", [P, STRIP])
        sc_sb = sb("sc_sb", [P, 2, N_LAT])
        sc_p = sb("sc_p", [P, P])
        ramp = sb("ramp", [P, 2, N_LAT])
        grow = sb("grow", [P, N_LAT])
        kw = sb("kw", [P, 2, DK])
        pcol, wcol = sb("pcol", [P, 2]), sb("wcol", [P, 2])
        acol = sb("acol", [P, 2])
        rgain = sb("rgain", [P, VT])
        cosR, sinR = sb("cosR", [P, N_LAT]), sb("sinR", [P, N_LAT])
        yg_hi, yg_lo = sb("yg_hi", [P, VT, N], f32r), sb("yg_lo", [P, VT, N], f32r)
        yR = qk

        sb.at = phase_at
        y_out = sb("y_out", [P, TT, D])

        acc = ctx.enter_context(nc.psum_tensor("acc", [P, 4, 512], f32))
        mix = ctx.enter_context(nc.psum_tensor("mix", [P, 4, 512], f32))
        accf, mixf = (t[:, :, :].rearrange("p a b -> p (a b)") for t in (acc, mix))
        ADA = mix[:, 3, 256:256 + 192].rearrange("p (l j c) -> p l j c", l=2, c=2)
        rB = mixf[:, 512:512 + N]
        ROWS = mix[0:2, 3, 0:W]
        S = Sems(nc, ctx)
        block = ctx.enter_context(nc.Block())

        SEGS = [(0, slice(0, N_CTX), slice(0, N_CTX), 0),
                (0, slice(N_CTX, HALF), slice(N_CTX, HALF), 1),
                (1, slice(0, HALF), slice(HALF, N), 1)]
        PARTS = [(slice(0, N_CTX), 0), (slice(N_CTX, N), 1)]
        tok = lambda t: slice(t * P, (t + 1) * P)
        pad = lambda t: slice(0, P) if t == 0 else slice(4 + t * P, 4 + (t + 1) * P)
        LAT = slice(4 + P, 4 + P + N_LAT)
        pair = lambda r: acc[:, 2 * r:2 * r + 2, 0:HALF]
        halves = lambda t: t.rearrange("p (b n) -> p b n", b=2)
        units = [(t, h) for t in range(TT) for h in range(NH)]

        @block.sync
        def _(eng):
            sp = Line(eng, "sp")
            job, ada = [0], [0]

            def kpn(w):
                return w.rearrange("(k p) n -> p k n", p=P)

            def load(dst, src, name):
                k = dst.shape[1]
                for a, b in ((0, k // 2), (k // 2, k)):
                    eng.dma_start(dst[:, a:b, :], src[:, a:b, :]).then_inc(S[name], sp.up(name, 16))

            def slot():
                s = job[0] % 2
                job[0] += 1
                if sp.due(f"w_lo{s}", 1):
                    eng.wait_ge(S[f"w_lo{s}"], sp.now(f"w_lo{s}", 1))
                return s

            def panel(src, cols=W):
                s = slot()
                k = src.shape[1]
                load(raw[s][:, 0:k * cols].rearrange("p (k n) -> p k n", n=cols), src, f"raw_in{s}")

            def gate_up(gate, up, f):
                s = slot()
                v = raw[s][:, :].rearrange("p (k n) -> p k n", n=W)
                for a, w in ((0, gate), (P, up)):
                    eng.dma_start(v[:, :, a:a + P], kpn(w)[:, :, bass.ds(f, P)]).then_inc(S[f"raw_in{s}"], sp.up(f"raw_in{s}", 16))

            def first_panel(n):
                dst = first_slots[n][:, :].rearrange("p (k n) -> p k n", n=W)
                load(dst, kpn(I["l0_w_ada"])[:, :, n * W:(n + 1) * W], f"first_in{n}")

            def ada_panel(w, n):
                s = ada[0] % 2
                ada[0] += 1
                if sp.due("ada_used", 2):
                    eng.wait_ge(S["ada_used"], sp.now("ada_used", 2))
                load(ada_raw[s][:, :].rearrange("p (k n) -> p k n", n=W), kpn(w)[:, :, bass.ds(n, W)], f"ada_in{s}")

            def small(dst, src):
                eng.dma_start(dst, src).then_inc(S["setup_in"], sp.up("setup_in", 16))

            rows = lambda a, n=P: a.rearrange("(r c) -> r c", c=n)
            for l in range(2):
                small(stg_a[48 * l:48 * l + 48, :], rows(I[f"l{l}_b_ada"]))
                small(stg_b[NM[l]:NM[l] + KT, :], rows(I[f"l{l}_norm_mix"]))
                small(stg_b[NF[l]:NF[l] + KT, :], rows(I[f"l{l}_norm_ffn"]))
            small(stg_b[FIN:FIN + KT, :], rows(I["final_norm"]))
            small(stg_b[COND:COND + KT, :], rows(I["c_ctx"]))
            small(stg_b[COND + KT:COND + 2 * KT, :], I["c"][0, :].rearrange("(r c) -> r c", c=P))
            small(stg_b[CONV_B:CONV_B + XBC_T, :], rows(I["l0_conv_b"]))
            small(stg_b[SSD_G:SSD_G + ST, :], rows(I["l0_ssd_gain"]))
            small(stg_b[CONV_W:CONV_W + TAPS * XBC_T, :], I["l0_conv_w"].rearrange("k (t c) -> (k t) c", c=P))
            for n, dst in enumerate((ident, upto, onward, ones)):
                small(dst[:, :], I["squares"][n, :, :])
            eng.dma_start(x_stage[:, 0, :], I["x_prompt"][0, :, :]).then_inc(S["x_in"], sp.up("x_in", 16))
            eng.dma_start(x_stage[:, 1:TT, :], I["x_sample"][0, :, :].rearrange("(t p) d -> p t d", p=P)).then_inc(S["x_in"], sp.up("x_in", 16))
            w_in, w_ada = kpn(I["l0_w_in"]), I["l0_w_ada"]
            cols = [i * W for i in range(3)] + [OFF_X + i * W for i in range(3)] + [OFF_Z + i * W for i in range(2)]
            for n in range(7):
                first_panel(n)
            for j in range(2):
                panel(w_in[:, :, cols[j]:cols[j] + W])
            sp.skip("ada_used", 7)
            eng.wait_ge(S["ada_used"], 1)
            ada_panel(w_ada, 7 * W)
            eng.wait_ge(S["x_T_read"], sp.next("x_T_read", 10))

            def aside(dst, src, slow=False):
                eng.dma_start(dst, src, allow_slow_non_contiguous=slow).then_inc(S["l0_in"], sp.up("l0_in", 16))

            aside(dtw[:, :, :], w_in[:, :, OFF_DT:OFF_DT + DTS])
            aside(kc[:, :], I["cache_k0"][0].rearrange("t h d -> t (h d)"))
            aside(vc[:, :], I["cache_v0"][0].rearrange("t h d -> t (h d)"))
            aside(qk_g[:, 0, :], I["l0_q_gain"].partition_broadcast(P))
            aside(qk_g[:, 1, :], I["l0_k_gain"].partition_broadcast(P))
            aside(dt_c[:, 0, :], I["l0_dt_bias"].rearrange("a b -> (a b)").partition_broadcast(P))
            aside(dt_c[:, 1, :], I["l0_a_log"].rearrange("a b -> (a b)").partition_broadcast(P))
            for b in range(2):
                aside(d_skip[HD * b:HD * b + HD, :],
                      I["l0_d_skip"].rearrange("(t b) -> b t", b=2)[b, :].partition_broadcast(HD), True)
                aside(s0[HD * b:HD * b + HD, :, :], I["state_ssd0"][0, b].rearrange("h n d -> n h d"))
            aside(cosA[:, :, :], I["rope_att"][0])
            aside(sinA[:, :, :], I["rope_att"][1])
            for j in range(2, 8):
                panel(w_in[:, :, cols[j]:cols[j] + W])
            eng.wait_ge(S["new_kv"], sp.next("new_kv"))
            for k, src in enumerate((qkv[:, 0, ATT_W:ATT_W + KV_W], qkv[:, 0, ATT_W + KV_W:QKV_W])):
                eng.dma_start(O[2 + k][0].rearrange("t h d -> t (h d)"), src).then_inc(S["kv_out"], sp.up("kv_out", 16))
            eng.wait_ge(S[sp.last], sp.ended())
            eng.sem_inc(S["kv_gone"], sp.told("kv_gone"))
            for n in range(8, ADA_JOBS):
                s = n % 2
                if n < 10:
                    eng.wait_ge(S[f"w_lo{s}"], 4)
                else:
                    eng.wait_ge(S["ada_used"], n - 1)
                load(raw[s][:, :].rearrange("p (k n) -> p k n", n=W), kpn(w_ada)[:, :, n * W:n * W + W], f"raw_in{s}")
            sp.skip("ada_used", ADA_JOBS - 8)
            eng.wait_ge(S["ada_used"], sp.now("ada_used"))
            for a in range(2):
                for j in range(2):
                    panel(kpn(I["l0_w_out"])[:, a * ST:a * ST + ST, j * 2 * W:(j + 1) * 2 * W], 2 * W)
            eng.wait_ge(S["s_out_ready"], sp.next("s_out_ready"))
            for b in range(2):
                eng.dma_start(O[4][0, b].rearrange("h n d -> n h d"), s_out[HD * b:HD * b + HD, :, :]).then_inc(S["out"], sp.up("out", 16))
            eng.wait_ge(S["l0_mixed"], sp.next("l0_mixed"))
            for n in range(2):
                ada_panel(I["l1_w_ada"], n * W)

            def ffn(l):
                gate, up, down = (I[f"l{l}_w_{n}"] for n in ("gate", "up", "down"))
                for f0, nf in CHUNKS:
                    per = {"w_lo0": 1, "w_lo1": 1, "raw_in0": 32, "raw_in1": 32}
                    if l == 0:
                        per |= {"ada_used": 2, "ada_in0": 32, "ada_in1": 32}
                    with sp.loop(nf // 2, per) as i:
                        for s in range(2):
                            gate_up(gate, up, (i * 2 + s + f0) * P)
                            if l == 0:
                                ada_panel(I["l1_w_ada"], (i * 2 + s + f0 + 2) * W)
                    for j in range(4):
                        panel(kpn(down)[:, f0:f0 + nf, j * W:j * W + W])

            ffn(0)
            w_in, w_out = kpn(I["l1_w_in"]), I["l1_w_out"]
            per = {"raw_in0": 128, "raw_in1": 128, "w_lo0": 4, "w_lo1": 4}
            with sp.loop(RH, per) as h:
                panel(w_in[:, :, bass.ds(h * DK, W)])
                panel(w_in[:, :, bass.ds(h * DK + D, W)])
                for j in range(2):
                    panel(w_in[:, :, bass.ds(h * DV + j * W + 2 * D, W)])
                for j in range(2):
                    panel(w_in[:, :, bass.ds(h * DV + j * W + 4 * D, W)])
                for j in range(2):
                    panel(w_out.rearrange("(h k p) n -> p (h k) n", p=P, k=VT)[:, bass.ds(h * VT, VT), j * 2 * W:(j + 1) * 2 * W], 2 * W)
            ffn(1)
            eng.wait_ge(S["y_ready"], sp.next("y_ready", 10))
            eng.dma_start(O[0][0], y_out[:, 0, :]).then_inc(S["out"], sp.up("out", 16))
            eng.dma_start(O[1][0].rearrange("(t p) d -> p t d", p=P), y_out[:, 1:TT, :]).then_inc(S["out"], sp.up("out", 16))
            eng.wait_ge(S[sp.last], sp.ended())
            for b in range(2):
                eng.wait_ge(S[f"fs_out{b}"], 32 * RH)

        @block.tensor
        def _(eng):
            pe = Line(eng, "pe")
            job, tile, ada = [0], [0], [0]
            mm = eng.matmul

            def next_tile():
                r = tile[0] % 2
                tile[0] += 1
                if pe.due(f"acc_free{r}", 1):
                    eng.wait_ge(S[f"acc_free{r}"], pe.now(f"acc_free{r}", 1))
                return r

            def next_job():
                s = job[0] % 2
                job[0] += 1
                eng.wait_ge(S[f"w_lo{s}"], pe.next(f"w_lo{s}"))
                return s

            def tile_a(s, xh, xl, kts, col, cols=W, came=None, h_from=None):
                r = next_tile()
                for k in range(kts):
                    if came:
                        eng.wait_ge(S[came], pe.next(came))
                    if h_from is not None:
                        eng.wait_ge(S["h_ready"], h_from + k + 1)
                    for n, (w, x) in enumerate(((w_hi[s], xh), (w_hi[s], xl), (w_lo[s], xh))):
                        for b in range(2):
                            last = mm(acc[:, 2 * r + b, 0:HALF], w[:, k * cols + col:k * cols + col + P],
                                      x[:, k, b * HALF:(b + 1) * HALF],
                                      start=(k == 0 and n == 0), stop=(k == kts - 1 and n == 2))
                last.then_inc(S[f"acc_ready{r}"], pe.up(f"acc_ready{r}"))

            def first_pair(s):
                r = [next_tile() for _ in range(2)]
                for k in range(KT):
                    eng.wait_ge(S["h_ready"], pe.next("h_ready"))
                    for c in range(2):
                        for n, (w, x) in enumerate(((w_hi[s], h_hi), (w_hi[s], h_lo), (w_lo[s], h_hi))):
                            for b in range(2):
                                last = mm(acc[:, 2 * r[c] + b, 0:HALF], w[:, k * W + c * P:k * W + (c + 1) * P],
                                          x[:, k, b * HALF:(b + 1) * HALF],
                                          start=(k == 0 and n == 0), stop=(k == KT - 1 and n == 2))
                        if k == KT - 1:
                            last.then_inc(S[f"acc_ready{r[c]}"], pe.up(f"acc_ready{r[c]}"))

            def tile_b(s, t, came=None):
                r = next_tile()
                for k in range(KT):
                    if came:
                        eng.wait_ge(S[came], pe.next(came))
                    for n, (x, w) in enumerate(((h_hi, w_hi[s]), (h_hi, w_lo[s]), (h_lo, w_hi[s]))):
                        last = mm(acc[:, 2 * r, 0:W], x[:, k, tok(t)], w[:, k * W:(k + 1) * W],
                                  start=(k == 0 and n == 0), stop=(k == KT - 1 and n == 2))
                last.then_inc(S[f"acc_ready{r}"], pe.up(f"acc_ready{r}"))

            def ada_turn(l, n):
                eng.wait_ge(S["row_in"], pe.next("row_in"))
                for c in range(2):
                    last = mm(ADA[:, l, bass.ds(n * 2 + c, 1), :].rearrange("p o c -> p (o c)"),
                              ada_row[:, c * P:(c + 1) * P], ident[0:2, 0:2], start=True, stop=True)
                last.then_inc(S["ada_turned"], pe.up("ada_turned"))

            def ada_job(l, n, pending=True, first=False):
                if pending:
                    ada_turn(l, n - 1)
                if first:
                    w = first_slots[n]
                    eng.wait_ge(S[f"first_in{n}"], 32)
                elif l == 0 and n >= 8:
                    w = raw[n % 2]
                    eng.wait_ge(S[f"raw_in{n % 2}"], 32 * (4 + (n - 8) // 2 + 1))
                else:
                    s = ada[0] % 2
                    ada[0] += 1
                    w = ada_raw[s]
                    eng.wait_ge(S[f"ada_in{s}"], pe.next(f"ada_in{s}", 32))
                for k in range(KT):
                    last = mm(ROWS, scond[:, k, :], w[:, k * W:(k + 1) * W], start=(k == 0), stop=(k == KT - 1))
                last.then_inc(S["ada_used"], pe.up("ada_used"))

            def rms_sum():
                eng.wait_ge(S["sq_done"], pe.next("sq_done"))
                for t in range(TT):
                    last = mm(mixf[:, t:t + 1], sq_sum[:, tok(t)], ones[:, 0:1], start=True, stop=True)
                last.then_inc(S["stat"], pe.up("stat"))

            def rms_back():
                eng.wait_ge(S["rinv"], pe.next("rinv"))
                for t in range(TT):
                    last = mm(mixf[:, 512 + t * P:512 + (t + 1) * P],
                              stt[:, 4, t:t + 1].broadcast_to([P, P]), ident[:, :], start=True, stop=True)
                last.then_inc(S["rb"], pe.up("rb"))

            def rms():
                rms_sum()
                rms_back()

            eng.wait_ge(S["setup_in"], pe.next("setup_in", 16 * 16))
            eng.transpose(mix[:, 0, 0:96], stg_a[:, :], ident[0:96, 0:96])
            eng.transpose(mix[:, 0, 96:96 + N_ROWS], stg_b[:, :], ident[0:N_ROWS, 0:N_ROWS]).then_inc(S["vec_T"], pe.up("vec_T"))
            eng.wait_ge(S["x_in"], pe.next("x_in", 32))
            for n in range(2 * TT):
                t, half = divmod(n, 2)
                if pe.due("x_T_read", 2):
                    eng.wait_ge(S["x_T_read"], pe.now("x_T_read", 2))
                for k in range(4):
                    last = eng.transpose(acc[:, n % 2, k * P:(k + 1) * P],
                                         x_stage[:, t, (half * 4 + k) * P:(half * 4 + k + 1) * P], ident[:, :])
                last.then_inc(S["x_T"], pe.up("x_T"))
            eng.wait_ge(S["cond"], pe.next("cond"))
            for n in range(8):
                ada_job(0, n, n > 0, first=n < 7)
            ada_turn(0, 7)
            rms()
            eng.wait_ge(S["mod_read"], pe.next("mod_read"))
            eng.wait_ge(S["x_T_read"], pe.now("x_T_read"))
            for j in range(8):
                s = next_job()
                for t in range(TT if j < 3 else 2):
                    if j < 3:
                        tile_b(s, t, "h_ready" if j == 0 and t == 0 else None)
                    else:
                        tile_a(s, h_hi, h_lo, KT, t * P)
                if j == 5:
                    eng.wait_ge(S["dtw_lo"], pe.next("dtw_lo"))
                    r = next_tile()
                    for t in range(TT):
                        for k in range(KT):
                            for m, (x, w) in enumerate(((h_hi, dtw_hi), (h_hi, dtw_lo), (h_lo, dtw_hi))):
                                last = mm(acc[:, 2 * r, t * DTS:(t + 1) * DTS], x[:, k, tok(t)], w[:, k, :],
                                          start=(k == 0 and m == 0), stop=(k == KT - 1 and m == 2))
                    last.then_inc(S[f"acc_ready{r}"], pe.up(f"acc_ready{r}"))
            eng.wait_ge(S["acc_free0"], pe.now("acc_free0"))
            eng.wait_ge(S["acc_free1"], pe.now("acc_free1"))
            eng.wait_ge(S["l0_in"], pe.next("l0_in", 16 * 13))
            eng.wait_ge(S["roped"], pe.next("roped"))
            for t in range(TT):
                eng.transpose(accf[:, t * P:(t + 1) * P], qkv[:, t, ATT_W:ATT_W + KV_W], ident[:, :])
            eng.transpose(accf[:, N:N + PAST], kc[:, :], ident[:, :]).then_inc(S["kT_made"], pe.up("kT_made"))
            for t in range(TT):
                if pe.due("qT_sb", 2):
                    eng.wait_ge(S["qT_sb"], pe.now("qT_sb", 2))
                for j in range(4):
                    last = eng.transpose(acc[:, 2 + t % 2, j * P:(j + 1) * P], qkv[:, t, j * P:(j + 1) * P], ident[:, :])
                last.then_inc(S["qT_made"], pe.up("qT_made"))
            eng.wait_ge(S["qT_sb"], pe.now("qT_sb"))
            U = len(units)
            for i in range(U + 2):
                if i < U:
                    t, h = units[i]
                    b, g = i % 2, h // 4
                    if pe.due("exp_done", 2):
                        eng.wait_ge(S["exp_done"], pe.now("exp_done", 2))
                    q = qT[HD * g:HD * g + HD, h % 4, tok(t)]
                    spans = [(0, N_CTX, 0)] if t == 0 else [(0, 512, P), (512, P, P + 512)]
                    for at, n_, k0 in spans:
                        last = mm(mixf[:, 1024 * b + at:1024 * b + at + n_], q, kT[HD * g:HD * g + HD, k0:k0 + n_],
                                  start=True, stop=True)
                    last.then_inc(S["scores"], pe.up("scores"))
                if 1 <= i <= U:
                    t, h = units[i - 1]
                    b = (i - 1) % 2
                    eng.wait_ge(S["exp_done"], i)
                    if pe.due("att_read", 2):
                        eng.wait_ge(S["att_read"], pe.now("att_read", 2))
                    for m in range(1 if t == 0 else TT):
                        last = eng.transpose(accf[:, 1024 * b + m * P:1024 * b + (m + 1) * P],
                                             probs[:, b, m * P:(m + 1) * P], ident[:, :])
                    last.then_inc(S["pT_made"], pe.up("pT_made"))
                if i >= 2:
                    t, h = units[i - 2]
                    b, g = i % 2, h // 4
                    eng.wait_ge(S["pT_sb"], pe.next("pT_sb"))
                    vs = [qkv[:, t_, ATT_W + KV_W + HD * g:ATT_W + KV_W + HD * g + HD] for t_ in ([0] if t == 0 else range(1, TT))]
                    if t:
                        vs.append(vc[:, HD * g:HD * g + HD])
                    for m, v in enumerate(vs):
                        last = mm(accf[:, 1024 * b + 768:1024 * b + 768 + HD], pT[:, b, m * P:(m + 1) * P], v,
                                  start=(m == 0), stop=(m == len(vs) - 1))
                    last.then_inc(S["att_made"], pe.up("att_made"))
            eng.wait_ge(S["att_read"], U)
            eng.wait_ge(S["exp_done"], U)
            eng.wait_ge(S["a_ready"], pe.next("a_ready"))
            for t in range(TT):
                for d in range(2):
                    tri = (upto, onward)[d]
                    others = [] if t == 0 else (range(1, t) if d == 0 else range(t + 1, TT))
                    parts = [(ones, t_) for t_ in others] + [(tri, t)]
                    for m, (w, t_) in enumerate(parts):
                        last = mm(mixf[:, t * DTS + NH * d:t * DTS + NH * d + NH], w[:, :], a_tok[:, t_, NH * d:NH * d + NH],
                                  start=(m == 0), stop=(m == len(parts) - 1))
            last.then_inc(S["cum_made"], pe.up("cum_made"))
            eng.wait_ge(S["conv_ready"], pe.next("conv_ready"))
            for t in range(TT):
                if pe.due("xt_read", 2):
                    eng.wait_ge(S["xt_read"], pe.now("xt_read", 2))
                for j in range(ST):
                    last = eng.transpose(acc[:, t % 2, j * P:(j + 1) * P], conv[:, j, pad(t)], ident[:, :])
                last.then_inc(S["xt_made"], pe.up("xt_made"))
            eng.transpose(acc[:, 2, 0:P], conv[:, ST, pad(0)], ident[:, :]).then_inc(S["bt_made"], pe.up("bt_made"))
            for g in range(2):
                B, C = (conv[HD * g:HD * g + HD, ST + m, :] for m in range(2))
                for J in range(LT):
                    n = g * (LT + 1) + J
                    if pe.due("cb_read", 2):
                        eng.wait_ge(S["cb_read"], pe.now("cb_read", 2))
                    mm(mix[:, 1 + n % 2, :], B[:, pad(J + 1)], C[:, LAT], start=True, stop=True).then_inc(S["cb_made"], pe.up("cb_made"))
                n += 1
                if pe.due("cb_read", 2):
                    eng.wait_ge(S["cb_read"], pe.now("cb_read", 2))
                mm(mix[:, 1 + n % 2, 0:P], B[:, pad(0)], C[:, pad(0)], start=True, stop=True).then_inc(S["cb_made"], pe.up("cb_made"))
            eng.wait_ge(S["cum_read"], pe.next("cum_read"))
            eng.wait_ge(S["xt_read"], TT)
            eng.wait_ge(S["bt_read"], 1)
            eng.wait_ge(S["cb_read"], 2 * (LT + 1))
            for h in range(NH + 1):
                if h < NH:
                    if pe.due("rows_read", 1):
                        eng.wait_ge(S["rows_read"], pe.now("rows_read", 1))
                    for d in range(2):
                        for t in range(TT):
                            c = cum[:, t, NH * d + h:NH * d + h + 1].broadcast_to([P, P])
                            last = mm(accf[:, 1024 * d + t * P:1024 * d + (t + 1) * P], c, ident[:, :], start=True, stop=True)
                    last.then_inc(S["rows_made"], pe.up("rows_made"))
                    ada_job(0, 8 + 2 * h, h > 0)
                if h >= 1:
                    g = h - 1
                    eng.wait_ge(S["m_ready"], pe.next("m_ready"))
                    if pe.due("y_read", 2):
                        eng.wait_ge(S["y_read"], pe.now("y_read", 2))
                    cols = slice(g * HD, (g + 1) * HD)
                    bank = mix[:, g % 2, 0:TT * HD]
                    dg = dgs[g % 2]
                    mm(bank[:, 0:HD], dg[:, 0, :], x_tok[:, 0, cols], start=True, stop=True)
                    for I_ in range(LT):
                        o = bank[:, (I_ + 1) * HD:(I_ + 2) * HD]
                        for J in range(LT):
                            m_ = dg[:, I_ + 1, :] if J == I_ else M_off[:, J, I_ * P:(I_ + 1) * P]
                            mm(o, m_, x_tok[:, J + 1, cols], start=(J == 0), stop=False)
                        last = mm(o, ce[:, I_ * P:(I_ + 1) * P], s0[:, g, :], start=False, stop=True)
                    last.then_inc(S["y_made"], pe.up("y_made"))
                if h < NH:
                    ada_job(0, 9 + 2 * h)
            ada_turn(0, ADA_JOBS - 1)
            for h in range(NH):
                eng.wait_ge(S["bw_ready"], pe.next("bw_ready"))
                mm(mix[:, 2, h * HD:(h + 1) * HD], bw[:, h % 2, :], x_tok[:, 0, h * HD:(h + 1) * HD], start=True, stop=True).then_inc(S["fs_made"], pe.up("fs_made"))
            eng.wait_ge(S["y_read"], NH)
            for t in range(TT):
                if pe.due("aT_read", 2):
                    eng.wait_ge(S["aT_read"], pe.now("aT_read", 2))
                for j in range(ST):
                    last = eng.transpose(acc[:, 2 + t % 2, j * P:(j + 1) * P], att_tok[:, t, j * P:(j + 1) * P], ident[:, :])
                last.then_inc(S["aT_made"], pe.up("aT_made"))
            for t in range(TT):
                if pe.due("yT_read", 2):
                    eng.wait_ge(S["yT_read"], pe.now("yT_read", 2))
                for j in range(ST):
                    last = eng.transpose(acc[:, t % 2, j * P:(j + 1) * P], y_tok[:, t, j * P:(j + 1) * P], ident[:, :])
                last.then_inc(S["yT_made"], pe.up("yT_made"))
            eng.wait_ge(S["s_out_ready"], 1)
            eng.wait_ge(S["aT_read"], TT)
            eng.wait_ge(S["yT_read"], TT)
            eng.wait_ge(S["h_ready"], pe.next("h_ready"))
            for j in range(2):
                s = next_job()
                for c in range(4):
                    tile_a(s, h_hi, h_lo, ST, c * P, 2 * W)
                    if j == 1 and c == 1:
                        rms_sum()
            rms_back()
            for j in range(2):
                s = next_job()
                for c in range(4):
                    tile_a(s, h_hi[:, ST:, :], h_lo[:, ST:, :], ST, c * P, 2 * W, came="h_ready" if j == c == 0 else None)
                if j == 0:
                    eng.wait_ge(S["mod_read"], pe.next("mod_read"))
                ada_job(1, j, j > 0)

            def ffn(l):
                rms()
                def gate_up(f, s_, first):
                    s = next_job()
                    if first:
                        first_pair(s)
                    else:
                        tile_a(s, h_hi, h_lo, KT, 0)
                        tile_a(s, h_hi, h_lo, KT, P)
                    if l == 0:
                        ada_job(1, f + s_ + 2)

                for f0, nf in CHUNKS:
                    per = {"w_lo0": 1, "w_lo1": 1, "acc_free0": 2, "acc_free1": 2, "acc_ready0": 2, "acc_ready1": 2}
                    if l == 0:
                        per |= {"ada_in0": 32, "ada_in1": 32, "ada_used": 2, "row_in": 2, "ada_turned": 2}
                    turns = nf // 2
                    if f0 == 0:
                        for s_ in range(2):
                            gate_up(0, s_, s_ == 0)
                        turns -= 1
                    with pe.loop(turns, per) as i:
                        for s_ in range(2):
                            gate_up(i * 2 + f0 + 2 * (f0 == 0), s_, False)
                    for j in range(4):
                        s = next_job()
                        tile_a(s, gu_hi, gu_lo, nf, 0, came="gu_ready" if j == 0 else None)
                        tile_a(s, gu_hi, gu_lo, nf, P)

            ffn(0)
            ada_turn(1, ADA_JOBS - 1)
            rms()
            pe.skip("h_ready", KT)
            h_made = pe.now("h_ready")
            per = {"w_lo0": 4, "w_lo1": 4, "acc_free0": 13, "acc_free1": 13, "acc_ready0": 13, "acc_ready1": 13,
                   "rope_done": 1, "kp_made": 1, "kw_ready": 1, "head_in": 16 * 8, "score_made": 5, "sc_ready": 5,
                   "y_part": 5, "qg_ready": 2, "state_done": 2, "v_in": 1, "fs_made1": 4, "fs_ready": 4, "yr_read": 1,
                   "sq_done": 1, "stat": 1, "rinv": 1, "rb": 1, "yg_ready": 4}
            with pe.loop(RH, per):
                for j in range(2):
                    s = next_job()
                    for c in range(2):
                        tile_a(s, h_hi, h_lo, KT, c * P, h_from=h_made - KT if j == c == 0 else None)
                for j in range(2):
                    s = next_job()
                    for t in range(TT):
                        tile_b(s, t)
                eng.wait_ge(S["acc_free0"], pe.now("acc_free0"))
                eng.wait_ge(S["acc_free1"], pe.now("acc_free1"))
                eng.wait_ge(S["rope_done"], pe.next("rope_done"))
                for k in range(2):
                    last = eng.transpose(mix[:, 0, k * P:(k + 1) * P], qk[:, 2 + k, 0:P], ident[:, :])
                last.then_inc(S["kp_made"], pe.up("kp_made"))

                def score(J):
                    n = N_LAT if J < LT else N_CTX
                    i0, j0 = (N_CTX, (J + 1) * P) if J < LT else (0, 0)
                    for k in range(2):
                        last = mm(mix[:, 1 + J % 2, 0:n], qk[:, 2 + k, j0:j0 + P], qk[:, k, i0:i0 + n],
                                  start=(k == 0), stop=(k == 1))
                    last.then_inc(S["score_made"], pe.up("score_made"))

                def states(b):
                    eng.wait_ge(S["qg_ready"], pe.next("qg_ready"))
                    for v in range(VT):
                        for k in range(2):
                            last = mm(acc[:, v, :], S0[:, b, k, v * P:(v + 1) * P], qg[:, k, :],
                                      start=(b == 0 and k == 0), stop=(b == 1 and k == 1))
                    last.then_inc(S["state_done"], pe.up("state_done"))

                score(0)
                score(1)
                eng.wait_ge(S["head_in"], pe.next("head_in", 16 * 8))
                states(0)
                eng.wait_ge(S["v_in"], pe.next("v_in"))
                for J in range(LT + 1):
                    eng.wait_ge(S["sc_ready"], pe.next("sc_ready"))
                    if J == LT:
                        eng.wait_ge(S["kw_ready"], pe.next("kw_ready"))
                    for v in range(VT):
                        if J < LT:
                            last = mm(acc[:, v, :], v_tok[:, J + 1, v * P:(v + 1) * P], sc_sb[:, J % 2, :], start=False, stop=False)
                        else:
                            last = mm(mix[:, 0, v * P:(v + 1) * P], v_tok[:, 0, v * P:(v + 1) * P], sc_p[:, :], start=True, stop=True)
                    last.then_inc(S["y_part"], pe.up("y_part"))
                    if J + 2 <= LT:
                        score(J + 2)
                def final_state(n):
                    b, k = divmod(n, 2)
                    if n >= 2:
                        eng.wait_ge(S["fs_ready"], pe.next("fs_ready"))
                    mm(mix[:, 1 + n % 2, :], kw[:, b, k * P:(k + 1) * P], v_tok[:, 0, :], start=True, stop=True).then_inc(S["fs_made1"], pe.up("fs_made1"))

                final_state(0)
                final_state(1)
                states(1)
                final_state(2)
                final_state(3)
                eng.wait_ge(S["yr_read"], pe.next("yr_read"))
                s = next_job()
                tile_a(s, h_hi, h_lo, KT, 0)
                rms_sum()
                tile_a(s, h_hi, h_lo, KT, P)
                eng.wait_ge(S["fs_ready"], pe.next("fs_ready", 2))
                rms_back()
                s = next_job()
                for c in range(2):
                    tile_a(s, h_hi, h_lo, KT, c * P)
                for j in range(2):
                    s = next_job()
                    for c in range(4):
                        tile_a(s, yg_hi, yg_lo, VT, c * P, 2 * W, came="yg_ready" if j == c == 0 else None)
            ffn(1)
            rms()
            for t in range(TT):
                for half in range(2):
                    n = 2 * t + half
                    if n == 0:
                        eng.wait_ge(S["final_ready"], pe.next("final_ready"))
                    if pe.due("y_ready", 2):
                        eng.wait_ge(S["y_ready"], pe.now("y_ready", 2))
                    for k in range(4):
                        last = eng.transpose(acc[:, n % 2, k * P:(k + 1) * P], xT[:, half * 4 + k, tok(t)], ident[:, :])
                    last.then_inc(S["out_T"], pe.up("out_T"))

        @block.scalar
        def _(eng):
            ac = Line(eng, "act")
            act = eng.activation
            job, tile = [0], [0]

            def split_hi():
                s = job[0] % 2
                job[0] += 1
                eng.wait_ge(S[f"raw_in{s}"], ac.next(f"raw_in{s}", 32))
                act(w_hi[s][:, :], raw[s][:, :], ACT.Copy).then_inc(S[f"w_hi{s}"], ac.up(f"w_hi{s}"))

            def ada_rows():
                eng.wait_ge(S["ada_used"], ac.next("ada_used"))
                act(ada_row[:, :], ROWS, ACT.Copy).then_inc(S["row_in"], ac.up("row_in"))

            def tile_of():
                r = tile[0] % 2
                tile[0] += 1
                eng.wait_ge(S[f"acc_ready{r}"], ac.next(f"acc_ready{r}"))
                return r

            def pass_tiles(n):
                for _ in range(n - 1):
                    ac.skip(f"acc_ready{tile[0] % 2}")
                    tile[0] += 1
                tile_of()

            def root(n=TT):
                eng.wait_ge(S["mean"], ac.next("mean"))
                act(stt[:, 1, 0:n], stt[:, 0, 0:n], ACT.Sqrt).then_inc(S["root"], ac.up("root"))

            def modulate(l, m):
                for k in range(KT):
                    eng.wait_ge(S["normed"], ac.next("normed"))
                    for cols, c in PARTS:
                        ins = act(h_hi[:, k, cols], nbuf[k % 4][:, cols], ACT.Identity, bias=mod[l][:, SH[m] + k, c:c + 1])
                    ins.then_inc(S["h_hi"], ac.up("h_hi"))

            eng.wait_ge(S["vec_read"], ac.next("vec_read"))
            act(scond[:, :, :].rearrange("p k c -> p c k"),
                       vec[:, COND:COND + 2 * KT].rearrange("p (c k) -> p c k", c=2), ACT.Silu).then_inc(S["cond"], ac.up("cond"))
            for n in range(7):
                ada_rows()
            split_hi()
            split_hi()
            ada_rows()
            root()
            eng.wait_ge(S["gain_ready"], ac.next("gain_ready"))
            modulate(0, 0)
            eng.wait_ge(S["l0_in"], ac.next("l0_in", 16 * 13))
            act(dtw_hi[:, :, :], dtw[:, :, :], ACT.Copy).then_inc(S["dtw_hi"], ac.up("dtw_hi"))
            for j in range(8):
                if j < 3:
                    for t in range(TT):
                        r = tile_of()
                        dst, src = qkv[:, t, j * W:(j + 1) * W], acc[:, 2 * r, 0:W]
                        if j < 2:
                            dst = qkv[:, t, 0:ATT_W].rearrange("p (i g d) -> p i g d", g=2, d=HD)[:, :, j, :]
                            src = src.rearrange("p (i d) -> p i d", d=HD)
                        act(dst, src, ACT.Copy).then_inc(S["act"], ac.up("act"))
                        eng.wait_ge(S[ac.last], ac.ended())
                        eng.sem_inc(S[f"acc_free{r}"], ac.told(f"acc_free{r}"))
                    if j == 2:
                        eng.wait_ge(S[ac.last], ac.ended())
                        eng.sem_inc(S["qkv_in"], ac.told("qkv_in"))
                else:
                    for c in range(2):
                        r = tile_of()
                        i = (j - 3) * 2 + c
                        if j < 6:
                            for b, src, dst, _ in SEGS:
                                o = 2 if dst.start == 0 else 6
                                ins = act(xpad[:, i, dst.start + o:dst.stop + o], acc[:, 2 * r + b, src], ACT.Copy)
                            ins.then_inc(S["act"], ac.up("act"))
                            eng.wait_ge(S[ac.last], ac.ended())
                            eng.sem_inc(S[f"acc_free{r}"], ac.told(f"acc_free{r}"))
                            eng.wait_ge(S[ac.last], ac.ended())
                            eng.sem_inc(S["xb_in"], ac.told("xb_in"))
                        else:
                            act(halves(zT[:, i - 6, :]), pair(r), ACT.Silu).then_inc(S["act"], ac.up("act"))
                            eng.wait_ge(S[ac.last], ac.ended())
                            eng.sem_inc(S[f"acc_free{r}"], ac.told(f"acc_free{r}"))
                if j == 5:
                    r = tile_of()
                    act(dt_tok[:, :, :].rearrange("p t c -> p (t c)"), acc[:, 2 * r, 0:TT * DTS], ACT.Copy).then_inc(S["act"], ac.up("act"))
                    eng.wait_ge(S[ac.last], ac.ended())
                    eng.sem_inc(S[f"acc_free{r}"], ac.told(f"acc_free{r}"))
                    eng.wait_ge(S[ac.last], ac.ended())
                    eng.sem_inc(S["dt_in"], ac.told("dt_in"))
                if j < 6:
                    split_hi()
                if j == 3:
                    root(TT * 10)
            eng.wait_ge(S["dt_abs"], ac.next("dt_abs"))
            act(dt_t[1][:, :, :], dt_t[1][:, :, :], ACT.Exp, scale=-1.0).then_inc(S["dt_exp"], ac.up("dt_exp"))
            eng.wait_ge(S["dt_u"], ac.next("dt_u"))
            act(dt_t[3][:, :, :], dt_t[0][:, :, :], ACT.Ln)
            act(dt_c[:, 1, :], dt_c[:, 1, :], ACT.Exp).then_inc(S["dt_ln"], ac.up("dt_ln"))
            eng.wait_ge(S["kT_made"], ac.next("kT_made"))
            act(kT[:, :], accf[:, 0:N + PAST], ACT.Copy).then_inc(S["act"], ac.up("act"))
            for t in range(TT):
                eng.wait_ge(S["qT_made"], ac.next("qT_made"))
                act(qT[:, :, tok(t)], acc[:, 2 + t % 2, :].rearrange("p (j n) -> p j n", j=4), ACT.Copy).then_inc(S["qT_sb"], ac.up("qT_sb"))
            for u, (t, h) in enumerate(units):
                b = u % 2
                n = N_CTX if t == 0 else N
                eng.wait_ge(S["max_ready"], ac.next("max_ready"))
                if ac.due("pT_made", 2):
                    eng.wait_ge(S["pT_made"], ac.now("pT_made", 2))
                act(probs[:, b, 0:n], mixf[:, 1024 * b:1024 * b + n], ACT.Exp, bias=nmax[:, u % 4:u % 4 + 1],
                           scale=ATT_SCALE, accum_out=rsum[:, u % 4:u % 4 + 1]).then_inc(S["exp_done"], ac.up("exp_done"))
            for i in range(XBC_T):
                if i % 2 == 0:
                    eng.wait_ge(S["conv_raw"], ac.next("conv_raw"))
                for cols in (slice(0, N_CTX), LAT):
                    ins = act(conv[:, i, cols], conv[:, i, cols], ACT.Silu, bias=vec[:, CONV_B + i:CONV_B + i + 1])
            ins.then_inc(S["conv_ready"], ac.up("conv_ready"))
            eng.wait_ge(S["cum_read"], ac.next("cum_read"))
            for h in range(NH):
                eng.wait_ge(S["arg_ready"], ac.next("arg_ready"))
                act(dgs[h % 2], dgs[h % 2], ACT.Exp).then_inc(S["diag_exp"], ac.up("diag_exp"))
                if ac.due("m_ready", 1):
                    eng.wait_ge(S["m_ready"], ac.now("m_ready", 1))
                for J in range(LT):
                    if J < LT - 1:
                        act(E_off[:, J, (J + 1) * P:], accf[:, (J + 2) * P:N], ACT.Exp, bias=ncum[:, J + 1, h:h + 1])
                    if J:
                        act(E_off[:, J, 0:J * P], accf[:, 1024 + P:1024 + (J + 1) * P], ACT.Exp,
                            bias=ncum[:, J + 1, NH + h:NH + h + 1])
                for b in range(2):
                    ins = act(ecum[HD * b:HD * b + HD, :], accf[HD * b:HD * b + HD, 1024 * b + P:1024 * b + N], ACT.Exp)
                ins.then_inc(S["rows_read"], ac.up("rows_read"))
                ada_rows()
                ada_rows()
            eng.wait_ge(S["wst_arg"], ac.next("wst_arg"))
            act(wst[:, :], wst[:, :], ACT.Exp).then_inc(S["wst_exp"], ac.up("wst_exp"))
            for s in range(2):
                ac.skip(f"raw_in{s}", 32 * (ADA_JOBS - 8) // 2)
            split_hi()
            split_hi()
            for t in range(TT):
                eng.wait_ge(S["aT_made"], ac.next("aT_made"))
                act(h_hi[:, 0:ST, tok(t)], acc[:, 2 + t % 2, :].rearrange("p (j n) -> p j n", j=4), ACT.Copy).then_inc(S["h_hi"], ac.up("h_hi"))
            pass_tiles(4)
            split_hi()
            root()
            for j in range(ST):
                eng.wait_ge(S["y32_ready"], ac.next("y32_ready"))
                act(h_hi[:, ST + j, :], h32[:, :], ACT.Copy).then_inc(S["h_hi"], ac.up("h_hi"))
            pass_tiles(4)
            split_hi()
            for j in range(2):
                pass_tiles(4)
                split_hi()
                ada_rows()

            def ffn(l):
                root()
                if l == 0:
                    eng.wait_ge(S["gain_ready"], ac.next("gain_ready"))
                modulate(l, 1)
                for f0, nf in CHUNKS:
                    per = {"acc_ready0": 2, "acc_ready1": 2, "acc_free0": 2, "silu_ready": 2, "gu32_ready": 2, "gu_hi": 2,
                           "gu_ready": 2, "raw_in0": 32, "raw_in1": 32, "w_hi0": 1, "w_hi1": 1, "act": 2}
                    if l == 0:
                        per |= {"ada_used": 2, "row_in": 2}
                    with ac.loop(nf // 2, per) as i:
                        for s in range(2):
                            r = tile_of()
                            act(halves(silu_g[:, :]), pair(r), ACT.Silu).then_inc(S["act"], ac.up("act"))
                            eng.wait_ge(S[ac.last], ac.ended())
                            eng.sem_inc(S[f"acc_free{r}"], ac.told(f"acc_free{r}"))
                            eng.wait_ge(S[ac.last], ac.ended())
                            eng.sem_inc(S["silu_ready"], ac.told("silu_ready"))
                            tile_of()
                            split_hi()
                            eng.wait_ge(S["gu32_ready"], ac.next("gu32_ready"))
                            act(gu_hi[:, bass.ds(i * 2 + s, 1), :].rearrange("p o n -> p (o n)"), gu32[:, :], ACT.Copy).then_inc(S["gu_hi"], ac.up("gu_hi"))
                            if l == 0:
                                ada_rows()
                    for j in range(4):
                        pass_tiles(2)
                        if not (l == 1 and f0 == CHUNKS[-1][0] and j >= 2):
                            split_hi()

            ffn(0)
            root()
            eng.wait_ge(S["gain_ready"], ac.next("gain_ready"))
            modulate(1, 0)
            per = {"acc_ready0": 13, "acc_ready1": 13, "acc_free0": 9, "acc_free1": 9, "raw_in0": 128, "raw_in1": 128,
                   "w_hi0": 4, "w_hi1": 4, "qk_in": 1, "v_in": 1, "acol_ready": 1, "head_in": 128, "decay_exp": 1, "arg1_ready": 1, "strip_exp": 1,
                   "grow_used": 2, "grow_ready": 2, "wcol_ready": 1, "mean": 1, "root": 1, "z32_ready": 4, "yg_hi": 4, "yg_ready": 4,
                   "g_in": 4, "fs_made1": 4, "fs_ready": 4, "fs_out0": 32, "fs_out1": 32, "act": 18}
            with ac.loop(RH, per):
                eng.wait_ge(S["head_in"], ac.next("head_in", 128))
                act(acol[:, :], acol[:, :], ACT.Exp).then_inc(S["decay_exp"], ac.up("decay_exp"))
                for j in range(2):
                    for c in range(2):
                        r = tile_of()
                        act(halves(qk[:, 2 * j + c, :]), pair(r), ACT.Copy, scale=1.0 if j == 0 else K_SCALE).then_inc(S["act"], ac.up("act"))
                        eng.wait_ge(S[ac.last], ac.ended())
                        eng.sem_inc(S[f"acc_free{r}"], ac.told(f"acc_free{r}"))
                    split_hi()
                eng.wait_ge(S[ac.last], ac.ended())
                eng.sem_inc(S["qk_in"], ac.told("qk_in"))
                eng.wait_ge(S["arg1_ready"], ac.next("arg1_ready"))
                act(strip[:, :], strip[:, :], ACT.Exp).then_inc(S["strip_exp"], ac.up("strip_exp"))
                act(grow[:, :], ramp[:, 0, :], ACT.Exp, scale=acol[:, 0:1]).then_inc(S["grow_ready"], ac.up("grow_ready"))
                for b in range(2):
                    ins = act(wcol[:, b:b + 1], pcol[:, b:b + 1], ACT.Exp, scale=acol[:, b:b + 1])
                ins.then_inc(S["wcol_ready"], ac.up("wcol_ready"))
                for j in range(2):
                    for t in range(TT):
                        r = tile_of()
                        act(v_tok[:, t, j * W:(j + 1) * W], acc[:, 2 * r, 0:W], ACT.Copy).then_inc(S["act"], ac.up("act"))
                        eng.wait_ge(S[ac.last], ac.ended())
                        eng.sem_inc(S[f"acc_free{r}"], ac.told(f"acc_free{r}"))
                    split_hi()
                eng.wait_ge(S[ac.last], ac.ended())
                eng.sem_inc(S["v_in"], ac.told("v_in"))
                eng.wait_ge(S["grow_used"], ac.next("grow_used"))
                act(grow[:, :], ramp[:, 1, :], ACT.Exp, scale=acol[:, 1:2]).then_inc(S["grow_ready"], ac.up("grow_ready"))
                eng.wait_ge(S["grow_used"], ac.next("grow_used"))
                for n in range(4):
                    eng.wait_ge(S["fs_made1"], ac.next("fs_made1"))
                    if n >= 2:
                        eng.wait_ge(S[f"fs_out{n % 2}"], ac.next(f"fs_out{n % 2}", 16))
                    act(tbuf[:, n % 2, 0:DV], mix[:, 1 + n % 2, :], ACT.Copy).then_inc(S["fs_ready"], ac.up("fs_ready"))
                def y_high(v):
                    eng.wait_ge(S["z32_ready"], ac.next("z32_ready"))
                    act(yg_hi[:, v, :], h32[:, :], ACT.Copy).then_inc(S["yg_hi"], ac.up("yg_hi"))

                for v in range(VT):
                    r = tile_of()
                    if v < 2:
                        eng.wait_ge(S[f"fs_out{v}"], ac.next(f"fs_out{v}", 16))
                    else:
                        eng.wait_ge(S["yg_ready"], ac.next("yg_ready"))
                    act(halves(tbuf[:, v % 2, :]), pair(r), ACT.Silu).then_inc(S["act"], ac.up("act"))
                    eng.wait_ge(S[ac.last], ac.ended())
                    eng.sem_inc(S[f"acc_free{r}"], ac.told(f"acc_free{r}"))
                    eng.sem_inc(S["g_in"], ac.told("g_in"))
                    if v == 0:
                        root()
                    if v == 1:
                        split_hi()
                        y_high(0)
                        y_high(1)
                    if v >= 2:
                        y_high(v)
                split_hi()
                eng.wait_ge(S["yg_ready"], ac.next("yg_ready", 2))
                for j in range(2):
                    pass_tiles(4)
                    split_hi()
            ffn(1)
            root()

        @block.vector
        def _(eng):
            v = Line(eng, "dve")
            tt, ts, st3 = eng.tensor_tensor, eng.tensor_scalar, eng.scalar_tensor_tensor
            job, tile = [0], [0]

            def split_lo():
                s = job[0] % 2
                job[0] += 1
                eng.wait_ge(S[f"w_hi{s}"], v.next(f"w_hi{s}"))
                tt(w_lo[s][:, :], raw[s][:, :], w_hi[s][:, :].bitcast(f32), ALU.subtract).then_inc(S[f"w_lo{s}"], v.up(f"w_lo{s}"))

            def pass_tiles(n):
                for _ in range(n):
                    v.skip(f"acc_ready{tile[0] % 2}")
                    tile[0] += 1

            def tile_of():
                r = tile[0] % 2
                tile[0] += 1
                eng.wait_ge(S[f"acc_ready{r}"], v.next(f"acc_ready{r}"))
                return r

            def square_in(src, first):
                if first:
                    tt(sq_sum[:, :], src, src, ALU.mult).then_inc(S["dve"], v.up("dve"))
                    eng.wait_ge(S[v.last], v.ended())
                else:
                    tt(sq[:, :], src, src, ALU.mult).then_inc(S["dve"], v.up("dve"))
                    eng.wait_ge(S[v.last], v.ended())
                    tt(sq_sum[:, :], sq_sum[:, :], sq[:, :], ALU.add).then_inc(S["dve"], v.up("dve"))
                    eng.wait_ge(S[v.last], v.ended())

            def inverse_root(n, name="dve"):
                m, r, y, t, out = (stt[:, i, 0:n] for i in range(5))
                eng.wait_ge(S["root"], v.next("root"))
                eng.reciprocal(y, r).then_inc(S["dve"], v.up("dve"))
                eng.wait_ge(S[v.last], v.ended())
                tt(t, y, y, ALU.mult).then_inc(S["dve"], v.up("dve"))
                eng.wait_ge(S[v.last], v.ended())
                tt(t, t, m, ALU.mult).then_inc(S["dve"], v.up("dve"))
                eng.wait_ge(S[v.last], v.ended())
                ts(t, t, -0.5, 1.5, ALU.mult, ALU.add).then_inc(S["dve"], v.up("dve"))
                eng.wait_ge(S[v.last], v.ended())
                tt(out, y, t, ALU.mult).then_inc(S[name], v.up(name))

            def rms_to_inverse(width, before=None):
                eng.wait_ge(S[v.last], v.ended())
                eng.sem_inc(S["sq_done"], v.told("sq_done"))
                if before:
                    before()
                eng.wait_ge(S["stat"], v.next("stat"))
                ts(stt[:, 0, 0:TT], mixf[:, 0:TT], 1.0 / width, EPS, ALU.mult, ALU.add).then_inc(S["mean"], v.up("mean"))
                inverse_root(TT, "rinv")

            def rms(width):
                rms_to_inverse(width)
                eng.wait_ge(S["rb"], v.next("rb"))

            def modulate(l, m):
                def normed(k):
                    for cols, c in PARTS:
                        ins = st3(nbuf[k % 4][:, cols], xT[:, k, cols], gain[l][m][:, k, c:c + 1], rB[:, cols], ALU.mult, ALU.mult)
                    ins.then_inc(S["normed"], v.up("normed"))

                normed(0)
                for k in range(KT):
                    if k + 1 < KT:
                        if k >= 3:
                            eng.wait_ge(S["h_ready"], v.made["h_ready"] - 2)
                        normed(k + 1)
                    eng.wait_ge(S["normed"], v.made["normed"] - (k + 1 < KT))
                    eng.wait_ge(S["h_hi"], v.next("h_hi"))
                    for cols, c in PARTS:
                        ins = st3(h_lo[:, k, cols], nbuf[k % 4][:, cols], mod[l][:, SH[m] + k, c:c + 1],
                                  h_hi[:, k, cols].bitcast(f32), ALU.add, ALU.subtract)
                    ins.then_inc(S["h_ready"], v.up("h_ready"))
                eng.wait_ge(S[v.last], v.ended())

            def mods(l, a, b):
                tt(mod[l][:, a:b, :], ADA[:, l, a:b, :],
                         b_ada[:, l, a:b].unsqueeze(2).broadcast_to([P, b - a, 2]), ALU.add).then_inc(S["mod_read"], v.up("mod_read"))
                eng.wait_ge(S[v.last], v.ended())

            def gains(l, m):
                row = (NM, NF)[m][l]
                for c in range(2):
                    ins = st3(gain[l][m][:, :, c], mod[l][:, SC[m]:SC[m] + KT, c], 1.0, vec[:, row:row + KT], ALU.add, ALU.mult)
                return ins

            def into_x(l, m, d, squares=True):
                r = tile_of()
                for b, src, dst, c in SEGS:
                    ins = st3(xT[:, d, dst], acc[:, 2 * r + b, src], mod[l][:, GA[m] + d, c:c + 1], xT[:, d, dst], ALU.mult, ALU.add)
                ins.then_inc(S["dve"], v.up("dve"))
                eng.wait_ge(S[v.last], v.ended())
                eng.sem_inc(S[f"acc_free{r}"], v.told(f"acc_free{r}"))
                eng.wait_ge(S[v.last], v.ended())
                if squares:
                    square_in(xT[:, d, :], d == 0)

            eng.wait_ge(S["vec_T"], v.next("vec_T"))
            eng.tensor_copy(b_ada[:, :, :].rearrange("p l j -> p (l j)"), mix[:, 0, 0:96])
            eng.tensor_copy(vec[:, :], mix[:, 0, 96:96 + N_ROWS]).then_inc(S["vec_read"], v.up("vec_read"))
            for n in range(2 * TT):
                t, half = divmod(n, 2)
                eng.wait_ge(S["x_T"], v.next("x_T"))
                eng.tensor_copy(xT[:, half * 4:half * 4 + 4, tok(t)], acc[:, n % 2, :].rearrange("p (k n) -> p k n", k=4)).then_inc(S["x_T_read"], v.up("x_T_read"))
            eng.wait_ge(S[v.last], v.ended())
            for k in range(KT):
                square_in(xT[:, k, :], k == 0)
            split_lo()
            split_lo()
            eng.wait_ge(S["ada_turned"], v.next("ada_turned", 8))
            mods(0, 0, 16)
            gains(0, 0).then_inc(S["gain_ready"], v.up("gain_ready"))
            rms(D)
            modulate(0, 0)
            eng.wait_ge(S["dtw_hi"], v.next("dtw_hi"))
            tt(dtw_lo[:, :, :], dtw[:, :, :], dtw_hi[:, :, :].bitcast(f32), ALU.subtract).then_inc(S["dtw_lo"], v.up("dtw_lo"))
            heads = lambda a: a.rearrange("p (h d) -> p h d", d=HD)
            for j in range(8):
                pass_tiles((TT, TT, TT, 2, 2, 3, 2, 2)[j])
                if j < 6:
                    split_lo()
                if j == 2:
                    eng.wait_ge(S["qkv_in"], v.next("qkv_in"))
                    for t in range(TT):
                        tt(sq[:, :], qkv[:, t, 0:N], qkv[:, t, 0:N], ALU.mult).then_inc(S["dve"], v.up("dve"))
                        eng.wait_ge(S[v.last], v.ended())
                        eng.tensor_reduce(stt[:, 3, t * 10:(t + 1) * 10], heads(sq[:, :]), X, ALU.add).then_inc(S["dve"], v.up("dve"))
                        eng.wait_ge(S[v.last], v.ended())
                    ts(stt[:, 0, :], stt[:, 3, :], 1.0 / HD, EPS, ALU.mult, ALU.add).then_inc(S["mean"], v.up("mean"))
                    inverse_root(TT * 10)
                    eng.wait_ge(S[v.last], v.ended())
                    for t in range(TT):
                        x = heads(qkv[:, t, 0:N])
                        tt(x, x, stt[:, 4, t * 10:(t + 1) * 10].unsqueeze(2).broadcast_to([P, 10, HD]), ALU.mult).then_inc(S["dve"], v.up("dve"))
                        eng.wait_ge(S[v.last], v.ended())
                        tt(x[:, 0:NH, :], x[:, 0:NH, :], qk_g[:, 0, :].unsqueeze(1).broadcast_to([P, NH, HD]), ALU.mult)
                        ins = tt(x[:, NH:, :], x[:, NH:, :], qk_g[:, 1, :].unsqueeze(1).broadcast_to([P, NKV, HD]), ALU.mult)
                        ins.then_inc(S["new_kv" if t == 0 else "dve"], v.up("new_kv" if t == 0 else "dve"))
                        eng.wait_ge(S[v.last], v.ended())
                        if t:
                            a, b = x[:, :, 0:32], x[:, :, 32:HD]
                            co, si = (c[:, t - 1, :].unsqueeze(1).broadcast_to([P, 10, 32]) for c in (cosA, sinA))
                            r = [tbuf[:, i // 2, (i % 2) * 320:(i % 2 + 1) * 320].rearrange("p (h d) -> p h d", d=32) for i in range(4)]
                            for o, p_, q_ in zip(r, (a, b, b, a), (co, si, co, si)):
                                ins = tt(o, p_, q_, ALU.mult)
                            ins.then_inc(S["dve"], v.up("dve"))
                            eng.wait_ge(S[v.last], v.ended())
                            tt(a, r[0], r[1], ALU.subtract)
                            ins = tt(b, r[2], r[3], ALU.add)
                            ins.then_inc(S["roped" if t == TT - 1 else "dve"], v.up("roped" if t == TT - 1 else "dve"))
                            eng.wait_ge(S[v.last], v.ended())
                if 3 <= j < 6:
                    i, n = 2 * (j - 3), PADDED - 4
                    if j == 3:
                        eng.wait_ge(S["pads"], v.next("pads"))
                    else:
                        eng.wait_ge(S["conv_raw"], j - 3)
                    eng.wait_ge(S["xb_in"], v.next("xb_in", 2))
                    for k in range(TAPS):
                        for i_ in (i, i + 1):
                            tap = vec[:, CONV_W + k * XBC_T + i_:CONV_W + k * XBC_T + i_ + 1]
                            if k == 0:
                                ins = ts(conv[:, i_, 0:n], xpad[:, i_, 0:n], tap, None, ALU.mult)
                            else:
                                if i_ == i:
                                    eng.wait_ge(S[v.last], v.ended())
                                ins = st3(conv[:, i_, 0:n], xpad[:, i_, k:k + n], tap, conv[:, i_, 0:n], ALU.mult, ALU.add)
                        ins.then_inc(S["dve" if k < TAPS - 1 else "conv_raw"], v.up("dve" if k < TAPS - 1 else "conv_raw"))
                if j == 5:
                    eng.wait_ge(S["dt_in"], v.next("dt_in"))
                    tt(dt_tok[:, :, :], dt_tok[:, :, :], dt_c[:, 0, :].unsqueeze(1).broadcast_to([P, TT, DTS]), ALU.add).then_inc(S["dve"], v.up("dve"))
                    eng.wait_ge(S[v.last], v.ended())
                    st3(dt_t[1][:, :, :], dt_tok[:, :, :], -1.0, dt_tok[:, :, :], ALU.mult, ALU.max).then_inc(S["dt_abs"], v.up("dt_abs"))
                    eng.wait_ge(S[v.last], v.ended())
                    ts(dt_tok[:, :, :], dt_tok[:, :, :], 0.0, None, ALU.max).then_inc(S["dve"], v.up("dve"))
            eng.wait_ge(S["dt_exp"], v.next("dt_exp"))
            e, u, c = (t[:, :, :] for t in (dt_t[1], dt_t[0], dt_t[2]))
            ts(u, e, 1.0, None, ALU.add).then_inc(S["dt_u"], v.up("dt_u"))
            eng.wait_ge(S[v.last], v.ended())
            ts(c, u, -1.0, None, ALU.add).then_inc(S["dve"], v.up("dve"))
            eng.wait_ge(S[v.last], v.ended())
            tt(c, e, c, ALU.subtract).then_inc(S["dve"], v.up("dve"))
            eng.wait_ge(S[v.last], v.ended())
            eng.reciprocal(e, u).then_inc(S["dve"], v.up("dve"))
            eng.wait_ge(S[v.last], v.ended())
            tt(c, c, e, ALU.mult).then_inc(S["dve"], v.up("dve"))
            eng.wait_ge(S[v.last], v.ended())
            eng.wait_ge(S["dt_ln"], v.next("dt_ln"))
            tt(dt_tok[:, :, :], dt_tok[:, :, :], c, ALU.add).then_inc(S["dve"], v.up("dve"))
            eng.wait_ge(S[v.last], v.ended())
            tt(dt_tok[:, :, :], dt_tok[:, :, :], dt_t[3][:, :, :], ALU.add).then_inc(S["dve"], v.up("dve"))
            eng.wait_ge(S[v.last], v.ended())
            tt(a_tok[:, :, :], dt_tok[:, :, :], dt_c[:, 1, :].unsqueeze(1).broadcast_to([P, TT, DTS]), ALU.mult).then_inc(S["dve"], v.up("dve"))
            eng.wait_ge(S[v.last], v.ended())
            ts(a_tok[:, :, :], a_tok[:, :, :], -1.0, None, ALU.mult).then_inc(S["a_ready"], v.up("a_ready"))
            U = len(units)
            for i in range(U + 2):
                if i < U:
                    t, h = units[i]
                    n = N_CTX if t == 0 else N
                    eng.wait_ge(S["scores"], v.next("scores"))
                    if v.due("exp_done", 4):
                        eng.wait_ge(S["exp_done"], v.now("exp_done", 4))
                    eng.tensor_reduce(nmax[:, i % 4:i % 4 + 1], mixf[:, 1024 * (i % 2):1024 * (i % 2) + n], X, ALU.max).then_inc(S["dve"], v.up("dve"))
                    eng.wait_ge(S[v.last], v.ended())
                    ts(nmax[:, i % 4:i % 4 + 1], nmax[:, i % 4:i % 4 + 1], -ATT_SCALE, None, ALU.mult).then_inc(S["max_ready"], v.up("max_ready"))
                if 1 <= i <= U:
                    t, h = units[i - 1]
                    n = N_CTX if t == 0 else N
                    b = (i - 1) % 2
                    eng.wait_ge(S["pT_made"], v.next("pT_made"))
                    if v.due("att_made", 2):
                        eng.wait_ge(S["att_made"], v.now("att_made", 2))
                    eng.tensor_copy(pT[:, b, 0:n], accf[:, 1024 * b:1024 * b + n]).then_inc(S["pT_sb"], v.up("pT_sb"))
                if i >= 2:
                    t, h = units[i - 2]
                    u, b = i - 2, i % 2
                    eng.reciprocal(rrec[:, u % 4:u % 4 + 1], rsum[:, u % 4:u % 4 + 1]).then_inc(S["dve"], v.up("dve"))
                    eng.wait_ge(S[v.last], v.ended())
                    eng.wait_ge(S["att_made"], u + 1)
                    ts(att_tok[:, t, h * HD:(h + 1) * HD], accf[:, 1024 * b + 768:1024 * b + 768 + HD],
                             rrec[:, u % 4:u % 4 + 1], None, ALU.mult).then_inc(S["att_read"], v.up("att_read"))
            eng.wait_ge(S["kv_gone"], 1)
            eng.wait_ge(S["cum_made"], v.next("cum_made"))
            both = mixf[:, 0:TT * DTS].rearrange("p (t c) -> p t c", c=DTS)
            eng.tensor_copy(cum[:, :, :], both)
            ts(ncum[:, :, :], both, -1.0, None, ALU.mult).then_inc(S["cum_read"], v.up("cum_read"))
            eng.wait_ge(S[v.last], v.ended())
            for t in range(TT):
                eng.wait_ge(S["xt_made"], v.next("xt_made"))
                eng.tensor_copy(x_tok[:, t, :], acc[:, t % 2, :]).then_inc(S["xt_read"], v.up("xt_read"))
            eng.wait_ge(S["bt_made"], v.next("bt_made"))
            eng.tensor_copy(b_tok[:, :], acc[:, 2, 0:P]).then_inc(S["bt_read"], v.up("bt_read"))
            for g in range(2):
                for J in range(LT + 1):
                    n = g * (LT + 1) + J
                    eng.wait_ge(S["cb_made"], v.next("cb_made"))
                    if J < LT:
                        eng.tensor_copy(Gt[g][:, J * N_LAT:(J + 1) * N_LAT], mix[:, 1 + n % 2, :]).then_inc(S["cb_read"], v.up("cb_read"))
                    else:
                        eng.tensor_copy(Gp[:, g, :], mix[:, 1 + n % 2, 0:P]).then_inc(S["cb_read"], v.up("cb_read"))
            eng.wait_ge(S["conv_ready"], v.next("conv_ready"))
            f, w = (lambda h, t: ncum[:, t, h:h + 1]), (lambda h, t: dt_tok[:, t, h:h + 1])

            def y_in(h):
                eng.wait_ge(S["y_made"], v.next("y_made"))
                eng.tensor_copy(y_tok[:, :, h * HD:(h + 1) * HD], mix[:, h % 2, 0:TT * HD].rearrange("p (t d) -> p t d", d=HD)).then_inc(S["y_read"], v.up("y_read"))

            for h in range(NH):
                g = h // 4
                eng.wait_ge(S["rows_made"], v.next("rows_made"))
                dg = dgs[h % 2]
                if h:
                    eng.wait_ge(S["m_ready"], h)
                if h % 4 == 0:
                    for b in range(2):
                        ins = eng.tensor_copy(ct2[HD * b:HD * b + HD, :], conv[HD * g:HD * g + HD, ST + 1, LAT])
                    ins.then_inc(S["dve"], v.up("dve"))
                eng.tensor_copy(tot[:, h:h + 1], accf[:, P - 1:P])
                eng.tensor_copy(tot[:, NH + h:NH + h + 1], accf[:, 1024:1025]).then_inc(S["dve"], v.up("dve"))
                for t in range(TT):
                    ins = ts(dm[:, t, :], accf[:, 1024 + t * P:1024 + (t + 1) * P], f(NH + h, t), None, ALU.add)
                ins.then_inc(S["dve"], v.up("dve"))
                eng.wait_ge(S[v.last], v.ended())
                for t in range(TT):
                    ins = st3(dg[:, t, :], accf[:, t * P:(t + 1) * P], f(h, t), dm[:, t, :], ALU.add, ALU.min)
                ins.then_inc(S["arg_ready"], v.up("arg_ready"))
                eng.wait_ge(S[v.last], v.ended())
                for t in range(TT):
                    ins = ts(dm[:, t, :], upto[:, :], w(h, t), None, ALU.mult)
                ins.then_inc(S["dve"], v.up("dve"))
                eng.wait_ge(S[v.last], v.ended())
                for t in range(TT):
                    ins = st3(dm[:, t, :], onward[:, :], w(NH + h, t), dm[:, t, :], ALU.mult, ALU.add)
                ins.then_inc(S["dve"], v.up("dve"))
                eng.wait_ge(S[v.last], v.ended())
                diag = Gt[g][:, :].rearrange("p (j c) -> p j c", j=LT)[:, :, 0:P]
                tt(dm[:, 0, :], dm[:, 0, :], Gp[:, g, :], ALU.mult)
                tt(dm[:, 1:, :], dm[:, 1:, :], diag, ALU.mult).then_inc(S["dve"], v.up("dve"))
                eng.wait_ge(S[v.last], v.ended())
                eng.wait_ge(S["diag_exp"], v.next("diag_exp"))
                tt(dg, dg, dm, ALU.mult).then_inc(S["dve"], v.up("dve"))
                if h:
                    y_in(h - 1)
                eng.wait_ge(S["rows_read"], v.next("rows_read"))
                eng.wait_ge(S["dve"], v.made["dve"])
                for J in range(LT):
                    if J < LT - 1:
                        c = slice((J + 1) * P, N_LAT)
                        st3(M_off[:, J, c], E_off[:, J, c], w(h, J + 1), Gt[g][:, J * N_LAT + c.start:J * N_LAT + c.stop], ALU.mult, ALU.mult)
                    if J:
                        c = slice(0, J * P)
                        st3(M_off[:, J, c], E_off[:, J, c], w(NH + h, J + 1), Gt[g][:, J * N_LAT:J * N_LAT + c.stop], ALU.mult, ALU.mult)
                tt(ce[:, :], ecum[:, :], ct2[:, :], ALU.mult).then_inc(S["m_ready"], v.up("m_ready"))
            y_in(NH - 1)
            tt(wst[:, :], tot[:, :], ncum[:, 0, :], ALU.add).then_inc(S["wst_arg"], v.up("wst_arg"))
            eng.wait_ge(S["wst_exp"], v.next("wst_exp"))
            tt(wst[:, :], wst[:, :], dt_tok[:, 0, :], ALU.mult).then_inc(S["dve"], v.up("dve"))
            eng.wait_ge(S[v.last], v.ended())
            for h in range(NH):
                g = h // 4
                if v.due("fs_made", 2):
                    eng.wait_ge(S["fs_made"], v.now("fs_made", 2))
                for b in range(2):
                    ins = ts(bw[:, h % 2, b * HD:(b + 1) * HD], b_tok[:, g * HD:(g + 1) * HD], wst[:, b * NH + h:b * NH + h + 1], None, ALU.mult)
                ins.then_inc(S["bw_ready"], v.up("bw_ready"))
            eng.wait_ge(S["fs_made"], NH)
            eng.tensor_copy(s_out[:, :, :].rearrange("p h d -> p (h d)"), mix[:, 2, :]).then_inc(S["s_out_ready"], v.up("s_out_ready"))
            eng.wait_ge(S["ada_turned"], v.next("ada_turned", 16))
            mods(0, 16, 48)
            gains(0, 1).then_inc(S["gain_ready"], v.up("gain_ready"))
            split_lo()
            split_lo()
            for t in range(TT):
                eng.wait_ge(S["aT_made"], v.next("aT_made"))
                eng.wait_ge(S["h_hi"], v.next("h_hi"))
                tt(h_lo[:, 0:ST, tok(t)], acc[:, 2 + t % 2, :].rearrange("p (j n) -> p j n", j=4), h_hi[:, 0:ST, tok(t)].bitcast(f32), ALU.subtract).then_inc(S["aT_read"], v.up("aT_read"))
            eng.wait_ge(S[v.last], v.ended())
            eng.sem_inc(S["h_ready"], v.told("h_ready"))
            for t in range(TT):
                eng.wait_ge(S["yT_made"], v.next("yT_made"))
                for j in range(ST):
                    ins = st3(conv[:, j, pad(t)], conv[:, j, pad(t)], d_skip[:, j:j + 1], acc[:, t % 2, j * P:(j + 1) * P], ALU.mult, ALU.add)
                ins.then_inc(S["yT_read"], v.up("yT_read"))
            eng.wait_ge(S[v.last], v.ended())
            for j in range(ST):
                tt(zT[:, j, 0:N_CTX], zT[:, j, 0:N_CTX], conv[:, j, 0:N_CTX], ALU.mult)
                tt(zT[:, j, N_CTX:], zT[:, j, N_CTX:], conv[:, j, LAT], ALU.mult).then_inc(S["dve"], v.up("dve"))
                eng.wait_ge(S[v.last], v.ended())
                square_in(zT[:, j, :], j == 0)
                into_x(0, 0, j, squares=False)
            split_lo()
            rms_to_inverse(SSD_W, before=lambda: [into_x(0, 0, d, squares=False) for d in (ST, ST + 1)])
            into_x(0, 0, ST + 2, squares=False)
            into_x(0, 0, ST + 3, squares=False)
            eng.wait_ge(S["rb"], v.next("rb"))
            for j in range(ST):
                st3(h32[:, :], zT[:, j, :], vec[:, SSD_G + j:SSD_G + j + 1], rB, ALU.mult, ALU.mult).then_inc(S["y32_ready"], v.up("y32_ready"))
                eng.wait_ge(S[v.last], v.ended())
                eng.wait_ge(S["h_hi"], v.next("h_hi"))
                tt(h_lo[:, ST + j, :], h32[:, :], h_hi[:, ST + j, :].bitcast(f32), ALU.subtract).then_inc(S["h_ready"], v.up("h_ready"))
                eng.wait_ge(S[v.last], v.ended())
            eng.sem_inc(S["l0_mixed"], v.told("l0_mixed"))
            split_lo()
            for d in range(KT):
                into_x(0, 0, d)
                if d % 4 == 3:
                    split_lo()

            def ffn(l):
                rms(D)
                modulate(l, 1)
                for f0, nf in CHUNKS:
                    per = {"acc_ready0": 2, "acc_ready1": 2, "acc_free1": 2, "silu_ready": 2, "gu32_ready": 2, "gu_hi": 2,
                           "gu_ready": 2, "w_hi0": 1, "w_hi1": 1, "w_lo0": 1, "w_lo1": 1, "dve": 2}
                    with v.loop(nf // 2, per) as i:
                        for s in range(2):
                            pass_tiles(1)
                            eng.wait_ge(S["silu_ready"], v.next("silu_ready"))
                            r = tile_of()
                            tt(halves(gu32[:, :]), halves(silu_g[:, :]), pair(r), ALU.mult).then_inc(S["dve"], v.up("dve"))
                            eng.wait_ge(S[v.last], v.ended())
                            eng.sem_inc(S[f"acc_free{r}"], v.told(f"acc_free{r}"))
                            eng.wait_ge(S[v.last], v.ended())
                            eng.sem_inc(S["gu32_ready"], v.told("gu32_ready"))
                            split_lo()
                            eng.wait_ge(S["gu_hi"], v.next("gu_hi"))
                            f_ = bass.ds(i * 2 + s, 1)
                            one = lambda a: a[:, f_, :].rearrange("p o n -> p (o n)")
                            tt(one(gu_lo), gu32[:, :], one(gu_hi).bitcast(f32), ALU.subtract).then_inc(S["gu_ready"], v.up("gu_ready"))
                            eng.wait_ge(S[v.last], v.ended())
                    for j in range(4):
                        for c in range(2):
                            into_x(l, 1, 2 * j + c)
                        if not (l == 1 and f0 == CHUNKS[-1][0] and j >= 2):
                            split_lo()

            ffn(0)
            eng.wait_ge(S[v.last], v.ended())
            eng.sem_inc(S["ffn_over"], v.told("ffn_over"))
            eng.wait_ge(S["ada_turned"], v.next("ada_turned", 24))
            mods(1, 0, 48)
            gains(1, 0)
            gains(1, 1).then_inc(S["gain_ready"], v.up("gain_ready"))
            rms(D)
            modulate(1, 0)
            eng.wait_ge(S["l1_in"], v.next("l1_in", 16 * 5))
            eng.wait_ge(S[v.last], v.ended())
            eng.sem_inc(S["head_used"], v.told("head_used"))
            per = {"acc_ready0": 13, "acc_ready1": 13, "acc_free0": 4, "acc_free1": 4, "w_hi0": 4, "w_hi1": 4, "w_lo0": 4, "w_lo1": 4,
                   "head_in": 128, "decay_exp": 1, "arg1_ready": 1, "strip_exp": 1, "grow_ready": 2, "grow_used": 2, "wcol_ready": 1,
                   "qk_in": 1, "rope_done": 1, "kp_made": 1, "kw_ready": 1, "score_made": 5, "sc_ready": 5, "y_part": 5,
                   "qg_ready": 2, "state_done": 2, "yr_read": 1,
                   "sq_done": 1, "stat": 1, "mean": 1, "root": 1, "rinv": 1, "rb": 1,
                   "g_in": 4, "z32_ready": 4, "yg_hi": 4, "yg_ready": 4, "head_used": 1}
            own = [0]
            DVE_PER = 45
            per["dve"] = DVE_PER
            flat = lambda a: a.rearrange("p a n -> p (a n)")
            with v.loop(RH, per):
                eng.wait_ge(S["head_in"], v.next("head_in", 128))
                eng.wait_ge(S["decay_exp"], v.next("decay_exp"))
                ts(acol[:, :], acol[:, :], -1.0, None, ALU.mult).then_inc(S["dve"], v.up("dve"))
                eng.wait_ge(S[v.last], v.ended())
                tmp = flat(sc_sb[:, :, :])[:, 0:STRIP]
                ts(tmp, strip[:, :], 0.0, acol[:, 0:1], ALU.max, ALU.mult).then_inc(S["dve"], v.up("dve"))
                eng.wait_ge(S[v.last], v.ended())
                ts(strip[:, :], strip[:, :], -1.0, 0.0, ALU.mult, ALU.max).then_inc(S["dve"], v.up("dve"))
                eng.wait_ge(S[v.last], v.ended())
                st3(strip[:, :], strip[:, :], acol[:, 1:2], tmp, ALU.mult, ALU.add).then_inc(S["arg1_ready"], v.up("arg1_ready"))
                for j in range(2):
                    pass_tiles(2)
                    split_lo()
                eng.wait_ge(S["qk_in"], v.next("qk_in"))
                for m in range(2):
                    a, b = qk[:, 2 * m, N_CTX:], qk[:, 2 * m + 1, N_CTX:]
                    r = [tbuf[:, 0, 0:N_LAT], tbuf[:, 1, 0:N_LAT], h32[:, 0:N_LAT], sq[:, 0:N_LAT]]
                    for o, p_, q_ in zip(r, (a, b, b, a), (cosR, sinR, cosR, sinR)):
                        ins = tt(o, p_, q_[:, :], ALU.mult)
                    ins.then_inc(S["dve"], v.up("dve"))
                    eng.wait_ge(S[v.last], v.ended())
                    tt(a, r[0], r[1], ALU.subtract)
                    tt(b, r[2], r[3], ALU.add).then_inc(S["rope_done" if m else "dve"], v.up("rope_done" if m else "dve"))
                    eng.wait_ge(S[v.last], v.ended())
                eng.wait_ge(S["strip_exp"], v.next("strip_exp"))
                tt(strip[:, (LT - 1) * P:LT * P], strip[:, (LT - 1) * P:LT * P], ident[:, :], ALU.add).then_inc(S["dve"], v.up("dve"))
                eng.wait_ge(S[v.last], v.ended())

                def decayed(b):
                    eng.wait_ge(S["grow_ready"], v.next("grow_ready"))
                    ins = tt(qg[:, :, :], qk[:, 0:2, N_CTX:], grow[:, :].unsqueeze(1).broadcast_to([P, 2, N_LAT]), ALU.mult)
                    ins.then_inc(S["qg_ready"], v.up("qg_ready"))
                    eng.wait_ge(S[v.last], v.ended())
                    eng.sem_inc(S["grow_used"], v.told("grow_used"))

                decayed(0)
                for j in range(2):
                    pass_tiles(TT)
                    split_lo()
                eng.wait_ge(S["kp_made"], v.next("kp_made"))
                eng.wait_ge(S["wcol_ready"], v.next("wcol_ready"))
                for b in range(2):
                    ins = ts(kw[:, b, :], mix[:, 0, 0:DK], wcol[:, b:b + 1], None, ALU.mult)
                ins.then_inc(S["kw_ready"], v.up("kw_ready"))
                for J in range(LT + 1):
                    eng.wait_ge(S["score_made"], v.next("score_made"))
                    if J == 0:
                        eng.wait_ge(S[v.last], v.ended())
                    if 2 <= J:
                        eng.wait_ge(S["y_part"], v.next("y_part"))
                    if J < LT:
                        tt(sc_sb[:, J % 2, :], mix[:, 1 + J % 2, :], strip[:, (LT - 1 - J) * P:(LT - 1 - J) * P + N_LAT], ALU.mult).then_inc(S["sc_ready"], v.up("sc_ready"))
                    else:
                        tt(sc_p[:, :], mix[:, 1 + J % 2, 0:P], strip[:, (LT - 1) * P:LT * P], ALU.mult).then_inc(S["sc_ready"], v.up("sc_ready"))
                eng.wait_ge(S["state_done"], v.next("state_done"))
                decayed(1)
                eng.wait_ge(S["y_part"], v.next("y_part", 2))
                eng.wait_ge(S["state_done"], v.next("state_done"))
                eng.tensor_copy(yR[:, :, 0:N_CTX], mix[:, 0, :].rearrange("p (a n) -> p a n", a=VT))
                eng.tensor_copy(yR[:, :, N_CTX:], acc[:, :, :]).then_inc(S["yr_read"], v.up("yr_read"))
                eng.wait_ge(S[v.last], v.ended())
                for j in range(VT):
                    square_in(yR[:, j, :], j == 0)
                rms(DV)
                for j in range(VT):
                    st3(yR[:, j, :], yR[:, j, :], rgain[:, j:j + 1], rB, ALU.mult, ALU.mult).then_inc(S["dve"], v.up("dve"))
                    eng.wait_ge(S[v.last], v.ended())
                eng.sem_inc(S["head_used"], v.told("head_used"))
                for n in range(VT):
                    eng.wait_ge(S["g_in"], v.next("g_in"))
                    tt(h32[:, :], tbuf[:, n % 2, :], yR[:, n, :], ALU.mult).then_inc(S["z32_ready"], v.up("z32_ready"))
                    eng.wait_ge(S[v.last], v.ended())
                    eng.wait_ge(S["yg_hi"], v.next("yg_hi"))
                    tt(yg_lo[:, n, :], h32[:, :], yg_hi[:, n, :].bitcast(f32), ALU.subtract).then_inc(S["yg_ready"], v.up("yg_ready"))
                    eng.wait_ge(S[v.last], v.ended())
                    if n % 2:
                        pass_tiles(2)
                        split_lo()
                for j in range(2):
                    for c in range(4):
                        into_x(1, 0, 4 * j + c)
                    split_lo()
            ffn(1)
            rms(D)
            for k in range(KT):
                ins = st3(xT[:, k, :], xT[:, k, :], vec[:, FIN + k:FIN + k + 1], rB, ALU.mult, ALU.mult)
            ins.then_inc(S["final_ready"], v.up("final_ready"))
            for t in range(TT):
                for half in range(2):
                    eng.wait_ge(S["out_T"], v.next("out_T"))
                    eng.tensor_copy(y_out[:, t, half * 512:(half + 1) * 512], acc[:, half, :]).then_inc(S["y_ready"], v.up("y_ready"))

        @block.gpsimd
        def _(eng):
            po = Line(eng, "pool")
            tt, ts = eng.tensor_tensor, eng.tensor_scalar

            eng.wait_ge(S["x_T_read"], 2 * TT)
            for cols in (slice(0, 2), slice(2 + P, 6 + P), slice(PADDED - 2, PADDED)):
                ins = eng.memset(xpad[:, :, cols], 0.0)
            ins.then_inc(S["pads"], po.up("pads"))
            eng.wait_ge(S["ffn_over"], po.next("ffn_over"))
            for dst, src in ([(cosR[:, :], I["rope_ret"][0]), (sinR[:, :], I["rope_ret"][1]), (pcol[:, :], I["places"])]
                             + [(ramp[:, b, :], I["ramps"][b, :].partition_broadcast(P)) for b in range(2)]):
                eng.dma_start(dst, src).then_inc(S["l1_in"], po.up("l1_in", 16))
            per = {"head_used": 1, "head_in": 16 * 8, "fs_ready": 4, "fs_out0": 32, "fs_out1": 32}
            with po.loop(RH, per) as h:
                eng.wait_ge(S["head_used"], po.next("head_used"))
                eng.sem_inc(S["pool_go"], 1)
                o = bass.ds(h, 1)
                one = lambda a: a.rearrange("o p d -> p (o d)")
                eng.dma_start(strip[:, :], I["offsets"]).then_inc(S["head_in"], po.up("head_in", 16))
                eng.dma_start(rgain[:, :], I["l1_ret_gain"][bass.ds(h * DV, DV)].rearrange("(t p) -> p t", p=P),
                                     allow_slow_non_contiguous=True).then_inc(S["head_in"], po.up("head_in", 16))
                for b in range(2):
                    eng.dma_start(acol[:, b:b + 1], I["l1_decay"][b, o].partition_broadcast(P)).then_inc(S["head_in"], po.up("head_in", 16))
                    for k in range(2):
                        eng.dma_start(S0[:, b, k, :], one(I["state_ret1"][0, b, o, k * P:(k + 1) * P, :])).then_inc(S["head_in"], po.up("head_in", 16))
                for n in range(4):
                    b, k = divmod(n, 2)
                    eng.wait_ge(S["fs_ready"], po.next("fs_ready"))
                    eng.sem_inc(S["pool_go"], 1)
                    eng.dma_start(one(O[5][0, b, o, k * P:(k + 1) * P, :]), tbuf[:, n % 2, 0:DV]).then_inc(S[f"fs_out{n % 2}"], po.up(f"fs_out{n % 2}", 16))
            for b in range(2):
                eng.wait_ge(S[f"fs_out{b}"], 32 * RH)


_INS = ["x_prompt", "x_sample", "c", "cache_k0", "cache_v0", "state_ssd0", "state_ret1", "c_ctx",
        "l0_w_ada", "l0_b_ada", "l0_norm_mix", "l0_norm_ffn", "l0_w_in", "l0_w_out", "l0_q_gain", "l0_k_gain",
        "l0_conv_w", "l0_conv_b", "l0_dt_bias", "l0_a_log", "l0_d_skip", "l0_ssd_gain",
        "l0_w_gate", "l0_w_up", "l0_w_down", "l1_w_ada", "l1_b_ada", "l1_norm_mix", "l1_norm_ffn",
        "l1_w_in", "l1_w_out", "l1_decay", "l1_ret_gain", "l1_w_gate", "l1_w_up", "l1_w_down", "final_norm"]
_OUTS = [(1, N_CTX, D), (1, N_LAT, D), (1, N_CTX, NKV, HD), (1, N_CTX, NKV, HD),
         (1, 2, NH, HD, HD), (1, 2, RH, DK, DV)]


def _constants():
    import numpy as np

    i = np.arange(P)
    squares = np.stack([np.eye(P), i[:, None] <= i[None, :], i[:, None] >= i[None, :], np.ones((P, P))])
    n = np.arange(N_LAT)
    row, col = (n // GRID_W).astype(np.float32), (n % GRID_W).astype(np.float32)

    def rope(dim):
        f = dim // 4
        inv = np.float32(10000.0) ** (-np.arange(f, dtype=np.float32) / np.float32(f))
        ang = np.concatenate([row[:, None] * inv, col[:, None] * inv], axis=1).astype(np.float32)
        return np.stack([np.cos(ang.astype(np.float64)), np.sin(ang.astype(np.float64))])

    att = rope(HD).reshape(2, LT, P, HD // 2).transpose(0, 2, 1, 3)
    ret = rope(DK).transpose(0, 2, 1)
    offsets = (np.arange(STRIP)[None, :] - (LT - 1) * P) - i[:, None]
    ramps = np.stack([n + 1, N_LAT - n])
    places = np.stack([P - 1 - i, i], axis=1)
    f = lambda a: np.ascontiguousarray(a, dtype=np.float32)
    return {"squares": f(squares), "rope_att": f(att), "rope_ret": f(ret), "offsets": f(offsets),
            "ramps": f(ramps), "places": f(places)}


def kernel(**inputs):
    import numpy as _np
    import concourse.bacc as _bacc
    from concourse import mybir as _mybir
    from concourse.bass_utils import run_bass_kernel_spmd as _run

    nc = _bacc.Bacc("TRN2", target_bir_lowering=False, num_devices=1)
    arrays, ins, outs = {}, {}, []
    given = {name: _np.ascontiguousarray(inputs[name]) for name in _INS}
    for name, a in {**given, **_constants()}.items():
        arrays[f"in_{name}_dram"] = a
        ins[name] = nc.dram_tensor(f"in_{name}_dram", a.shape, _mybir.dt.from_np(a.dtype), kind="ExternalInput").ap()
    for i, shape in enumerate(_OUTS):
        outs.append(nc.dram_tensor(f"out_{i}_dram", shape, _mybir.dt.float32, kind="ExternalOutput").ap())
    trunk_kernel(nc, ins, outs)
    r = _run(nc, [arrays], core_ids=[0])
    return tuple(r.results[0][f"out_{i}_dram"] for i in range(len(_OUTS)))
```

```python
import concourse.bass as bass
from concourse import mybir
from contextlib import ExitStack, contextmanager

P = 128
D = 1024
KT = D // P
N_CTX = 128
N_LAT = 512
N = N_CTX + N_LAT
TT = N // P
GRID_W = 64
LT = N_LAT // P
HALF = N // 2
PAST = 128
EPS = 1e-6
HD = 64
NH = 8
NKV = 2
ATT_W = NH * HD
KV_W = NKV * HD
QKV_W = ATT_W + 2 * KV_W
SSD_W = NH * HD
ST = SSD_W // P
XBC_T = ST + 2
TAPS = 5
PADDED = N + 8
RH = 4
DK = 256
DV = 512
VT = DV // P
STRIP = N_LAT + (LT - 1) * P
D_FF = 2816
FT = D_FF // P
CHUNKS = [(0, 8), (8, 8), (16, 6)]
W = 256
SLOT = KT * W
OFF_Z = QKV_W
OFF_X = OFF_Z + SSD_W
OFF_DT = OFF_X + XBC_T * P
DTS = 2 * NH
ATT_SCALE = HD ** -0.5
K_SCALE = DK ** -0.5
ADA_JOBS = 6 * D // W
NM, NF, FIN, COND, CONV_B, SSD_G, CONV_W = (0, 16), (8, 24), 32, 40, 56, 62, 66
N_ROWS = 96
SH, SC, GA = (0, 24), (8, 32), (16, 40)


class Line:

    def __init__(self, eng, own):
        self.e, self.last = eng, own
        self.made, self.took, self.turn, self.per = {}, {}, None, {}

    def value(self, name, n):
        return n if self.turn is None else n + self.turn * self.per.get(name, 0)

    def up(self, name, k=1):
        self.last = name
        return self.told(name, k)

    def told(self, name, k=1):
        self.made[name] = self.made.get(name, 0) + k
        return k

    def ended(self):
        return self.value(self.last, self.made[self.last])

    def next(self, name, k=1):
        self.took[name] = self.took.get(name, 0) + k
        return self.value(name, self.took[name])

    def due(self, name, behind):
        self.next(name)
        assert self.turn is None or self.took[name] > behind, name
        return self.took[name] > behind

    def now(self, name, behind=0):
        return self.value(name, self.took[name] - behind)

    def skip(self, name, k=1):
        self.took[name] = self.took.get(name, 0) + k

    @contextmanager
    def loop(self, turns, per):
        made, took = dict(self.made), dict(self.took)
        with self.e.Fori(0, turns) as i:
            self.turn, self.per = i, per
            yield i
        self.turn = None
        for now, was in ((self.made, made), (self.took, took)):
            for name in now:
                grown = now[name] - was.get(name, 0)
                assert grown in (0, per.get(name, 0)), (name, grown, per)
                now[name] += grown * (turns - 1)


SIGNALS = {
    "sp act dve": "the engine's last instruction has ended",
    "pool_go": "nothing: GpSimd's place to wait at before a transfer",
    "squares_in setup_in x_in": "identity, triangles and ones; the small vectors; x",
    "first_in0 first_in1 first_in2 first_in3 first_in4 first_in5 first_in6 first_in7": "a panel of the first modulation",
    "raw_in0 raw_in1 ada_in0 ada_in1": "a panel of weights, of modulation weights, in slot {}",
    "l0_in l1_in head_in": "what a mixer needs beside its weights: layer 0's, layer 1's, a head's of layer 1",
    "w_hi0 w_hi1 w_lo0 w_lo1": "slot {}'s panel has its high, its low part",
    "ada_hi ada_lo dtw_hi dtw_lo sc_hi": "the same of a modulation's panel, of dt's weights, of the conditions",
    "acc_ready0 acc_ready1": "a product's tile stands in pair {} of banks",
    "acc_free0 acc_free1": "that tile is read",
    "vec_T vec_read cond": "small vectors turned, copied; SiLU of the conditions",
    "ada_used row_in ada_turned mod_read gain_ready": "a panel multiplied, its rows copied, turned to columns; columns read; gains made",
    "sq_done stat mean root": "squares added over tiles, over partitions (on TensorE), their mean, its root",
    "rinv rb": "1/rms of each token, on every partition",
    "normed h_hi h_ready": "a tile normed and scaled, its high part, its low part",
    "x_T x_T_read pads": "x turned, copied; the zeros around the convolved rows",
    "qkv_in xb_in conv_raw conv_ready": "q, k and v off the banks; a tile of x|B|C; two convolved; SiLU of all",
    "dt_rows dt_turned dt_in dt_abs dt_exp dt_u dt_ln": "dt feature-major, token-major, copied; the steps of its softplus",
    "roped new_kv kv_out kv_gone": "q and k ready; the prompt's ready, on their way, in DRAM",
    "kT_made qT_made qT_sb": "k, q turned; q copied",
    "scores max_ready exp_done": "a unit's scores, their maximum, their exponentials",
    "pT_made pT_sb att_made att_read": "probabilities turned, copied; output made, read",
    "a_ready cum_made cum_read": "log decays; their running sums made, copied",
    "xt_made xt_read bt_made bt_read cb_made cb_read": "x, B token-major and C.B, made and copied",
    "rows_made arg_ready diag_exp rows_read": "a head's sums along the tokens; the diagonal's exponents, exponentials; sums used",
    "m_ready y_made y_read": "a head's decayed C.B; its y made, copied",
    "wst_arg wst_exp bw_ready fs_made s_out_ready": "the steps of the prompt's final states",
    "aT_made aT_read y32_ready l0_mixed": "attention's output turned, read; y normed; all split",
    "silu_ready gu32_ready gu_hi gu_ready ffn_over": "SiLU(gate), its product with up, that one's parts; the FFN's buffers free",
    "head_used decay_exp arg1_ready strip_exp": "a head's small inputs used; decay rates, the strip's exponents and exponentials",
    "grow_ready grow_used wcol_ready": "decays along the tokens made, used; those of the prompt's keys",
    "qk_in rope_done v_in kp_made kw_ready": "q and k off the banks, rotated; v; the prompt's k turned, decayed",
    "score_made sc_ready y_part qg_ready state_done": "scores made, decayed, used; q decayed, times the cached state",
    "state_made fs_ready fs_out0 fs_out1": "a final state made, copied, in DRAM",
    "yr_read g_in z32_ready yg_hi yg_ready": "y copied; SiLU(g); their product and its parts",
    "final_ready out_T y_by_act y_by_dve": "half of the features normed; a piece turned, copied by ScalarE, by VectorE",
    "out": "a result is in DRAM",
}


class Floor:

    def __init__(self, nc):
        self.nc, self.at, self.top = nc, (nc.sbuf_base + 31) // 32 * 32, nc.sbuf_usable_end

    def __call__(self, name, shape, dt=mybir.dt.float32):
        size = 4
        for n in shape[1:]:
            size *= n
        t = self.nc.alloc_sbuf_tensor_at(name, shape, dt, offset=self.at)
        self.at += (size + 31) // 32 * 32
        assert self.at <= self.top, (name, self.at, self.top)
        return t


def trunk_kernel(nc, I, O):
    f32, f32r = mybir.dt.float32, mybir.dt.float32r
    ALU, ACT = mybir.AluOpType, mybir.ActivationFunctionType
    X = mybir.AxisListType.X
    ctx = ExitStack()
    with ctx:
        sb = Floor(nc)
        xT = sb("xT", [P, KT, N])
        h_at = sb.at
        h_hi, h_lo = sb("h_hi", [P, KT, N], f32r), sb("h_lo", [P, KT, N], f32r)
        h_end = sb.at
        raw = [sb(f"raw{s}", [P, SLOT]) for s in range(2)]
        w_hi = [sb(f"w_hi{s}", [P, SLOT], f32r) for s in range(2)]
        w_lo = [sb(f"w_lo{s}", [P, SLOT], f32r) for s in range(2)]
        squares = sb("squares", [P, 4, P])
        ident, upto, onward, ones = (squares[:, n, :] for n in range(4))
        b_ada = sb("b_ada", [P, 2, 48])
        vec = sb("vec", [P, N_ROWS])
        scond = sb("scond", [P, KT, 2])
        mod = [sb(f"mod{l}", [P, 48, 2]) for l in range(2)]
        ada_row = sb("ada_row", [4, W])
        sc4 = sb("sc4", [P, KT, 4], f32r)
        fold = sb("fold", [4, 2])
        gain = [[sb(f"gain{l}{m}", [P, KT, 2]) for m in range(2)] for l in range(2)]
        sq, sq_sum = sb("sq", [P, N]), sb("sq_sum", [P, N])
        stt = sb("stt", [P, 5, TT * 10])
        tbuf = sb("tbuf", [P, 2, N])
        h32 = sb("h32", [P, N])
        nbuf = (tbuf[:, 0, :], tbuf[:, 1, :], h32, sq)
        phase_at = sb.at

        ada_raw = [sb(f"ada_raw{s}", [P, SLOT]) for s in range(2)]
        part_at = sb.at
        x_stage = sb("x_stage", [P, TT, D])
        stg_a, stg_b = sb("stg_a", [96, P]), sb("stg_b", [N_ROWS, P])
        sb.at = part_at
        conv = sb("conv", [P, XBC_T, PADDED])
        sb.at = part_at + 2 * 4 * PADDED
        xpad = sb("xpad", [P, XBC_T, PADDED])
        att_tok = sb("att_tok", [P, TT, ATT_W])
        dt_tok, a_tok = sb("dt_tok", [P, TT, DTS]), sb("a_tok", [P, TT, DTS])
        dt_t = [h32[:, i * TT * DTS:(i + 1) * TT * DTS].rearrange("p (t c) -> p t c", c=DTS) for i in range(4)]
        dtT = sq[0:DTS, :]
        y_buf = (h32[:, :], sq[:, :])
        dt_c = sb("dt_c", [P, 2, DTS])
        d_skip = sb("d_skip", [P, ST])
        dtw = sb("dtw", [P, KT, DTS])
        dtw_hi, dtw_lo = sb("dtw_hi", [P, KT, DTS], f32r), sb("dtw_lo", [P, KT, DTS], f32r)
        zT = sb("zT", [P, ST, N])
        kc, vc = sb("kc", [P, KV_W]), sb("vc", [P, KV_W])
        qk_g = sb("qk_g", [P, 2, HD])
        cosA, sinA = sb("cosA", [P, LT, 32]), sb("sinA", [P, LT, 32])
        s0 = sb("s0", [P, NH, HD])
        qkv_at = sb.at
        qkv = sb("qkv", [P, TT, QKV_W])
        sb.at = h_at
        first_raw = [sb(f"first_raw{s}", [P, SLOT]) for s in range(5)]
        first_slots = ada_raw + first_raw + [raw[1]]
        sb.at = h_at
        qT, kT = sb("qT", [P, 4, N]), sb("kT", [P, N + PAST])
        probs, pT = sb("probs", [P, 2, N]), sb("pT", [P, 2, N])
        nmax, rsum, rrec = sb("nmax", [P, 4]), sb("rsum", [P, 4]), sb("rrec", [P, 4])
        sb.at = h_at
        G_LEN = LT * (N_LAT + P)
        Gt = [sb(f"G{g}", [P, G_LEN]) for g in range(2)]
        Gp = sb("Gp", [P, 2, P])
        x_tok = sb("x_tok", [P, TT, SSD_W])
        ecum, ce, ct2 = sb("ecum", [P, N_LAT]), sb("ce", [P, N_LAT]), sb("ct2", [P, N_LAT])
        assert sb.at <= h_end
        sb.at = qkv_at
        yT = sb("yT", [P, ST, N])
        cum, ncum = sb("cum", [P, TT, DTS]), sb("ncum", [P, TT, DTS])
        dgs = [a.rearrange("p (t n) -> p t n", t=TT) for a in (tbuf[:, 0, :], sq[:, :])]
        dm = tbuf[:, 1, :].rearrange("p (t n) -> p t n", t=TT)
        tot, wst = sb("tot", [P, DTS]), sb("wst", [P, DTS])
        b_tok = sb("b_tok", [P, 2 * HD])
        bw = sb("bw", [P, 2, 2 * HD])
        s_out = sb("s_out", [P, NH, HD])
        E_all = ada_raw[0][:, :].rearrange("p (j n) -> p j n", j=LT)
        M_all = ada_raw[1][:, :].rearrange("p (j n) -> p j n", j=LT)

        sb.at = part_at
        gu_hi, gu_lo = sb("gu_hi", [P, KT, N], f32r), sb("gu_lo", [P, KT, N], f32r)
        silu_g, gu32 = sb("silu_g", [P, N]), sb("gu32", [P, N])
        ada_hi, ada_lo = sb("ada_hi", [P, SLOT], f32r), sb("ada_lo", [P, SLOT], f32r)

        sb.at = phase_at
        S0 = sb("S0", [P, 2, 2, DV])
        qk = sb("qk", [P, 4, N])
        qg = sb("qg", [P, 2, N_LAT])
        v_tok = sb("v_tok", [P, TT, DV])
        strip = sb("strip", [P, STRIP])
        sc_sb = sb("sc_sb", [P, 2, N_LAT])
        sc_p = sb("sc_p", [P, P])
        ramp = sb("ramp", [P, 2, N_LAT])
        grow = sb("grow", [P, N_LAT])
        kw = sb("kw", [P, 2, DK])
        pcol, wcol = sb("pcol", [P, 2]), sb("wcol", [P, 2])
        acol = sb("acol", [P, 2])
        rgain = sb("rgain", [P, VT])
        cosR, sinR = sb("cosR", [P, N_LAT]), sb("sinR", [P, N_LAT])
        yg_hi, yg_lo = sb("yg_hi", [P, VT, N], f32r), sb("yg_lo", [P, VT, N], f32r)
        yR = qk

        sb.at = phase_at
        y_out = sb("y_out", [P, TT, D])

        acc = ctx.enter_context(nc.psum_tensor("acc", [P, 4, 512], f32))
        mix = ctx.enter_context(nc.psum_tensor("mix", [P, 4, 512], f32))
        accf, mixf = (t[:, :, :].rearrange("p a b -> p (a b)") for t in (acc, mix))
        ADA = mix[:, 3, 256:256 + 192].rearrange("p (l j c) -> p l j c", l=2, c=2)
        rB = mixf[:, 512:512 + N]
        ROWS = mix[0:4, 3, 0:W]
        S = {name: ctx.enter_context(nc.semaphore(name)) for names in SIGNALS for name in names.split()}
        block = ctx.enter_context(nc.Block())

        SEGS = [(0, slice(0, N_CTX), slice(0, N_CTX), 0),
                (0, slice(N_CTX, HALF), slice(N_CTX, HALF), 1),
                (1, slice(0, HALF), slice(HALF, N), 1)]
        PARTS = [(slice(0, N_CTX), 0), (slice(N_CTX, N), 1)]
        tok = lambda t: slice(t * P, (t + 1) * P)
        pad = lambda t: slice(0, P) if t == 0 else slice(4 + t * P, 4 + (t + 1) * P)
        LAT = slice(4 + P, 4 + P + N_LAT)
        pair = lambda r: acc[:, 2 * r:2 * r + 2, 0:HALF]
        halves = lambda t: t.rearrange("p (b n) -> p b n", b=2)
        units = [(t, h) for t in range(TT) for h in range(NH)]

        COPIER = ["y_by_act" if n < TT or n % 2 else "y_by_dve" for n in range(2 * TT)]
        copied = lambda n: COPIER[:n + 1].count(COPIER[n])

        @block.sync
        def _(eng):
            sp = Line(eng, "sp")
            job, ada = [0], [0]

            def kpn(w):
                return w.rearrange("(k p) n -> p k n", p=P)

            def load(dst, src, name):
                k = dst.shape[1]
                for a, b in ((0, k // 2), (k // 2, k)):
                    eng.dma_start(dst[:, a:b, :], src[:, a:b, :]).then_inc(S[name], sp.up(name, 16))

            def slot():
                s = job[0] % 2
                job[0] += 1
                if sp.due(f"w_lo{s}", 1):
                    eng.wait_ge(S[f"w_lo{s}"], sp.now(f"w_lo{s}", 1))
                return s

            def panel(src, cols=W):
                s = slot()
                k = src.shape[1]
                load(raw[s][:, 0:k * cols].rearrange("p (k n) -> p k n", n=cols), src, f"raw_in{s}")

            def gate_up(gate, up, f):
                s = slot()
                v = raw[s][:, :].rearrange("p (k n) -> p k n", n=W)
                for a, w in ((0, gate), (P, up)):
                    ins = eng.dma_start(v[:, :, a:a + P], kpn(w)[:, :, bass.ds(f, P)])
                    ins.then_inc(S[f"raw_in{s}"], sp.up(f"raw_in{s}", 16))

            def first_panel(n):
                dst = first_slots[n][:, :].rearrange("p (k n) -> p k n", n=W)
                load(dst, kpn(I["l0_w_ada"])[:, :, n * W:(n + 1) * W], f"first_in{n}")

            def ada_panel(w, n):
                s = ada[0] % 2
                ada[0] += 1
                if sp.due("ada_used", 2):
                    eng.wait_ge(S["ada_used"], sp.now("ada_used", 2))
                load(ada_raw[s][:, :].rearrange("p (k n) -> p k n", n=W), kpn(w)[:, :, bass.ds(n, W)], f"ada_in{s}")

            ins = eng.dma_start(squares[:, :, :], I["squares"].rearrange("n p m -> p n m"))
            ins.then_inc(S["squares_in"], sp.up("squares_in", 16))
            eng.dma_start(x_stage[:, 0, :], I["x_prompt"][0, :, :]).then_inc(S["x_in"], sp.up("x_in", 16))
            ins = eng.dma_start(x_stage[:, 1:TT, :], I["x_sample"][0, :, :].rearrange("(t p) d -> p t d", p=P))
            ins.then_inc(S["x_in"], sp.up("x_in", 16))
            w_in, w_ada = kpn(I["l0_w_in"]), I["l0_w_ada"]
            cols = [i * W for i in range(3)] + [OFF_X + i * W for i in range(3)] + [OFF_Z + i * W for i in range(2)]
            eng.wait_ge(S["setup_in"], 12 * 16)
            for n in range(8):
                if n == 7:
                    panel(w_in[:, :, cols[0]:cols[0] + W])
                first_panel(n)
            sp.skip("ada_used", 8)
            eng.wait_ge(S["ada_used"], 8)
            panel(w_in[:, :, cols[1]:cols[1] + W])
            eng.wait_ge(S["x_T_read"], sp.next("x_T_read", 10))

            def aside(dst, src, slow=False):
                eng.dma_start(dst, src, allow_slow_non_contiguous=slow).then_inc(S["l0_in"], sp.up("l0_in", 16))

            aside(dtw[:, :, :], w_in[:, :, OFF_DT:OFF_DT + DTS])
            aside(kc[:, :], I["cache_k0"][0].rearrange("t h d -> t (h d)"))
            aside(vc[:, :], I["cache_v0"][0].rearrange("t h d -> t (h d)"))
            aside(qk_g[:, 0, :], I["l0_q_gain"].partition_broadcast(P))
            aside(qk_g[:, 1, :], I["l0_k_gain"].partition_broadcast(P))
            aside(dt_c[:, 0, :], I["l0_dt_bias"].rearrange("a b -> (a b)").partition_broadcast(P))
            aside(dt_c[:, 1, :], I["l0_a_log"].rearrange("a b -> (a b)").partition_broadcast(P))
            for b in range(2):
                aside(d_skip[HD * b:HD * b + HD, :],
                      I["l0_d_skip"].rearrange("(t b) -> b t", b=2)[b, :].partition_broadcast(HD), True)
                aside(s0[HD * b:HD * b + HD, :, :], I["state_ssd0"][0, b].rearrange("h n d -> n h d"))
            aside(cosA[:, :, :], I["rope_att"][0])
            aside(sinA[:, :, :], I["rope_att"][1])
            for j in range(2, 8):
                panel(w_in[:, :, cols[j]:cols[j] + W])
            eng.wait_ge(S["new_kv"], sp.next("new_kv"))
            for k, src in enumerate((qkv[:, 0, ATT_W:ATT_W + KV_W], qkv[:, 0, ATT_W + KV_W:QKV_W])):
                eng.dma_start(O[2 + k][0].rearrange("t h d -> t (h d)"), src).then_inc(S["kv_out"], sp.up("kv_out", 16))
            eng.wait_ge(S[sp.last], sp.ended())
            eng.sem_inc(S["kv_gone"], sp.told("kv_gone"))
            for n in range(8, ADA_JOBS):
                s = n % 2
                if n < 10:
                    eng.wait_ge(S[f"w_lo{s}"], 4)
                else:
                    eng.wait_ge(S["ada_used"], n - 1)
                load(raw[s][:, :].rearrange("p (k n) -> p k n", n=W), kpn(w_ada)[:, :, n * W:n * W + W], f"raw_in{s}")
            sp.skip("ada_used", ADA_JOBS - 8)
            eng.wait_ge(S["ada_used"], sp.now("ada_used"))
            for a in range(2):
                for j in range(2):
                    panel(kpn(I["l0_w_out"])[:, a * ST:a * ST + ST, j * 2 * W:(j + 1) * 2 * W], 2 * W)
            eng.wait_ge(S["s_out_ready"], sp.next("s_out_ready"))
            for b in range(2):
                ins = eng.dma_start(O[4][0, b].rearrange("h n d -> n h d"), s_out[HD * b:HD * b + HD, :, :])
                ins.then_inc(S["out"], sp.up("out", 16))
            eng.wait_ge(S["l0_mixed"], sp.next("l0_mixed"))
            for n in range(2):
                ada_panel(I["l1_w_ada"], n * W)

            def ffn(l):
                gate, up, down = (I[f"l{l}_w_{n}"] for n in ("gate", "up", "down"))
                for f0, nf in CHUNKS:
                    per = {"w_lo0": 1, "w_lo1": 1, "raw_in0": 32, "raw_in1": 32}
                    if l == 0:
                        per |= {"ada_used": 2, "ada_in0": 32, "ada_in1": 32}
                    with sp.loop(nf // 2, per) as i:
                        for s in range(2):
                            gate_up(gate, up, (i * 2 + s + f0) * P)
                            if l == 0:
                                ada_panel(I["l1_w_ada"], (i * 2 + s + f0 + 2) * W)
                    for j in range(4):
                        panel(kpn(down)[:, f0:f0 + nf, j * W:j * W + W])

            ffn(0)
            w_in, w_out = kpn(I["l1_w_in"]), I["l1_w_out"]
            per = {"raw_in0": 128, "raw_in1": 128, "w_lo0": 4, "w_lo1": 4}
            with sp.loop(RH, per) as h:
                panel(w_in[:, :, bass.ds(h * DK, W)])
                panel(w_in[:, :, bass.ds(h * DK + D, W)])
                for j in range(2):
                    panel(w_in[:, :, bass.ds(h * DV + j * W + 2 * D, W)])
                for j in range(2):
                    panel(w_in[:, :, bass.ds(h * DV + j * W + 4 * D, W)])
                for j in range(2):
                    panel(w_out.rearrange("(h k p) n -> p (h k) n", p=P, k=VT)[:, bass.ds(h * VT, VT), j * 2 * W:(j + 1) * 2 * W], 2 * W)
            ffn(1)
            for n in range(2 * TT):
                half, t = divmod(n, TT)
                eng.wait_ge(S[COPIER[n]], copied(n))
                cols = slice(half * 512, (half + 1) * 512)
                dst = O[0][0, :, cols] if t == 0 else O[1][0, (t - 1) * P:t * P, cols]
                eng.dma_start(dst, y_out[:, t, cols]).then_inc(S["out"], sp.up("out", 16))
            eng.wait_ge(S[sp.last], sp.ended())
            for b in range(2):
                eng.wait_ge(S[f"fs_out{b}"], 32 * RH)

        @block.tensor
        def _(eng):
            pe = Line(eng, "pe")
            job, tile, ada = [0], [0], [0]
            mm = eng.matmul

            def next_tile():
                r = tile[0] % 2
                tile[0] += 1
                if pe.due(f"acc_free{r}", 1):
                    eng.wait_ge(S[f"acc_free{r}"], pe.now(f"acc_free{r}", 1))
                return r

            def next_job():
                s = job[0] % 2
                job[0] += 1
                eng.wait_ge(S[f"w_lo{s}"], pe.next(f"w_lo{s}"))
                return s

            def tile_a(s, xh, xl, kts, col, cols=W, came=None, h_from=None):
                r = next_tile()
                for k in range(kts):
                    if came:
                        eng.wait_ge(S[came], pe.next(came))
                    if h_from is not None:
                        eng.wait_ge(S["h_ready"], h_from + k + 1)
                    for n, (w, x) in enumerate(((w_hi[s], xh), (w_hi[s], xl), (w_lo[s], xh))):
                        for b in range(2):
                            last = mm(acc[:, 2 * r + b, 0:HALF], w[:, k * cols + col:k * cols + col + P],
                                      x[:, k, b * HALF:(b + 1) * HALF],
                                      start=(k == 0 and n == 0), stop=(k == kts - 1 and n == 2))
                last.then_inc(S[f"acc_ready{r}"], pe.up(f"acc_ready{r}"))

            def first_pair(s):
                r = [next_tile() for _ in range(2)]
                for k in range(KT):
                    eng.wait_ge(S["h_ready"], pe.next("h_ready"))
                    for c in range(2):
                        for n, (w, x) in enumerate(((w_hi[s], h_hi), (w_hi[s], h_lo), (w_lo[s], h_hi))):
                            for b in range(2):
                                last = mm(acc[:, 2 * r[c] + b, 0:HALF], w[:, k * W + c * P:k * W + (c + 1) * P],
                                          x[:, k, b * HALF:(b + 1) * HALF],
                                          start=(k == 0 and n == 0), stop=(k == KT - 1 and n == 2))
                        if k == KT - 1:
                            last.then_inc(S[f"acc_ready{r[c]}"], pe.up(f"acc_ready{r[c]}"))

            def tile_b(s, t, came=None):
                r = next_tile()
                for k in range(KT):
                    if came:
                        eng.wait_ge(S[came], pe.next(came))
                    for n, (x, w) in enumerate(((h_hi, w_hi[s]), (h_hi, w_lo[s]), (h_lo, w_hi[s]))):
                        last = mm(acc[:, 2 * r, 0:W], x[:, k, tok(t)], w[:, k * W:(k + 1) * W],
                                  start=(k == 0 and n == 0), stop=(k == KT - 1 and n == 2))
                last.then_inc(S[f"acc_ready{r}"], pe.up(f"acc_ready{r}"))

            def ada_turn(l, n, rows=2):
                eng.wait_ge(S["row_in"], pe.next("row_in"))
                for c in range(2):
                    last = mm(ADA[:, l, bass.ds(n * 2 + c, 1), :].rearrange("p o c -> p (o c)"),
                              ada_row[0:rows, c * P:(c + 1) * P], ident[0:2, 0:2] if rows == 2 else fold[:, :], start=True, stop=True)
                last.then_inc(S["ada_turned"], pe.up("ada_turned"))

            def ada_job(l, n, pending=True, first=False):
                if pending:
                    ada_turn(l, n - 1)
                if first:
                    w = first_slots[n]
                    eng.wait_ge(S[f"first_in{n}"], 32)
                elif l == 0 and n >= 8:
                    w = raw[n % 2]
                    eng.wait_ge(S[f"raw_in{n % 2}"], 32 * (4 + (n - 8) // 2 + 1))
                else:
                    s = ada[0] % 2
                    ada[0] += 1
                    w = ada_raw[s]
                    eng.wait_ge(S[f"ada_in{s}"], pe.next(f"ada_in{s}", 32))
                for k in range(KT):
                    last = mm(ROWS[0:2, :], scond[:, k, :], w[:, k * W:(k + 1) * W], start=(k == 0), stop=(k == KT - 1))
                last.then_inc(S["ada_used"], pe.up("ada_used"))

            def split_ada_job(l, n, turn_rows):
                ada_turn(l, n - 1, turn_rows)
                eng.wait_ge(S["ada_lo"], pe.next("ada_lo"))
                for k in range(KT):
                    cols = slice(k * W, (k + 1) * W)
                    mm(ROWS, sc4[:, k, :], ada_hi[:, cols], start=(k == 0), stop=False)
                    last = mm(ROWS[0:2, :], sc4[:, k, 0:2], ada_lo[:, cols], start=False, stop=(k == KT - 1))
                last.then_inc(S["ada_used"], pe.up("ada_used"))

            def rms_sum():
                eng.wait_ge(S["sq_done"], pe.next("sq_done"))
                for t in range(TT):
                    last = mm(mixf[:, t:t + 1], sq_sum[:, tok(t)], ones[:, 0:1], start=True, stop=True)
                last.then_inc(S["stat"], pe.up("stat"))

            def rms_back():
                eng.wait_ge(S["rinv"], pe.next("rinv"))
                for t in range(TT):
                    last = mm(mixf[:, 512 + t * P:512 + (t + 1) * P],
                              stt[:, 4, t:t + 1].broadcast_to([P, P]), ident[:, :], start=True, stop=True)
                last.then_inc(S["rb"], pe.up("rb"))

            def rms():
                rms_sum()
                rms_back()

            eng.wait_ge(S["squares_in"], 16)
            eng.wait_ge(S["setup_in"], 12 * 16)
            eng.transpose(mix[:, 0, 0:96], stg_a[:, :], ident[0:96, 0:96])
            ins = eng.transpose(mix[:, 0, 96:96 + N_ROWS], stg_b[:, :], ident[0:N_ROWS, 0:N_ROWS])
            ins.then_inc(S["vec_T"], pe.up("vec_T"))
            eng.wait_ge(S["x_in"], pe.next("x_in", 32))
            for n in range(2 * TT):
                t, half = divmod(n, 2)
                if pe.due("x_T_read", 2):
                    eng.wait_ge(S["x_T_read"], pe.now("x_T_read", 2))
                for k in range(4):
                    last = eng.transpose(acc[:, n % 2, k * P:(k + 1) * P],
                                         x_stage[:, t, (half * 4 + k) * P:(half * 4 + k + 1) * P], ident[:, :])
                last.then_inc(S["x_T"], pe.up("x_T"))
            eng.wait_ge(S["cond"], pe.next("cond"))
            for n in range(8):
                ada_job(0, n, n > 0, first=True)
                if n == 5:
                    rms_sum()
                if n == 6:
                    rms_back()
            ada_turn(0, 7)
            eng.wait_ge(S["mod_read"], pe.next("mod_read"))
            eng.wait_ge(S["x_T_read"], pe.now("x_T_read"))
            for j in range(8):
                s = next_job()
                for t in range(TT if j < 3 else 2):
                    if j < 3:
                        tile_b(s, t, "h_ready" if j == 0 and t == 0 else None)
                    else:
                        tile_a(s, h_hi, h_lo, KT, t * P)
                    if j == 6 and t == 0:
                        eng.wait_ge(S["dt_rows"], pe.next("dt_rows"))
                        for t_ in range(TT):
                            last = mm(mix[:, 0, t_ * DTS:(t_ + 1) * DTS], dtT[:, tok(t_)], ident[0:DTS, 0:DTS], start=True, stop=True)
                        last.then_inc(S["dt_turned"], pe.up("dt_turned"))
                if j == 5:
                    eng.wait_ge(S["dtw_lo"], pe.next("dtw_lo"))
                    r = next_tile()
                    for k in range(KT):
                        for m, (w, x) in enumerate(((dtw_hi, h_hi), (dtw_hi, h_lo), (dtw_lo, h_hi))):
                            for b in range(2):
                                last = mm(acc[0:DTS, 2 * r + b, 0:HALF], w[:, k, :], x[:, k, b * HALF:(b + 1) * HALF],
                                          start=(k == 0 and m == 0), stop=(k == KT - 1 and m == 2))
                    last.then_inc(S[f"acc_ready{r}"], pe.up(f"acc_ready{r}"))
            eng.wait_ge(S["dt_in"], pe.next("dt_in"))
            eng.wait_ge(S["acc_free0"], pe.now("acc_free0"))
            eng.wait_ge(S["acc_free1"], pe.now("acc_free1"))
            eng.wait_ge(S["l0_in"], pe.next("l0_in", 16 * 13))
            eng.wait_ge(S["roped"], pe.next("roped"))
            for t in range(TT):
                eng.transpose(accf[:, t * P:(t + 1) * P], qkv[:, t, ATT_W:ATT_W + KV_W], ident[:, :])
            eng.transpose(accf[:, N:N + PAST], kc[:, :], ident[:, :]).then_inc(S["kT_made"], pe.up("kT_made"))
            for t in range(TT):
                if pe.due("qT_sb", 2):
                    eng.wait_ge(S["qT_sb"], pe.now("qT_sb", 2))
                for j in range(4):
                    last = eng.transpose(acc[:, 2 + t % 2, j * P:(j + 1) * P], qkv[:, t, j * P:(j + 1) * P], ident[:, :])
                last.then_inc(S["qT_made"], pe.up("qT_made"))
            eng.wait_ge(S["qT_sb"], pe.now("qT_sb"))
            U = len(units)
            for i in range(U + 2):
                if i < U:
                    t, h = units[i]
                    b, g = i % 2, h // 4
                    if pe.due("exp_done", 2):
                        eng.wait_ge(S["exp_done"], pe.now("exp_done", 2))
                    q = qT[HD * g:HD * g + HD, h % 4, tok(t)]
                    spans = [(0, N_CTX, 0)] if t == 0 else [(0, 512, P), (512, P, P + 512)]
                    for at, n_, k0 in spans:
                        last = mm(mixf[:, 1024 * b + at:1024 * b + at + n_], q, kT[HD * g:HD * g + HD, k0:k0 + n_],
                                  start=True, stop=True)
                    last.then_inc(S["scores"], pe.up("scores"))
                if 1 <= i <= U:
                    t, h = units[i - 1]
                    b = (i - 1) % 2
                    eng.wait_ge(S["exp_done"], i)
                    if pe.due("att_read", 2):
                        eng.wait_ge(S["att_read"], pe.now("att_read", 2))
                    for m in range(1 if t == 0 else TT):
                        last = eng.transpose(accf[:, 1024 * b + m * P:1024 * b + (m + 1) * P],
                                             probs[:, b, m * P:(m + 1) * P], ident[:, :])
                    last.then_inc(S["pT_made"], pe.up("pT_made"))
                if i >= 2:
                    t, h = units[i - 2]
                    b, g = i % 2, h // 4
                    eng.wait_ge(S["pT_sb"], pe.next("pT_sb"))
                    vs = [qkv[:, t_, ATT_W + KV_W + HD * g:ATT_W + KV_W + HD * g + HD] for t_ in ([0] if t == 0 else range(1, TT))]
                    if t:
                        vs.append(vc[:, HD * g:HD * g + HD])
                    for m, v in enumerate(vs):
                        last = mm(accf[:, 1024 * b + 768:1024 * b + 768 + HD], pT[:, b, m * P:(m + 1) * P], v,
                                  start=(m == 0), stop=(m == len(vs) - 1))
                    last.then_inc(S["att_made"], pe.up("att_made"))
            eng.wait_ge(S["att_read"], U)
            eng.wait_ge(S["exp_done"], U)
            eng.wait_ge(S["a_ready"], pe.next("a_ready"))
            for t in range(TT):
                for d in range(2):
                    tri = (upto, onward)[d]
                    others = [] if t == 0 else (range(1, t) if d == 0 else range(t + 1, TT))
                    parts = [(ones, t_) for t_ in others] + [(tri, t)]
                    for m, (w, t_) in enumerate(parts):
                        last = mm(mixf[:, t * DTS + NH * d:t * DTS + NH * d + NH], w[:, :], a_tok[:, t_, NH * d:NH * d + NH],
                                  start=(m == 0), stop=(m == len(parts) - 1))
            last.then_inc(S["cum_made"], pe.up("cum_made"))
            eng.wait_ge(S["conv_ready"], pe.next("conv_ready"))
            for t in range(TT):
                if pe.due("xt_read", 2):
                    eng.wait_ge(S["xt_read"], pe.now("xt_read", 2))
                for j in range(ST):
                    last = eng.transpose(acc[:, t % 2, j * P:(j + 1) * P], conv[:, j, pad(t)], ident[:, :])
                last.then_inc(S["xt_made"], pe.up("xt_made"))
            eng.transpose(acc[:, 2, 0:P], conv[:, ST, pad(0)], ident[:, :]).then_inc(S["bt_made"], pe.up("bt_made"))
            for g in range(2):
                B, C = (conv[HD * g:HD * g + HD, ST + m, :] for m in range(2))
                for J in range(LT):
                    n = g * (LT + 1) + J
                    if pe.due("cb_read", 2):
                        eng.wait_ge(S["cb_read"], pe.now("cb_read", 2))
                    ins = mm(mix[:, 1 + n % 2, :], B[:, pad(J + 1)], C[:, LAT], start=True, stop=True)
                    ins.then_inc(S["cb_made"], pe.up("cb_made"))
                n += 1
                if pe.due("cb_read", 2):
                    eng.wait_ge(S["cb_read"], pe.now("cb_read", 2))
                ins = mm(mix[:, 1 + n % 2, 0:P], B[:, pad(0)], C[:, pad(0)], start=True, stop=True)
                ins.then_inc(S["cb_made"], pe.up("cb_made"))
            eng.wait_ge(S["cum_read"], pe.next("cum_read"))
            eng.wait_ge(S["xt_read"], TT)
            eng.wait_ge(S["bt_read"], 1)
            eng.wait_ge(S["cb_read"], 2 * (LT + 1))
            for h in range(NH + 1):
                if h < NH:
                    if pe.due("rows_read", 1):
                        eng.wait_ge(S["rows_read"], pe.now("rows_read", 1))
                    for d in range(2):
                        for t in range(TT):
                            c = cum[:, t, NH * d + h:NH * d + h + 1].broadcast_to([P, P])
                            last = mm(accf[:, 1024 * d + t * P:1024 * d + (t + 1) * P], c, ident[:, :], start=True, stop=True)
                    last.then_inc(S["rows_made"], pe.up("rows_made"))
                    ada_job(0, 8 + 2 * h, h > 0)
                if h >= 1:
                    g = h - 1
                    eng.wait_ge(S["m_ready"], pe.next("m_ready"))
                    if pe.due("y_read", 2):
                        eng.wait_ge(S["y_read"], pe.now("y_read", 2))
                    cols = slice(g * HD, (g + 1) * HD)
                    mm(mix[0:HD, 2, (g % 2) * P:(g % 2 + 1) * P], x_tok[:, 0, cols], dgs[g % 2][:, 0, :], start=True, stop=True)
                    for J in range(LT):
                        mm(mix[0:HD, g % 2, :], x_tok[:, J + 1, cols], M_all[:, J, :], start=(J == 0), stop=False)
                    last = mm(mix[0:HD, g % 2, :], s0[:, g, :], ce[:, :], start=False, stop=True)
                    last.then_inc(S["y_made"], pe.up("y_made"))
                if h < NH:
                    ada_job(0, 9 + 2 * h)
            ada_turn(0, ADA_JOBS - 1)
            for h in range(NH):
                eng.wait_ge(S["bw_ready"], pe.next("bw_ready"))
                ins = mm(mix[:, 2, h * HD:(h + 1) * HD], bw[:, h % 2, :], x_tok[:, 0, h * HD:(h + 1) * HD], start=True, stop=True)
                ins.then_inc(S["fs_made"], pe.up("fs_made"))
            eng.wait_ge(S["y_read"], NH)
            for t in range(TT):
                if pe.due("aT_read", 2):
                    eng.wait_ge(S["aT_read"], pe.now("aT_read", 2))
                for j in range(ST):
                    last = eng.transpose(acc[:, 2 + t % 2, j * P:(j + 1) * P], att_tok[:, t, j * P:(j + 1) * P], ident[:, :])
                last.then_inc(S["aT_made"], pe.up("aT_made"))
            eng.wait_ge(S["s_out_ready"], 1)
            eng.wait_ge(S["aT_read"], TT)
            eng.wait_ge(S["h_ready"], pe.next("h_ready"))
            for j in range(2):
                s = next_job()
                for c in range(4):
                    tile_a(s, h_hi, h_lo, ST, c * P, 2 * W)
                    if j == 1 and c == 1:
                        rms_sum()
            rms_back()
            for j in range(2):
                s = next_job()
                for c in range(4):
                    tile_a(s, h_hi[:, ST:, :], h_lo[:, ST:, :], ST, c * P, 2 * W, came="h_ready" if j == c == 0 else None)
                if j == 0:
                    eng.wait_ge(S["mod_read"], pe.next("mod_read"))
                ada_job(1, j, j > 0)

            def ffn(l):
                rms()

                def gate_up(f, s_, first):
                    s = next_job()
                    if first:
                        first_pair(s)
                    else:
                        tile_a(s, h_hi, h_lo, KT, 0)
                        tile_a(s, h_hi, h_lo, KT, P)
                    if l == 0:
                        split_ada_job(1, f + s_ + 2, 2 if first else 4)

                for f0, nf in CHUNKS:
                    per = {"w_lo0": 1, "w_lo1": 1, "acc_free0": 2, "acc_free1": 2, "acc_ready0": 2, "acc_ready1": 2}
                    if l == 0:
                        per |= {"ada_lo": 2, "ada_used": 2, "row_in": 2, "ada_turned": 2}
                    turns = nf // 2
                    if f0 == 0:
                        for s_ in range(2):
                            gate_up(0, s_, s_ == 0)
                        turns -= 1
                    with pe.loop(turns, per) as i:
                        for s_ in range(2):
                            gate_up(i * 2 + f0 + 2 * (f0 == 0), s_, False)
                    for j in range(4):
                        s = next_job()
                        tile_a(s, gu_hi, gu_lo, nf, 0, came="gu_ready" if j == 0 else None)
                        tile_a(s, gu_hi, gu_lo, nf, P)

            ffn(0)
            ada_turn(1, ADA_JOBS - 1, 4)
            rms()
            pe.skip("h_ready", KT)
            h_made = pe.now("h_ready")
            per = {"w_lo0": 4, "w_lo1": 4, "acc_free0": 13, "acc_free1": 13, "acc_ready0": 13, "acc_ready1": 13,
                   "rope_done": 1, "kp_made": 1, "kw_ready": 1, "head_in": 16 * 8, "score_made": 5, "sc_ready": 5,
                   "y_part": 5, "qg_ready": 2, "state_done": 2, "v_in": 1, "state_made": 4, "fs_ready": 4, "yr_read": 1,
                   "sq_done": 1, "stat": 1, "rinv": 1, "rb": 1, "yg_ready": 4}
            with pe.loop(RH, per):
                for j in range(2):
                    s = next_job()
                    for c in range(2):
                        tile_a(s, h_hi, h_lo, KT, c * P, h_from=h_made - KT if j == c == 0 else None)
                for j in range(2):
                    s = next_job()
                    for t in range(TT):
                        tile_b(s, t)
                eng.wait_ge(S["acc_free0"], pe.now("acc_free0"))
                eng.wait_ge(S["acc_free1"], pe.now("acc_free1"))
                eng.wait_ge(S["rope_done"], pe.next("rope_done"))
                for k in range(2):
                    last = eng.transpose(mix[:, 0, k * P:(k + 1) * P], qk[:, 2 + k, 0:P], ident[:, :])
                last.then_inc(S["kp_made"], pe.up("kp_made"))

                def score(J):
                    n = N_LAT if J < LT else N_CTX
                    i0, j0 = (N_CTX, (J + 1) * P) if J < LT else (0, 0)
                    for k in range(2):
                        last = mm(mix[:, 1 + J % 2, 0:n], qk[:, 2 + k, j0:j0 + P], qk[:, k, i0:i0 + n],
                                  start=(k == 0), stop=(k == 1))
                    last.then_inc(S["score_made"], pe.up("score_made"))

                def states(b):
                    eng.wait_ge(S["qg_ready"], pe.next("qg_ready"))
                    for v in range(VT):
                        for k in range(2):
                            last = mm(acc[:, v, :], S0[:, b, k, v * P:(v + 1) * P], qg[:, k, :],
                                      start=(b == 0 and k == 0), stop=(b == 1 and k == 1))
                    last.then_inc(S["state_done"], pe.up("state_done"))

                score(0)
                score(1)
                eng.wait_ge(S["head_in"], pe.next("head_in", 16 * 8))
                states(0)
                eng.wait_ge(S["v_in"], pe.next("v_in"))
                for J in range(LT + 1):
                    eng.wait_ge(S["sc_ready"], pe.next("sc_ready"))
                    if J == LT:
                        eng.wait_ge(S["kw_ready"], pe.next("kw_ready"))
                    for v in range(VT):
                        if J < LT:
                            last = mm(acc[:, v, :], v_tok[:, J + 1, v * P:(v + 1) * P], sc_sb[:, J % 2, :], start=False, stop=False)
                        else:
                            last = mm(mix[:, 0, v * P:(v + 1) * P], v_tok[:, 0, v * P:(v + 1) * P], sc_p[:, :], start=True, stop=True)
                    last.then_inc(S["y_part"], pe.up("y_part"))
                    if J + 2 <= LT:
                        score(J + 2)
                def final_state(n):
                    b, k = divmod(n, 2)
                    if n >= 2:
                        eng.wait_ge(S["fs_ready"], pe.next("fs_ready"))
                    ins = mm(mix[:, 1 + n % 2, :], kw[:, b, k * P:(k + 1) * P], v_tok[:, 0, :], start=True, stop=True)
                    ins.then_inc(S["state_made"], pe.up("state_made"))

                final_state(0)
                final_state(1)
                states(1)
                final_state(2)
                final_state(3)
                eng.wait_ge(S["yr_read"], pe.next("yr_read"))
                s = next_job()
                tile_a(s, h_hi, h_lo, KT, 0)
                rms_sum()
                tile_a(s, h_hi, h_lo, KT, P)
                eng.wait_ge(S["fs_ready"], pe.next("fs_ready", 2))
                rms_back()
                s = next_job()
                for c in range(2):
                    tile_a(s, h_hi, h_lo, KT, c * P)
                for j in range(2):
                    s = next_job()
                    for c in range(4):
                        tile_a(s, yg_hi, yg_lo, VT, c * P, 2 * W, came="yg_ready" if j == c == 0 else None)
            ffn(1)
            rms()
            for n in range(2 * TT):
                half, t = divmod(n, TT)
                if t == 0:
                    eng.wait_ge(S["final_ready"], pe.next("final_ready"))
                if n >= 4:
                    eng.wait_ge(S[COPIER[n - 4]], copied(n - 4))
                for k in range(4):
                    last = eng.transpose(acc[:, n % 4, k * P:(k + 1) * P], xT[:, half * 4 + k, tok(t)], ident[:, :])
                last.then_inc(S["out_T"], pe.up("out_T"))

        @block.scalar
        def _(eng):
            ac = Line(eng, "act")
            act = eng.activation
            job, tile = [0], [0]

            def split_hi():
                s = job[0] % 2
                job[0] += 1
                eng.wait_ge(S[f"raw_in{s}"], ac.next(f"raw_in{s}", 32))
                act(w_hi[s][:, :], raw[s][:, :], ACT.Copy).then_inc(S[f"w_hi{s}"], ac.up(f"w_hi{s}"))

            def ada_rows(rows=2):
                eng.wait_ge(S["ada_used"], ac.next("ada_used"))
                act(ada_row[0:rows, :], ROWS[0:rows, :], ACT.Copy).then_inc(S["row_in"], ac.up("row_in"))

            def split_ada_hi(s):
                eng.wait_ge(S[f"ada_in{s}"], ac.next(f"ada_in{s}", 32))
                eng.wait_ge(S["ada_used"], ac.now("ada_used"))
                act(ada_hi[:, :], ada_raw[s][:, :], ACT.Copy).then_inc(S["ada_hi"], ac.up("ada_hi"))

            def tile_of():
                r = tile[0] % 2
                tile[0] += 1
                eng.wait_ge(S[f"acc_ready{r}"], ac.next(f"acc_ready{r}"))
                return r

            def pass_tiles(n):
                for _ in range(n - 1):
                    ac.skip(f"acc_ready{tile[0] % 2}")
                    tile[0] += 1
                tile_of()

            def root(n=TT):
                eng.wait_ge(S["mean"], ac.next("mean"))
                act(stt[:, 1, 0:n], stt[:, 0, 0:n], ACT.Sqrt).then_inc(S["root"], ac.up("root"))

            def modulate(l, m):
                for k in range(KT):
                    eng.wait_ge(S["normed"], ac.next("normed"))
                    for cols, c in PARTS:
                        ins = act(h_hi[:, k, cols], nbuf[k % 4][:, cols], ACT.Identity, bias=mod[l][:, SH[m] + k, c:c + 1])
                    ins.then_inc(S["h_hi"], ac.up("h_hi"))

            def small(dst, src):
                eng.dma_start(dst, src).then_inc(S["setup_in"], ac.up("setup_in", 16))

            rows = lambda a, n=P: a.rearrange("(r c) -> r c", c=n)
            for l in range(2):
                small(stg_a[48 * l:48 * l + 48, :], rows(I[f"l{l}_b_ada"]))
                small(stg_b[NM[l]:NM[l] + KT, :], rows(I[f"l{l}_norm_mix"]))
                small(stg_b[NF[l]:NF[l] + KT, :], rows(I[f"l{l}_norm_ffn"]))
            small(stg_b[FIN:FIN + KT, :], rows(I["final_norm"]))
            small(stg_b[COND:COND + KT, :], rows(I["c_ctx"]))
            small(stg_b[COND + KT:COND + 2 * KT, :], I["c"][0, :].rearrange("(r c) -> r c", c=P))
            small(stg_b[CONV_B:CONV_B + XBC_T, :], rows(I["l0_conv_b"]))
            small(stg_b[SSD_G:SSD_G + ST, :], rows(I["l0_ssd_gain"]))
            small(stg_b[CONV_W:CONV_W + TAPS * XBC_T, :], I["l0_conv_w"].rearrange("k (t c) -> (k t) c", c=P))
            eng.wait_ge(S["vec_read"], ac.next("vec_read"))
            act(scond[:, :, :].rearrange("p k c -> p c k"),
                       vec[:, COND:COND + 2 * KT].rearrange("p (c k) -> p c k", c=2), ACT.Silu).then_inc(S["cond"], ac.up("cond"))
            eng.wait_ge(S[ac.last], ac.ended())
            act(sc4[:, :, 0:2], scond[:, :, :], ACT.Copy).then_inc(S["sc_hi"], ac.up("sc_hi"))
            for n in range(6):
                ada_rows()
            root()
            ada_rows()
            split_hi()
            ada_rows()
            eng.wait_ge(S["gain_ready"], ac.next("gain_ready"))
            modulate(0, 0)
            split_hi()
            for j in range(8):
                if j == 3:
                    eng.wait_ge(S["l0_in"], ac.next("l0_in", 16 * 13))
                    act(dtw_hi[:, :, :], dtw[:, :, :], ACT.Copy).then_inc(S["dtw_hi"], ac.up("dtw_hi"))
                if j < 3:
                    for t in range(TT):
                        r = tile_of()
                        dst, src = qkv[:, t, j * W:(j + 1) * W], acc[:, 2 * r, 0:W]
                        if j < 2:
                            dst = qkv[:, t, 0:ATT_W].rearrange("p (i g d) -> p i g d", g=2, d=HD)[:, :, j, :]
                            src = src.rearrange("p (i d) -> p i d", d=HD)
                        act(dst, src, ACT.Copy).then_inc(S["act"], ac.up("act"))
                        eng.wait_ge(S[ac.last], ac.ended())
                        eng.sem_inc(S[f"acc_free{r}"], ac.told(f"acc_free{r}"))
                    if j == 2:
                        eng.wait_ge(S[ac.last], ac.ended())
                        eng.sem_inc(S["qkv_in"], ac.told("qkv_in"))
                else:
                    for c in range(2):
                        if j == 3 and c == 1:
                            root(TT * 10)
                        r = tile_of()
                        i = (j - 3) * 2 + c
                        if j < 6:
                            for b, src, dst, _ in SEGS:
                                o = 2 if dst.start == 0 else 6
                                ins = act(xpad[:, i, dst.start + o:dst.stop + o], acc[:, 2 * r + b, src], ACT.Copy)
                            ins.then_inc(S["act"], ac.up("act"))
                            eng.wait_ge(S[ac.last], ac.ended())
                            eng.sem_inc(S[f"acc_free{r}"], ac.told(f"acc_free{r}"))
                            eng.wait_ge(S[ac.last], ac.ended())
                            eng.sem_inc(S["xb_in"], ac.told("xb_in"))
                        else:
                            act(halves(zT[:, i - 6, :]), pair(r), ACT.Silu).then_inc(S["act"], ac.up("act"))
                            eng.wait_ge(S[ac.last], ac.ended())
                            eng.sem_inc(S[f"acc_free{r}"], ac.told(f"acc_free{r}"))
                        if i == 6:
                            eng.wait_ge(S["dt_turned"], ac.next("dt_turned"))
                            ins = act(dt_tok[:, :, :].rearrange("p t c -> p (t c)"), mix[:, 0, 0:TT * DTS], ACT.Copy)
                            ins.then_inc(S["dt_in"], ac.up("dt_in"))
                if j == 5:
                    r = tile_of()
                    act(halves(dtT), acc[0:DTS, 2 * r:2 * r + 2, 0:HALF], ACT.Copy).then_inc(S["act"], ac.up("act"))
                    eng.wait_ge(S[ac.last], ac.ended())
                    eng.sem_inc(S[f"acc_free{r}"], ac.told(f"acc_free{r}"))
                    eng.sem_inc(S["dt_rows"], ac.told("dt_rows"))
                if j < 6:
                    split_hi()
                if j == 6:
                    eng.wait_ge(S["dt_abs"], ac.next("dt_abs"))
                    act(dt_t[1][:, :, :], dt_t[1][:, :, :], ACT.Exp, scale=-1.0).then_inc(S["dt_exp"], ac.up("dt_exp"))
                    act(dt_c[:, 1, :], dt_c[:, 1, :], ACT.Exp)
                    eng.wait_ge(S["dt_u"], ac.next("dt_u"))
                    act(dt_t[3][:, :, :], dt_t[0][:, :, :], ACT.Ln).then_inc(S["dt_ln"], ac.up("dt_ln"))
                if j >= 6:
                    for i in (range(4) if j == 6 else (4, 5)):
                        if i % 2 == 0:
                            eng.wait_ge(S["conv_raw"], ac.next("conv_raw"))
                        for cols in (slice(0, N_CTX), LAT):
                            ins = act(conv[:, i, cols], conv[:, i, cols], ACT.Silu, bias=vec[:, CONV_B + i:CONV_B + i + 1])
                    if j == 7:
                        ins.then_inc(S["conv_ready"], ac.up("conv_ready"))
            eng.wait_ge(S["kT_made"], ac.next("kT_made"))
            act(kT[:, :], accf[:, 0:N + PAST], ACT.Copy).then_inc(S["act"], ac.up("act"))
            for t in range(TT):
                eng.wait_ge(S["qT_made"], ac.next("qT_made"))
                ins = act(qT[:, :, tok(t)], acc[:, 2 + t % 2, :].rearrange("p (j n) -> p j n", j=4), ACT.Copy)
                ins.then_inc(S["qT_sb"], ac.up("qT_sb"))
            for u, (t, h) in enumerate(units):
                b = u % 2
                n = N_CTX if t == 0 else N
                eng.wait_ge(S["max_ready"], ac.next("max_ready"))
                if ac.due("pT_made", 2):
                    eng.wait_ge(S["pT_made"], ac.now("pT_made", 2))
                act(probs[:, b, 0:n], mixf[:, 1024 * b:1024 * b + n], ACT.Exp, bias=nmax[:, u % 4:u % 4 + 1],
                           scale=ATT_SCALE, accum_out=rsum[:, u % 4:u % 4 + 1]).then_inc(S["exp_done"], ac.up("exp_done"))
            eng.wait_ge(S["cum_read"], ac.next("cum_read"))
            for h in range(NH):
                eng.wait_ge(S["arg_ready"], ac.next("arg_ready"))
                act(dgs[h % 2], dgs[h % 2], ACT.Exp).then_inc(S["diag_exp"], ac.up("diag_exp"))
                if ac.due("m_ready", 1):
                    eng.wait_ge(S["m_ready"], ac.now("m_ready", 1))
                for J in range(LT):
                    if J < LT - 1:
                        act(E_all[:, J, (J + 1) * P:], accf[:, (J + 2) * P:N], ACT.Exp, bias=ncum[:, J + 1, h:h + 1])
                    if J:
                        act(E_all[:, J, 0:J * P], accf[:, 1024 + P:1024 + (J + 1) * P], ACT.Exp,
                            bias=ncum[:, J + 1, NH + h:NH + h + 1])
                for b in range(2):
                    ins = act(ecum[HD * b:HD * b + HD, :], accf[HD * b:HD * b + HD, 1024 * b + P:1024 * b + N], ACT.Exp)
                ins.then_inc(S["rows_read"], ac.up("rows_read"))
                ada_rows()
                ada_rows()
            eng.wait_ge(S["wst_arg"], ac.next("wst_arg"))
            act(wst[:, :], wst[:, :], ACT.Exp).then_inc(S["wst_exp"], ac.up("wst_exp"))
            for s in range(2):
                ac.skip(f"raw_in{s}", 32 * (ADA_JOBS - 8) // 2)
            split_hi()
            for t in range(TT):
                eng.wait_ge(S["aT_made"], ac.next("aT_made"))
                ins = act(h_hi[:, 0:ST, tok(t)], acc[:, 2 + t % 2, :].rearrange("p (j n) -> p j n", j=4), ACT.Copy)
                ins.then_inc(S["h_hi"], ac.up("h_hi"))
            split_hi()
            pass_tiles(4)
            split_hi()
            root()
            for j in range(ST):
                eng.wait_ge(S["y32_ready"], ac.next("y32_ready"))
                act(h_hi[:, ST + j, :], y_buf[j % 2], ACT.Copy).then_inc(S["h_hi"], ac.up("h_hi"))
            pass_tiles(4)
            split_hi()
            for j in range(2):
                pass_tiles(4)
                split_hi()
                ada_rows()

            def ffn(l):
                root()
                if l == 0:
                    eng.wait_ge(S["gain_ready"], ac.next("gain_ready"))
                modulate(l, 1)
                for f0, nf in CHUNKS:
                    per = {"acc_ready0": 2, "acc_ready1": 2, "acc_free0": 2, "silu_ready": 2, "gu32_ready": 2, "gu_hi": 2,
                           "gu_ready": 2, "raw_in0": 32, "raw_in1": 32, "w_hi0": 1, "w_hi1": 1, "act": 2}
                    if l == 0:
                        per |= {"ada_used": 2, "row_in": 2, "ada_in0": 32, "ada_in1": 32, "ada_hi": 2}
                    with ac.loop(nf // 2, per) as i:
                        for s in range(2):
                            if l == 0:
                                split_ada_hi(s)
                            r = tile_of()
                            act(halves(silu_g[:, :]), pair(r), ACT.Silu).then_inc(S["act"], ac.up("act"))
                            eng.wait_ge(S[ac.last], ac.ended())
                            eng.sem_inc(S[f"acc_free{r}"], ac.told(f"acc_free{r}"))
                            eng.wait_ge(S[ac.last], ac.ended())
                            eng.sem_inc(S["silu_ready"], ac.told("silu_ready"))
                            tile_of()
                            split_hi()
                            eng.wait_ge(S["gu32_ready"], ac.next("gu32_ready"))
                            ins = act(gu_hi[:, bass.ds(i * 2 + s, 1), :].rearrange("p o n -> p (o n)"), gu32[:, :], ACT.Copy)
                            ins.then_inc(S["gu_hi"], ac.up("gu_hi"))
                            if l == 0:
                                ada_rows(4)
                    for j in range(4):
                        pass_tiles(2)
                        if not (l == 1 and f0 == CHUNKS[-1][0] and j >= 2):
                            split_hi()

            for s in range(2):
                ac.skip(f"ada_in{s}", 32)
            ffn(0)
            root()
            eng.wait_ge(S["gain_ready"], ac.next("gain_ready"))
            modulate(1, 0)
            per = {"acc_ready0": 13, "acc_ready1": 13, "acc_free0": 9, "acc_free1": 9, "raw_in0": 128, "raw_in1": 128,
                   "w_hi0": 4, "w_hi1": 4, "qk_in": 1, "v_in": 1, "head_in": 128, "decay_exp": 1, "arg1_ready": 1, "strip_exp": 1,
                   "grow_used": 2, "grow_ready": 2, "wcol_ready": 1, "mean": 1, "root": 1, "z32_ready": 4, "yg_hi": 4, "yg_ready": 4,
                   "g_in": 4, "state_made": 4, "fs_ready": 4, "fs_out0": 32, "fs_out1": 32, "act": 18}
            with ac.loop(RH, per):
                for j in range(2):
                    for c in range(2):
                        r = tile_of()
                        ins = act(halves(qk[:, 2 * j + c, :]), pair(r), ACT.Copy, scale=1.0 if j == 0 else K_SCALE)
                        ins.then_inc(S["act"], ac.up("act"))
                        eng.wait_ge(S[ac.last], ac.ended())
                        eng.sem_inc(S[f"acc_free{r}"], ac.told(f"acc_free{r}"))
                    split_hi()
                    if j == 0:
                        eng.wait_ge(S["head_in"], ac.next("head_in", 128))
                        act(acol[:, :], acol[:, :], ACT.Exp).then_inc(S["decay_exp"], ac.up("decay_exp"))
                eng.wait_ge(S[ac.last], ac.ended())
                eng.sem_inc(S["qk_in"], ac.told("qk_in"))
                eng.wait_ge(S["arg1_ready"], ac.next("arg1_ready"))
                act(strip[:, :], strip[:, :], ACT.Exp).then_inc(S["strip_exp"], ac.up("strip_exp"))
                act(grow[:, :], ramp[:, 0, :], ACT.Exp, scale=acol[:, 0:1]).then_inc(S["grow_ready"], ac.up("grow_ready"))
                for b in range(2):
                    ins = act(wcol[:, b:b + 1], pcol[:, b:b + 1], ACT.Exp, scale=acol[:, b:b + 1])
                ins.then_inc(S["wcol_ready"], ac.up("wcol_ready"))
                for j in range(2):
                    for t in range(TT):
                        r = tile_of()
                        act(v_tok[:, t, j * W:(j + 1) * W], acc[:, 2 * r, 0:W], ACT.Copy).then_inc(S["act"], ac.up("act"))
                        eng.wait_ge(S[ac.last], ac.ended())
                        eng.sem_inc(S[f"acc_free{r}"], ac.told(f"acc_free{r}"))
                    split_hi()
                eng.wait_ge(S[ac.last], ac.ended())
                eng.sem_inc(S["v_in"], ac.told("v_in"))
                eng.wait_ge(S["grow_used"], ac.next("grow_used"))
                act(grow[:, :], ramp[:, 1, :], ACT.Exp, scale=acol[:, 1:2]).then_inc(S["grow_ready"], ac.up("grow_ready"))
                eng.wait_ge(S["grow_used"], ac.next("grow_used"))
                for n in range(4):
                    eng.wait_ge(S["state_made"], ac.next("state_made"))
                    if n >= 2:
                        eng.wait_ge(S[f"fs_out{n % 2}"], ac.next(f"fs_out{n % 2}", 16))
                    act(tbuf[:, n % 2, 0:DV], mix[:, 1 + n % 2, :], ACT.Copy).then_inc(S["fs_ready"], ac.up("fs_ready"))
                def y_high(v):
                    eng.wait_ge(S["z32_ready"], ac.next("z32_ready"))
                    act(yg_hi[:, v, :], h32[:, :], ACT.Copy).then_inc(S["yg_hi"], ac.up("yg_hi"))

                for v in range(VT):
                    r = tile_of()
                    if v < 2:
                        eng.wait_ge(S[f"fs_out{v}"], ac.next(f"fs_out{v}", 16))
                    else:
                        eng.wait_ge(S["yg_ready"], ac.next("yg_ready"))
                    act(halves(tbuf[:, v % 2, :]), pair(r), ACT.Silu).then_inc(S["act"], ac.up("act"))
                    eng.wait_ge(S[ac.last], ac.ended())
                    eng.sem_inc(S[f"acc_free{r}"], ac.told(f"acc_free{r}"))
                    eng.sem_inc(S["g_in"], ac.told("g_in"))
                    if v == 0:
                        root()
                    if v == 1:
                        split_hi()
                        y_high(0)
                        y_high(1)
                    if v >= 2:
                        y_high(v)
                split_hi()
                eng.wait_ge(S["yg_ready"], ac.next("yg_ready", 2))
                for j in range(2):
                    pass_tiles(4)
                    split_hi()
            ffn(1)
            root()
            for n in range(2 * TT):
                half, t = divmod(n, TT)
                if COPIER[n] == "y_by_act":
                    eng.wait_ge(S["out_T"], n + 1)
                    ins = act(y_out[:, t, half * 512:(half + 1) * 512], acc[:, n % 4, :], ACT.Copy)
                    ins.then_inc(S["y_by_act"], ac.up("y_by_act"))

        @block.vector
        def _(eng):
            v = Line(eng, "dve")
            tt, ts, st3 = eng.tensor_tensor, eng.tensor_scalar, eng.scalar_tensor_tensor
            job, tile = [0], [0]

            def split_lo():
                s = job[0] % 2
                job[0] += 1
                eng.wait_ge(S[f"w_hi{s}"], v.next(f"w_hi{s}"))
                ins = tt(w_lo[s][:, :], raw[s][:, :], w_hi[s][:, :].bitcast(f32), ALU.subtract)
                ins.then_inc(S[f"w_lo{s}"], v.up(f"w_lo{s}"))

            def pass_tiles(n):
                for _ in range(n):
                    v.skip(f"acc_ready{tile[0] % 2}")
                    tile[0] += 1

            def tile_of():
                r = tile[0] % 2
                tile[0] += 1
                eng.wait_ge(S[f"acc_ready{r}"], v.next(f"acc_ready{r}"))
                return r

            def square_in(src, first):
                if first:
                    tt(sq_sum[:, :], src, src, ALU.mult).then_inc(S["dve"], v.up("dve"))
                    eng.wait_ge(S[v.last], v.ended())
                else:
                    tt(sq[:, :], src, src, ALU.mult).then_inc(S["dve"], v.up("dve"))
                    eng.wait_ge(S[v.last], v.ended())
                    tt(sq_sum[:, :], sq_sum[:, :], sq[:, :], ALU.add).then_inc(S["dve"], v.up("dve"))
                    eng.wait_ge(S[v.last], v.ended())

            def inverse_root(n, name="dve"):
                m, r, y, t, out = (stt[:, i, 0:n] for i in range(5))
                eng.wait_ge(S["root"], v.next("root"))
                eng.reciprocal(y, r).then_inc(S["dve"], v.up("dve"))
                eng.wait_ge(S[v.last], v.ended())
                tt(t, y, y, ALU.mult).then_inc(S["dve"], v.up("dve"))
                eng.wait_ge(S[v.last], v.ended())
                tt(t, t, m, ALU.mult).then_inc(S["dve"], v.up("dve"))
                eng.wait_ge(S[v.last], v.ended())
                ts(t, t, -0.5, 1.5, ALU.mult, ALU.add).then_inc(S["dve"], v.up("dve"))
                eng.wait_ge(S[v.last], v.ended())
                tt(out, y, t, ALU.mult).then_inc(S[name], v.up(name))

            def rms_to_inverse(width, before=None):
                eng.wait_ge(S[v.last], v.ended())
                eng.sem_inc(S["sq_done"], v.told("sq_done"))
                if before:
                    before()
                eng.wait_ge(S["stat"], v.next("stat"))
                ts(stt[:, 0, 0:TT], mixf[:, 0:TT], 1.0 / width, EPS, ALU.mult, ALU.add).then_inc(S["mean"], v.up("mean"))
                inverse_root(TT, "rinv")

            def rms(width, meanwhile=None):
                rms_to_inverse(width)
                if meanwhile:
                    meanwhile()
                eng.wait_ge(S["rb"], v.next("rb"))

            def modulate(l, m):
                def normed(k):
                    for cols, c in PARTS:
                        ins = st3(nbuf[k % 4][:, cols], xT[:, k, cols], gain[l][m][:, k, c:c + 1], rB[:, cols], ALU.mult, ALU.mult)
                    ins.then_inc(S["normed"], v.up("normed"))

                normed(0)
                for k in range(KT):
                    if k + 1 < KT:
                        if k >= 3:
                            eng.wait_ge(S["h_ready"], v.made["h_ready"] - 2)
                        normed(k + 1)
                    eng.wait_ge(S["normed"], v.made["normed"] - (k + 1 < KT))
                    eng.wait_ge(S["h_hi"], v.next("h_hi"))
                    for cols, c in PARTS:
                        ins = st3(h_lo[:, k, cols], nbuf[k % 4][:, cols], mod[l][:, SH[m] + k, c:c + 1],
                                  h_hi[:, k, cols].bitcast(f32), ALU.add, ALU.subtract)
                    ins.then_inc(S["h_ready"], v.up("h_ready"))
                eng.wait_ge(S[v.last], v.ended())

            def mods(l, a, b):
                tt(mod[l][:, a:b, :], ADA[:, l, a:b, :],
                         b_ada[:, l, a:b].unsqueeze(2).broadcast_to([P, b - a, 2]), ALU.add).then_inc(S["mod_read"], v.up("mod_read"))
                eng.wait_ge(S[v.last], v.ended())

            def gains(l, m):
                row = (NM, NF)[m][l]
                for c in range(2):
                    ins = st3(gain[l][m][:, :, c], mod[l][:, SC[m]:SC[m] + KT, c], 1.0, vec[:, row:row + KT], ALU.add, ALU.mult)
                return ins

            def into_x(l, m, d, squares=True):
                r = tile_of()
                for b, src, dst, c in SEGS:
                    ins = st3(xT[:, d, dst], acc[:, 2 * r + b, src], mod[l][:, GA[m] + d, c:c + 1], xT[:, d, dst], ALU.mult, ALU.add)
                ins.then_inc(S["dve"], v.up("dve"))
                eng.wait_ge(S[v.last], v.ended())
                eng.sem_inc(S[f"acc_free{r}"], v.told(f"acc_free{r}"))
                eng.wait_ge(S[v.last], v.ended())
                if squares:
                    square_in(xT[:, d, :], d == 0)

            eng.wait_ge(S["vec_T"], v.next("vec_T"))
            eng.tensor_copy(b_ada[:, :, :].rearrange("p l j -> p (l j)"), mix[:, 0, 0:96])
            eng.tensor_copy(vec[:, :], mix[:, 0, 96:96 + N_ROWS]).then_inc(S["vec_read"], v.up("vec_read"))
            tt(fold[:, :], ident[0:4, 0:2], ident[0:4, 2:4], ALU.add)
            eng.wait_ge(S["sc_hi"], v.next("sc_hi"))
            tt(sc4[:, :, 2:4], scond[:, :, :], sc4[:, :, 0:2].bitcast(f32), ALU.subtract).then_inc(S["dve"], v.up("dve"))
            for n in range(2 * TT):
                t, half = divmod(n, 2)
                eng.wait_ge(S["x_T"], v.next("x_T"))
                ins = eng.tensor_copy(xT[:, half * 4:half * 4 + 4, tok(t)], acc[:, n % 2, :].rearrange("p (k n) -> p k n", k=4))
                ins.then_inc(S["x_T_read"], v.up("x_T_read"))
            eng.wait_ge(S[v.last], v.ended())
            for k in range(KT):
                square_in(xT[:, k, :], k == 0)
            rms(D, split_lo)
            eng.wait_ge(S["ada_turned"], v.next("ada_turned", 8))
            mods(0, 0, 16)
            gains(0, 0).then_inc(S["gain_ready"], v.up("gain_ready"))
            eng.wait_ge(S[v.last], v.ended())
            modulate(0, 0)
            split_lo()
            heads = lambda a: a.rearrange("p (h d) -> p h d", d=HD)

            def norm_and_turn(t):
                x = heads(qkv[:, t, 0:N])
                ins = tt(x, x, stt[:, 4, t * 10:(t + 1) * 10].unsqueeze(2).broadcast_to([P, 10, HD]), ALU.mult)
                ins.then_inc(S["dve"], v.up("dve"))
                eng.wait_ge(S[v.last], v.ended())
                tt(x[:, 0:NH, :], x[:, 0:NH, :], qk_g[:, 0, :].unsqueeze(1).broadcast_to([P, NH, HD]), ALU.mult)
                ins = tt(x[:, NH:, :], x[:, NH:, :], qk_g[:, 1, :].unsqueeze(1).broadcast_to([P, NKV, HD]), ALU.mult)
                ins.then_inc(S["new_kv" if t == 0 else "dve"], v.up("new_kv" if t == 0 else "dve"))
                eng.wait_ge(S[v.last], v.ended())
                if t:
                    a, b = x[:, :, 0:32], x[:, :, 32:HD]
                    co, si = (c[:, t - 1, :].unsqueeze(1).broadcast_to([P, 10, 32]) for c in (cosA, sinA))
                    r = [tbuf[:, i // 2, (i % 2) * 320:(i % 2 + 1) * 320].rearrange("p (h d) -> p h d", d=32) for i in range(4)]
                    for o, p_, q_ in zip(r, (a, b, b, a), (co, si, co, si)):
                        ins = tt(o, p_, q_, ALU.mult)
                    ins.then_inc(S["dve"], v.up("dve"))
                    eng.wait_ge(S[v.last], v.ended())
                    tt(a, r[0], r[1], ALU.subtract)
                    ins = tt(b, r[2], r[3], ALU.add)
                    ins.then_inc(S["roped" if t == TT - 1 else "dve"], v.up("roped" if t == TT - 1 else "dve"))
                    eng.wait_ge(S[v.last], v.ended())

            for j in range(8):
                pass_tiles((TT, TT, TT, 2, 2, 3, 2, 2)[j])
                if j < 6:
                    split_lo()
                if j == 2:
                    eng.wait_ge(S["qkv_in"], v.next("qkv_in"))
                    for t in range(TT):
                        tt(sq[:, :], qkv[:, t, 0:N], qkv[:, t, 0:N], ALU.mult).then_inc(S["dve"], v.up("dve"))
                        eng.wait_ge(S[v.last], v.ended())
                        ins = eng.tensor_reduce(stt[:, 3, t * 10:(t + 1) * 10], heads(sq[:, :]), X, ALU.add)
                        ins.then_inc(S["dve"], v.up("dve"))
                        eng.wait_ge(S[v.last], v.ended())
                    ts(stt[:, 0, :], stt[:, 3, :], 1.0 / HD, EPS, ALU.mult, ALU.add).then_inc(S["mean"], v.up("mean"))
                if 3 <= j < 6:
                    i, n = 2 * (j - 3), PADDED - 4
                    if j == 3:
                        eng.wait_ge(S["pads"], v.next("pads"))
                    else:
                        eng.wait_ge(S["conv_raw"], j - 3)
                    eng.wait_ge(S["xb_in"], v.next("xb_in", 2))
                    for k in range(TAPS):
                        for i_ in (i, i + 1):
                            tap = vec[:, CONV_W + k * XBC_T + i_:CONV_W + k * XBC_T + i_ + 1]
                            if k == 0:
                                ins = ts(conv[:, i_, 0:n], xpad[:, i_, 0:n], tap, None, ALU.mult)
                            else:
                                if i_ == i:
                                    eng.wait_ge(S[v.last], v.ended())
                                ins = st3(conv[:, i_, 0:n], xpad[:, i_, k:k + n], tap, conv[:, i_, 0:n], ALU.mult, ALU.add)
                        ins.then_inc(S["dve" if k < TAPS - 1 else "conv_raw"], v.up("dve" if k < TAPS - 1 else "conv_raw"))
                if j == 3:
                    inverse_root(TT * 10)
                    eng.wait_ge(S[v.last], v.ended())
                    eng.wait_ge(S["dtw_hi"], v.next("dtw_hi"))
                    ins = tt(dtw_lo[:, :, :], dtw[:, :, :], dtw_hi[:, :, :].bitcast(f32), ALU.subtract)
                    ins.then_inc(S["dtw_lo"], v.up("dtw_lo"))
                for t in ((), (), (), (0,), (1,), (), (), (4,))[j]:
                    norm_and_turn(t)
                if j == 6:
                    eng.wait_ge(S["dt_in"], v.next("dt_in"))
                    ins = tt(dt_tok[:, :, :], dt_tok[:, :, :], dt_c[:, 0, :].unsqueeze(1).broadcast_to([P, TT, DTS]), ALU.add)
                    ins.then_inc(S["dve"], v.up("dve"))
                    eng.wait_ge(S[v.last], v.ended())
                    ins = st3(dt_t[1][:, :, :], dt_tok[:, :, :], -1.0, dt_tok[:, :, :], ALU.mult, ALU.max)
                    ins.then_inc(S["dt_abs"], v.up("dt_abs"))
                    eng.wait_ge(S[v.last], v.ended())
                    ts(dt_tok[:, :, :], dt_tok[:, :, :], 0.0, None, ALU.max).then_inc(S["dve"], v.up("dve"))
                    norm_and_turn(2)
                    eng.wait_ge(S["dt_exp"], v.next("dt_exp"))
                    e, u, c = (t[:, :, :] for t in (dt_t[1], dt_t[0], dt_t[2]))
                    ts(u, e, 1.0, None, ALU.add).then_inc(S["dt_u"], v.up("dt_u"))
                    eng.wait_ge(S[v.last], v.ended())
                    ts(c, u, -1.0, None, ALU.add).then_inc(S["dve"], v.up("dve"))
                    eng.wait_ge(S[v.last], v.ended())
                    tt(c, e, c, ALU.subtract).then_inc(S["dve"], v.up("dve"))
                    eng.wait_ge(S[v.last], v.ended())
                    eng.reciprocal(e, u).then_inc(S["dve"], v.up("dve"))
                    eng.wait_ge(S[v.last], v.ended())
                    tt(c, c, e, ALU.mult).then_inc(S["dve"], v.up("dve"))
                    eng.wait_ge(S[v.last], v.ended())
                    norm_and_turn(3)
                    eng.wait_ge(S["dt_ln"], v.next("dt_ln"))
                    tt(dt_tok[:, :, :], dt_tok[:, :, :], c, ALU.add).then_inc(S["dve"], v.up("dve"))
                    eng.wait_ge(S[v.last], v.ended())
                    tt(dt_tok[:, :, :], dt_tok[:, :, :], dt_t[3][:, :, :], ALU.add).then_inc(S["dve"], v.up("dve"))
                    eng.wait_ge(S[v.last], v.ended())
                    ins = tt(a_tok[:, :, :], dt_tok[:, :, :], dt_c[:, 1, :].unsqueeze(1).broadcast_to([P, TT, DTS]), ALU.mult)
                    ins.then_inc(S["dve"], v.up("dve"))
                    eng.wait_ge(S[v.last], v.ended())
                    ts(a_tok[:, :, :], a_tok[:, :, :], -1.0, None, ALU.mult).then_inc(S["a_ready"], v.up("a_ready"))
            U = len(units)
            for i in range(U + 2):
                if i < U:
                    t, h = units[i]
                    n = N_CTX if t == 0 else N
                    eng.wait_ge(S["scores"], v.next("scores"))
                    if v.due("exp_done", 4):
                        eng.wait_ge(S["exp_done"], v.now("exp_done", 4))
                    ins = eng.tensor_reduce(nmax[:, i % 4:i % 4 + 1], mixf[:, 1024 * (i % 2):1024 * (i % 2) + n], X, ALU.max)
                    ins.then_inc(S["dve"], v.up("dve"))
                    eng.wait_ge(S[v.last], v.ended())
                    ins = ts(nmax[:, i % 4:i % 4 + 1], nmax[:, i % 4:i % 4 + 1], -ATT_SCALE, None, ALU.mult)
                    ins.then_inc(S["max_ready"], v.up("max_ready"))
                if 1 <= i <= U:
                    t, h = units[i - 1]
                    n = N_CTX if t == 0 else N
                    b = (i - 1) % 2
                    eng.wait_ge(S["pT_made"], v.next("pT_made"))
                    if v.due("att_made", 2):
                        eng.wait_ge(S["att_made"], v.now("att_made", 2))
                    eng.tensor_copy(pT[:, b, 0:n], accf[:, 1024 * b:1024 * b + n]).then_inc(S["pT_sb"], v.up("pT_sb"))
                if i >= 2:
                    t, h = units[i - 2]
                    u, b = i - 2, i % 2
                    eng.reciprocal(rrec[:, u % 4:u % 4 + 1], rsum[:, u % 4:u % 4 + 1]).then_inc(S["dve"], v.up("dve"))
                    eng.wait_ge(S[v.last], v.ended())
                    eng.wait_ge(S["att_made"], u + 1)
                    ts(att_tok[:, t, h * HD:(h + 1) * HD], accf[:, 1024 * b + 768:1024 * b + 768 + HD],
                             rrec[:, u % 4:u % 4 + 1], None, ALU.mult).then_inc(S["att_read"], v.up("att_read"))
            eng.wait_ge(S["kv_gone"], 1)
            eng.wait_ge(S["cum_made"], v.next("cum_made"))
            both = mixf[:, 0:TT * DTS].rearrange("p (t c) -> p t c", c=DTS)
            eng.tensor_copy(cum[:, :, :], both)
            ts(ncum[:, :, :], both, -1.0, None, ALU.mult).then_inc(S["cum_read"], v.up("cum_read"))
            eng.wait_ge(S[v.last], v.ended())
            for t in range(TT):
                eng.wait_ge(S["xt_made"], v.next("xt_made"))
                eng.tensor_copy(x_tok[:, t, :], acc[:, t % 2, :]).then_inc(S["xt_read"], v.up("xt_read"))
            eng.wait_ge(S["bt_made"], v.next("bt_made"))
            eng.tensor_copy(b_tok[:, :], acc[:, 2, 0:P]).then_inc(S["bt_read"], v.up("bt_read"))
            for g in range(2):
                for J in range(LT + 1):
                    n = g * (LT + 1) + J
                    eng.wait_ge(S["cb_made"], v.next("cb_made"))
                    if J < LT:
                        ins = eng.tensor_copy(Gt[g][:, J * N_LAT:(J + 1) * N_LAT], mix[:, 1 + n % 2, :])
                        ins.then_inc(S["cb_read"], v.up("cb_read"))
                    else:
                        eng.tensor_copy(Gp[:, g, :], mix[:, 1 + n % 2, 0:P]).then_inc(S["cb_read"], v.up("cb_read"))
            eng.wait_ge(S["conv_ready"], v.next("conv_ready"))
            f, w = (lambda h, t: ncum[:, t, h:h + 1]), (lambda h, t: dt_tok[:, t, h:h + 1])

            def y_in(h):
                eng.wait_ge(S["y_made"], v.next("y_made"))
                dst = yT[HD * (h % 2):HD * (h % 2) + HD, h // 2, :]
                eng.tensor_copy(dst[:, 0:N_CTX], mix[0:HD, 2, (h % 2) * P:(h % 2 + 1) * P])
                ins = eng.tensor_copy(dst[:, N_CTX:], mix[0:HD, h % 2, :])
                ins.then_inc(S["y_read"], v.up("y_read"))

            for h in range(NH):
                g = h // 4
                eng.wait_ge(S["rows_made"], v.next("rows_made"))
                dg = dgs[h % 2]
                if h:
                    eng.wait_ge(S["m_ready"], h)
                if h % 4 == 0:
                    for b in range(2):
                        ins = eng.tensor_copy(ct2[HD * b:HD * b + HD, :], conv[HD * g:HD * g + HD, ST + 1, LAT])
                    ins.then_inc(S["dve"], v.up("dve"))
                eng.tensor_copy(tot[:, h:h + 1], accf[:, P - 1:P])
                eng.tensor_copy(tot[:, NH + h:NH + h + 1], accf[:, 1024:1025]).then_inc(S["dve"], v.up("dve"))
                for t in range(TT):
                    ins = ts(dm[:, t, :], accf[:, 1024 + t * P:1024 + (t + 1) * P], f(NH + h, t), None, ALU.add)
                ins.then_inc(S["dve"], v.up("dve"))
                eng.wait_ge(S[v.last], v.ended())
                for t in range(TT):
                    ins = st3(dg[:, t, :], accf[:, t * P:(t + 1) * P], f(h, t), dm[:, t, :], ALU.add, ALU.min)
                ins.then_inc(S["arg_ready"], v.up("arg_ready"))
                eng.wait_ge(S[v.last], v.ended())
                for t in range(TT):
                    ins = ts(dm[:, t, :], upto[:, :], w(h, t), None, ALU.mult)
                ins.then_inc(S["dve"], v.up("dve"))
                eng.wait_ge(S[v.last], v.ended())
                for t in range(TT):
                    ins = st3(dm[:, t, :], onward[:, :], w(NH + h, t), dm[:, t, :], ALU.mult, ALU.add)
                ins.then_inc(S["dve"], v.up("dve"))
                eng.wait_ge(S[v.last], v.ended())
                diag = Gt[g][:, :].rearrange("p (j c) -> p j c", j=LT)[:, :, 0:P]
                tt(dm[:, 0, :], dm[:, 0, :], Gp[:, g, :], ALU.mult)
                tt(dm[:, 1:, :], dm[:, 1:, :], diag, ALU.mult).then_inc(S["dve"], v.up("dve"))
                eng.wait_ge(S[v.last], v.ended())
                eng.wait_ge(S["diag_exp"], v.next("diag_exp"))
                tt(dg[:, 0, :], dg[:, 0, :], dm[:, 0, :], ALU.mult).then_inc(S["dve"], v.up("dve"))
                if h:
                    y_in(h - 1)
                for J in range(LT):
                    tt(M_all[:, J, J * P:(J + 1) * P], dg[:, J + 1, :], dm[:, J + 1, :], ALU.mult)
                eng.wait_ge(S["rows_read"], v.next("rows_read"))
                eng.wait_ge(S["dve"], v.made["dve"])
                for J in range(LT):
                    if J < LT - 1:
                        c = slice((J + 1) * P, N_LAT)
                        st3(M_all[:, J, c], E_all[:, J, c], w(h, J + 1), Gt[g][:, J * N_LAT + c.start:J * N_LAT + c.stop], ALU.mult, ALU.mult)
                    if J:
                        c = slice(0, J * P)
                        st3(M_all[:, J, c], E_all[:, J, c], w(NH + h, J + 1), Gt[g][:, J * N_LAT:J * N_LAT + c.stop], ALU.mult, ALU.mult)
                tt(ce[:, :], ecum[:, :], ct2[:, :], ALU.mult).then_inc(S["m_ready"], v.up("m_ready"))
            y_in(NH - 1)
            tt(wst[:, :], tot[:, :], ncum[:, 0, :], ALU.add).then_inc(S["wst_arg"], v.up("wst_arg"))
            eng.wait_ge(S["wst_exp"], v.next("wst_exp"))
            tt(wst[:, :], wst[:, :], dt_tok[:, 0, :], ALU.mult).then_inc(S["dve"], v.up("dve"))
            eng.wait_ge(S[v.last], v.ended())
            for h in range(NH):
                g = h // 4
                if v.due("fs_made", 2):
                    eng.wait_ge(S["fs_made"], v.now("fs_made", 2))
                for b in range(2):
                    ins = ts(bw[:, h % 2, b * HD:(b + 1) * HD], b_tok[:, g * HD:(g + 1) * HD], wst[:, b * NH + h:b * NH + h + 1], None, ALU.mult)
                ins.then_inc(S["bw_ready"], v.up("bw_ready"))
            eng.wait_ge(S["fs_made"], NH)
            ins = eng.tensor_copy(s_out[:, :, :].rearrange("p h d -> p (h d)"), mix[:, 2, :])
            ins.then_inc(S["s_out_ready"], v.up("s_out_ready"))
            eng.wait_ge(S["ada_turned"], v.next("ada_turned", 16))
            mods(0, 16, 48)
            gains(0, 1).then_inc(S["gain_ready"], v.up("gain_ready"))
            split_lo()
            for t in range(TT):
                eng.wait_ge(S["aT_made"], v.next("aT_made"))
                eng.wait_ge(S["h_hi"], v.next("h_hi"))
                ins = tt(h_lo[:, 0:ST, tok(t)], acc[:, 2 + t % 2, :].rearrange("p (j n) -> p j n", j=4), h_hi[:, 0:ST, tok(t)].bitcast(f32), ALU.subtract)
                ins.then_inc(S["aT_read"], v.up("aT_read"))
            eng.wait_ge(S[v.last], v.ended())
            eng.sem_inc(S["h_ready"], v.told("h_ready"))
            split_lo()
            for j in range(ST):
                for cols, here in ((slice(0, N_CTX), slice(0, N_CTX)), (LAT, slice(N_CTX, N))):
                    ins = st3(conv[:, j, cols], conv[:, j, cols], d_skip[:, j:j + 1], yT[:, j, here], ALU.mult, ALU.add)
            ins.then_inc(S["dve"], v.up("dve"))
            eng.wait_ge(S[v.last], v.ended())
            for j in range(ST):
                tt(zT[:, j, 0:N_CTX], zT[:, j, 0:N_CTX], conv[:, j, 0:N_CTX], ALU.mult)
                tt(zT[:, j, N_CTX:], zT[:, j, N_CTX:], conv[:, j, LAT], ALU.mult).then_inc(S["dve"], v.up("dve"))
                eng.wait_ge(S[v.last], v.ended())
                square_in(zT[:, j, :], j == 0)
                into_x(0, 0, j, squares=False)
            split_lo()
            rms_to_inverse(SSD_W, before=lambda: [into_x(0, 0, d, squares=False) for d in (ST, ST + 1)])
            into_x(0, 0, ST + 2, squares=False)
            into_x(0, 0, ST + 3, squares=False)
            eng.wait_ge(S["rb"], v.next("rb"))

            def y_normed(j):
                ins = st3(y_buf[j % 2], zT[:, j, :], vec[:, SSD_G + j:SSD_G + j + 1], rB, ALU.mult, ALU.mult)
                ins.then_inc(S["y32_ready"], v.up("y32_ready"))

            y_normed(0)
            for j in range(ST):
                if j + 1 < ST:
                    y_normed(j + 1)
                eng.wait_ge(S["h_hi"], v.next("h_hi"))
                ins = tt(h_lo[:, ST + j, :], y_buf[j % 2], h_hi[:, ST + j, :].bitcast(f32), ALU.subtract)
                ins.then_inc(S["h_ready"], v.up("h_ready"))
                eng.wait_ge(S[v.last], v.ended())
            eng.sem_inc(S["l0_mixed"], v.told("l0_mixed"))
            split_lo()
            for d in range(KT):
                into_x(0, 0, d)
                if d == 3:
                    split_lo()

            def ffn(l):
                rms(D, split_lo)
                modulate(l, 1)
                for f0, nf in CHUNKS:
                    per = {"acc_ready0": 2, "acc_ready1": 2, "acc_free1": 2, "silu_ready": 2, "gu32_ready": 2, "gu_hi": 2,
                           "gu_ready": 2, "w_hi0": 1, "w_hi1": 1, "w_lo0": 1, "w_lo1": 1, "dve": 2}
                    if l == 0:
                        per |= {"ada_hi": 2, "ada_lo": 2}
                    with v.loop(nf // 2, per) as i:
                        for s in range(2):
                            pass_tiles(1)
                            if l == 0:
                                eng.wait_ge(S["ada_hi"], v.next("ada_hi"))
                                ins = tt(ada_lo[:, :], ada_raw[s][:, :], ada_hi[:, :].bitcast(f32), ALU.subtract)
                                ins.then_inc(S["ada_lo"], v.up("ada_lo"))
                            eng.wait_ge(S["silu_ready"], v.next("silu_ready"))
                            r = tile_of()
                            tt(halves(gu32[:, :]), halves(silu_g[:, :]), pair(r), ALU.mult).then_inc(S["dve"], v.up("dve"))
                            eng.wait_ge(S[v.last], v.ended())
                            eng.sem_inc(S[f"acc_free{r}"], v.told(f"acc_free{r}"))
                            eng.wait_ge(S[v.last], v.ended())
                            eng.sem_inc(S["gu32_ready"], v.told("gu32_ready"))
                            split_lo()
                            eng.wait_ge(S["gu_hi"], v.next("gu_hi"))
                            f_ = bass.ds(i * 2 + s, 1)
                            one = lambda a: a[:, f_, :].rearrange("p o n -> p (o n)")
                            ins = tt(one(gu_lo), gu32[:, :], one(gu_hi).bitcast(f32), ALU.subtract)
                            ins.then_inc(S["gu_ready"], v.up("gu_ready"))
                            eng.wait_ge(S[v.last], v.ended())
                    for j in range(4):
                        for c in range(2):
                            into_x(l, 1, 2 * j + c)
                        if f0 != CHUNKS[-1][0] or j < (3, 2)[l]:
                            split_lo()

            ffn(0)
            eng.wait_ge(S[v.last], v.ended())
            eng.sem_inc(S["ffn_over"], v.told("ffn_over"))
            def layer1_modulation():
                eng.wait_ge(S["ada_turned"], v.next("ada_turned", 24))
                mods(1, 0, 48)
                gains(1, 0)
                gains(1, 1).then_inc(S["gain_ready"], v.up("gain_ready"))
                eng.wait_ge(S[v.last], v.ended())

            rms(D, layer1_modulation)
            modulate(1, 0)
            eng.wait_ge(S["l1_in"], v.next("l1_in", 16 * 5))
            eng.wait_ge(S[v.last], v.ended())
            eng.sem_inc(S["head_used"], v.told("head_used"))
            per = {"acc_ready0": 13, "acc_ready1": 13, "acc_free0": 4, "acc_free1": 4, "w_hi0": 4, "w_hi1": 4, "w_lo0": 4, "w_lo1": 4,
                   "head_in": 128, "decay_exp": 1, "arg1_ready": 1, "strip_exp": 1, "grow_ready": 2, "grow_used": 2, "wcol_ready": 1,
                   "qk_in": 1, "rope_done": 1, "kp_made": 1, "kw_ready": 1, "score_made": 5, "sc_ready": 5, "y_part": 5,
                   "qg_ready": 2, "state_done": 2, "yr_read": 1,
                   "sq_done": 1, "stat": 1, "mean": 1, "root": 1, "rinv": 1, "rb": 1,
                   "g_in": 4, "z32_ready": 4, "yg_hi": 4, "yg_ready": 4, "head_used": 1}
            per["dve"] = 45
            flat = lambda a: a.rearrange("p a n -> p (a n)")
            with v.loop(RH, per):
                split_lo()
                pass_tiles(2)
                split_lo()
                eng.wait_ge(S["head_in"], v.next("head_in", 128))
                eng.wait_ge(S["decay_exp"], v.next("decay_exp"))
                ts(acol[:, :], acol[:, :], -1.0, None, ALU.mult).then_inc(S["dve"], v.up("dve"))
                eng.wait_ge(S[v.last], v.ended())
                tmp = flat(sc_sb[:, :, :])[:, 0:STRIP]
                ts(tmp, strip[:, :], 0.0, acol[:, 0:1], ALU.max, ALU.mult).then_inc(S["dve"], v.up("dve"))
                eng.wait_ge(S[v.last], v.ended())
                ts(strip[:, :], strip[:, :], -1.0, 0.0, ALU.mult, ALU.max).then_inc(S["dve"], v.up("dve"))
                eng.wait_ge(S[v.last], v.ended())
                ins = st3(strip[:, :], strip[:, :], acol[:, 1:2], tmp, ALU.mult, ALU.add)
                ins.then_inc(S["arg1_ready"], v.up("arg1_ready"))
                pass_tiles(2)
                split_lo()
                eng.wait_ge(S["qk_in"], v.next("qk_in"))
                for m in range(2):
                    a, b = qk[:, 2 * m, N_CTX:], qk[:, 2 * m + 1, N_CTX:]
                    r = [tbuf[:, 0, 0:N_LAT], tbuf[:, 1, 0:N_LAT], h32[:, 0:N_LAT], sq[:, 0:N_LAT]]
                    for o, p_, q_ in zip(r, (a, b, b, a), (cosR, sinR, cosR, sinR)):
                        ins = tt(o, p_, q_[:, :], ALU.mult)
                    ins.then_inc(S["dve"], v.up("dve"))
                    eng.wait_ge(S[v.last], v.ended())
                    tt(a, r[0], r[1], ALU.subtract)
                    tt(b, r[2], r[3], ALU.add).then_inc(S["rope_done" if m else "dve"], v.up("rope_done" if m else "dve"))
                    eng.wait_ge(S[v.last], v.ended())
                eng.wait_ge(S["strip_exp"], v.next("strip_exp"))
                ins = tt(strip[:, (LT - 1) * P:LT * P], strip[:, (LT - 1) * P:LT * P], ident[:, :], ALU.add)
                ins.then_inc(S["dve"], v.up("dve"))
                eng.wait_ge(S[v.last], v.ended())

                def decayed(b):
                    eng.wait_ge(S["grow_ready"], v.next("grow_ready"))
                    ins = tt(qg[:, :, :], qk[:, 0:2, N_CTX:], grow[:, :].unsqueeze(1).broadcast_to([P, 2, N_LAT]), ALU.mult)
                    ins.then_inc(S["qg_ready"], v.up("qg_ready"))
                    eng.wait_ge(S[v.last], v.ended())
                    eng.sem_inc(S["grow_used"], v.told("grow_used"))

                decayed(0)
                for j in range(2):
                    pass_tiles(TT)
                    split_lo()
                eng.wait_ge(S["kp_made"], v.next("kp_made"))
                eng.wait_ge(S["wcol_ready"], v.next("wcol_ready"))
                for b in range(2):
                    ins = ts(kw[:, b, :], mix[:, 0, 0:DK], wcol[:, b:b + 1], None, ALU.mult)
                ins.then_inc(S["kw_ready"], v.up("kw_ready"))
                for J in range(LT + 1):
                    eng.wait_ge(S["score_made"], v.next("score_made"))
                    if J == 0:
                        eng.wait_ge(S[v.last], v.ended())
                    if 2 <= J:
                        eng.wait_ge(S["y_part"], v.next("y_part"))
                    if J < LT:
                        ins = tt(sc_sb[:, J % 2, :], mix[:, 1 + J % 2, :], strip[:, (LT - 1 - J) * P:(LT - 1 - J) * P + N_LAT], ALU.mult)
                        ins.then_inc(S["sc_ready"], v.up("sc_ready"))
                    else:
                        ins = tt(sc_p[:, :], mix[:, 1 + J % 2, 0:P], strip[:, (LT - 1) * P:LT * P], ALU.mult)
                        ins.then_inc(S["sc_ready"], v.up("sc_ready"))
                eng.wait_ge(S["state_done"], v.next("state_done"))
                decayed(1)
                eng.wait_ge(S["y_part"], v.next("y_part", 2))
                eng.wait_ge(S["state_done"], v.next("state_done"))
                eng.tensor_copy(yR[:, :, 0:N_CTX], mix[:, 0, :].rearrange("p (a n) -> p a n", a=VT))
                eng.tensor_copy(yR[:, :, N_CTX:], acc[:, :, :]).then_inc(S["yr_read"], v.up("yr_read"))
                eng.wait_ge(S[v.last], v.ended())
                for j in range(VT):
                    square_in(yR[:, j, :], j == 0)
                rms(DV)
                for j in range(VT):
                    st3(yR[:, j, :], yR[:, j, :], rgain[:, j:j + 1], rB, ALU.mult, ALU.mult).then_inc(S["dve"], v.up("dve"))
                    eng.wait_ge(S[v.last], v.ended())
                eng.sem_inc(S["head_used"], v.told("head_used"))
                for n in range(VT):
                    eng.wait_ge(S["g_in"], v.next("g_in"))
                    tt(h32[:, :], tbuf[:, n % 2, :], yR[:, n, :], ALU.mult).then_inc(S["z32_ready"], v.up("z32_ready"))
                    eng.wait_ge(S[v.last], v.ended())
                    eng.wait_ge(S["yg_hi"], v.next("yg_hi"))
                    ins = tt(yg_lo[:, n, :], h32[:, :], yg_hi[:, n, :].bitcast(f32), ALU.subtract)
                    ins.then_inc(S["yg_ready"], v.up("yg_ready"))
                    eng.wait_ge(S[v.last], v.ended())
                    if n % 2:
                        pass_tiles(2)
                        split_lo()
                for j in range(2):
                    for c in range(4):
                        into_x(1, 0, 4 * j + c)
                    if j == 0:
                        split_lo()
            ffn(1)
            rms(D)
            for k in range(KT):
                ins = st3(xT[:, k, :], xT[:, k, :], vec[:, FIN + k:FIN + k + 1], rB, ALU.mult, ALU.mult)
                if k % 4 == 3:
                    ins.then_inc(S["final_ready"], v.up("final_ready"))
            for n in range(2 * TT):
                half, t = divmod(n, TT)
                if COPIER[n] == "y_by_dve":
                    eng.wait_ge(S["out_T"], n + 1)
                    ins = eng.tensor_copy(y_out[:, t, half * 512:(half + 1) * 512], acc[:, n % 4, :])
                    ins.then_inc(S["y_by_dve"], v.up("y_by_dve"))

        @block.gpsimd
        def _(eng):
            po = Line(eng, "pool")

            eng.wait_ge(S["x_T_read"], 2 * TT)
            for cols in (slice(0, 2), slice(2 + P, 6 + P), slice(PADDED - 2, PADDED)):
                ins = eng.memset(xpad[:, :, cols], 0.0)
            ins.then_inc(S["pads"], po.up("pads"))
            eng.wait_ge(S["ffn_over"], po.next("ffn_over"))
            for dst, src in ([(cosR[:, :], I["rope_ret"][0]), (sinR[:, :], I["rope_ret"][1]), (pcol[:, :], I["places"])]
                             + [(ramp[:, b, :], I["ramps"][b, :].partition_broadcast(P)) for b in range(2)]):
                eng.dma_start(dst, src).then_inc(S["l1_in"], po.up("l1_in", 16))
            per = {"head_used": 1, "head_in": 16 * 8, "fs_ready": 4, "fs_out0": 32, "fs_out1": 32}
            with po.loop(RH, per) as h:
                eng.wait_ge(S["head_used"], po.next("head_used"))
                eng.sem_inc(S["pool_go"], 1)
                o = bass.ds(h, 1)
                one = lambda a: a.rearrange("o p d -> p (o d)")
                eng.dma_start(strip[:, :], I["offsets"]).then_inc(S["head_in"], po.up("head_in", 16))
                eng.dma_start(rgain[:, :], I["l1_ret_gain"][bass.ds(h * DV, DV)].rearrange("(t p) -> p t", p=P),
                                     allow_slow_non_contiguous=True).then_inc(S["head_in"], po.up("head_in", 16))
                for b in range(2):
                    ins = eng.dma_start(acol[:, b:b + 1], I["l1_decay"][b, o].partition_broadcast(P))
                    ins.then_inc(S["head_in"], po.up("head_in", 16))
                    for k in range(2):
                        ins = eng.dma_start(S0[:, b, k, :], one(I["state_ret1"][0, b, o, k * P:(k + 1) * P, :]))
                        ins.then_inc(S["head_in"], po.up("head_in", 16))
                for n in range(4):
                    b, k = divmod(n, 2)
                    eng.wait_ge(S["fs_ready"], po.next("fs_ready"))
                    eng.sem_inc(S["pool_go"], 1)
                    ins = eng.dma_start(one(O[5][0, b, o, k * P:(k + 1) * P, :]), tbuf[:, n % 2, 0:DV])
                    ins.then_inc(S[f"fs_out{n % 2}"], po.up(f"fs_out{n % 2}", 16))
            for b in range(2):
                eng.wait_ge(S[f"fs_out{b}"], 32 * RH)


_INS = ["x_prompt", "x_sample", "c", "cache_k0", "cache_v0", "state_ssd0", "state_ret1", "c_ctx",
        "l0_w_ada", "l0_b_ada", "l0_norm_mix", "l0_norm_ffn", "l0_w_in", "l0_w_out", "l0_q_gain", "l0_k_gain",
        "l0_conv_w", "l0_conv_b", "l0_dt_bias", "l0_a_log", "l0_d_skip", "l0_ssd_gain",
        "l0_w_gate", "l0_w_up", "l0_w_down", "l1_w_ada", "l1_b_ada", "l1_norm_mix", "l1_norm_ffn",
        "l1_w_in", "l1_w_out", "l1_decay", "l1_ret_gain", "l1_w_gate", "l1_w_up", "l1_w_down", "final_norm"]
_OUTS = [(1, N_CTX, D), (1, N_LAT, D), (1, N_CTX, NKV, HD), (1, N_CTX, NKV, HD),
         (1, 2, NH, HD, HD), (1, 2, RH, DK, DV)]


def _constants():
    import numpy as np

    i = np.arange(P)
    squares = np.stack([np.eye(P), i[:, None] <= i[None, :], i[:, None] >= i[None, :], np.ones((P, P))])
    n = np.arange(N_LAT)
    row, col = (n // GRID_W).astype(np.float32), (n % GRID_W).astype(np.float32)

    def rope(dim):
        f = dim // 4
        inv = np.float32(10000.0) ** (-np.arange(f, dtype=np.float32) / np.float32(f))
        ang = np.concatenate([row[:, None] * inv, col[:, None] * inv], axis=1).astype(np.float32)
        return np.stack([np.cos(ang.astype(np.float64)), np.sin(ang.astype(np.float64))])

    att = rope(HD).reshape(2, LT, P, HD // 2).transpose(0, 2, 1, 3)
    ret = rope(DK).transpose(0, 2, 1)
    offsets = (np.arange(STRIP)[None, :] - (LT - 1) * P) - i[:, None]
    ramps = np.stack([n + 1, N_LAT - n])
    places = np.stack([P - 1 - i, i], axis=1)
    f = lambda a: np.ascontiguousarray(a, dtype=np.float32)
    return {"squares": f(squares), "rope_att": f(att), "rope_ret": f(ret), "offsets": f(offsets),
            "ramps": f(ramps), "places": f(places)}


def kernel(**inputs):
    import numpy as _np
    import concourse.bacc as _bacc
    from concourse import mybir as _mybir
    from concourse.bass_utils import run_bass_kernel_spmd as _run

    nc = _bacc.Bacc("TRN2", target_bir_lowering=False, num_devices=1)
    arrays, ins, outs = {}, {}, []
    given = {name: _np.ascontiguousarray(inputs[name]) for name in _INS}
    for name, a in {**given, **_constants()}.items():
        arrays[f"in_{name}_dram"] = a
        ins[name] = nc.dram_tensor(f"in_{name}_dram", a.shape, _mybir.dt.from_np(a.dtype), kind="ExternalInput").ap()
    for i, shape in enumerate(_OUTS):
        outs.append(nc.dram_tensor(f"out_{i}_dram", shape, _mybir.dt.float32, kind="ExternalOutput").ap())
    trunk_kernel(nc, ins, outs)
    r = _run(nc, [arrays], core_ids=[0])
    return tuple(r.results[0][f"out_{i}_dram"] for i in range(len(_OUTS)))
```
